# Optimizing a Trainium2 kernel written in Bass

```python
import jax, jax.numpy as jnp
from jax import lax
import numpy as np

D_MODEL = 1024
BATCH = 1
SEQ = 256
DEPTH = 2

MIX_WIDTH = D_MODEL
GM_HEADS = 4
GM_WIDTH = MIX_WIDTH // 2
GM_HEAD_DIM = GM_WIDTH // GM_HEADS
GM_CHUNK = 128
GLA_HEADS = 4
GLA_WIDTH = MIX_WIDTH - GM_WIDTH
GLA_DV = GLA_WIDTH // GLA_HEADS
GLA_KEY_WIDTH = GLA_WIDTH // 2
GLA_DK = GLA_KEY_WIDTH // GLA_HEADS
GLA_GATE_RANK = 16
GLA_TAU = 16.0
GLA_CHUNK = 64
IN_COLS = 2 * GM_WIDTH + 2 * GLA_KEY_WIDTH + 2 * GLA_WIDTH + GLA_GATE_RANK
D_FF = 2816
N_EXPERTS = 8
TOP_K = 2
D_FF_EXPERT = 3584
N_DENSE = (DEPTH + 1) // 2
N_MOE = DEPTH // 2
LN_EPS = 1e-5
RMS_EPS = 1e-6
DEEPNORM_ALPHA = (2 * DEPTH) ** 0.25
DEEPNORM_BETA = (8 * DEPTH) ** -0.25


def layer_norm(x, g, b):
    xf = x.astype(jnp.float32)
    mu = jnp.mean(xf, axis=-1, keepdims=True)
    var = jnp.mean(jnp.square(xf - mu), axis=-1, keepdims=True)
    y = (xf - mu) * lax.rsqrt(var + LN_EPS) * g.astype(jnp.float32) + b.astype(jnp.float32)
    return y.astype(x.dtype)

def chunked_spatial_gating(u, v, w_s, b_s, ln_g, ln_b):
    B, S, _ = u.shape
    n = S // GM_CHUNK
    v = layer_norm(v.reshape(B, S, GM_HEADS, GM_HEAD_DIM),
                   ln_g.reshape(GM_HEADS, GM_HEAD_DIM), ln_b.reshape(GM_HEADS, GM_HEAD_DIM))
    v = v.reshape(B, n, GM_CHUNK, GM_HEADS, GM_HEAD_DIM)
    causal = jnp.tril(jnp.ones((GM_CHUNK, GM_CHUNK), dtype=bool))
    w = jnp.where(causal[None], w_s, 0)
    s = jnp.einsum('hts,bnshc->bnthc', w, v) + b_s.T[None, None, :, :, None]
    return u * s.reshape(B, S, GM_WIDTH)

def gla_chunked(q, k, v, log_a):
    B, S, H, dk = q.shape
    dv = v.shape[-1]
    n = S // GLA_CHUNK

    def to_chunks(t):
        return t.astype(jnp.float32).reshape(B, n, GLA_CHUNK, H, t.shape[-1]).transpose(1, 0, 3, 2, 4)

    q, k, v, log_a = to_chunks(q), to_chunks(k), to_chunks(v), to_chunks(log_a)
    q = q * (dk ** -0.5)
    b = jnp.cumsum(log_a, axis=3)
    b_last = b[:, :, :, -1:, :]
    q_dec = q * jnp.exp(b)
    k_inv = k * jnp.exp(-b)
    k_dec = k * jnp.exp(b_last - b)
    causal = jnp.tril(jnp.ones((GLA_CHUNK, GLA_CHUNK), dtype=bool))
    scores = jnp.where(causal, jnp.einsum('nbhid,nbhjd->nbhij', q_dec, k_inv), 0.0)
    o_intra = jnp.einsum('nbhij,nbhje->nbhie', scores, v)

    def step(state, inp):
        q_c, k_c, v_c, decay_c = inp
        o = jnp.einsum('bhid,bhde->bhie', q_c, state)
        state = state * decay_c[..., 0, :, None] + jnp.einsum('bhjd,bhje->bhde', k_c, v_c)
        return state, o

    state0 = jnp.zeros((B, H, dk, dv), jnp.float32)
    _, o_inter = lax.scan(step, state0, (q_dec, k_dec, v, jnp.exp(b_last)))
    o = o_intra + o_inter
    return o.transpose(1, 0, 3, 2, 4).reshape(B, S, H, dv)

def hybrid_mixer(x, w_in, gm_ws, gm_bs, gm_ln_g, gm_ln_b, gla_wa2, gla_ba, gla_norm_g, w_out):
    B, S, _ = x.shape
    proj = x @ w_in
    o1 = GM_WIDTH
    o2 = o1 + GM_WIDTH
    o3 = o2 + GLA_KEY_WIDTH
    o4 = o3 + GLA_KEY_WIDTH
    o5 = o4 + GLA_WIDTH
    o6 = o5 + GLA_WIDTH
    gm_u, gm_v, q, k, v, g, a_lr = jnp.split(proj, [o1, o2, o3, o4, o5, o6], axis=-1)
    gm_u = jax.nn.gelu(gm_u, approximate=False)
    gm_v = jax.nn.gelu(gm_v, approximate=False)
    out_a = chunked_spatial_gating(gm_u, gm_v, gm_ws, gm_bs, gm_ln_g, gm_ln_b)
    log_a = jax.nn.log_sigmoid((a_lr @ gla_wa2 + gla_ba).astype(jnp.float32)) / GLA_TAU
    o = gla_chunked(q.reshape(B, S, GLA_HEADS, GLA_DK), k.reshape(B, S, GLA_HEADS, GLA_DK),
                    v.reshape(B, S, GLA_HEADS, GLA_DV), log_a.reshape(B, S, GLA_HEADS, GLA_DK))
    o = o * lax.rsqrt(jnp.mean(jnp.square(o), axis=-1, keepdims=True) + RMS_EPS)
    o = o * gla_norm_g.reshape(GLA_HEADS, GLA_DV).astype(jnp.float32)
    out_b = o.reshape(B, S, GLA_WIDTH).astype(x.dtype) * jax.nn.silu(g)
    return jnp.concatenate([out_a, out_b], axis=-1) @ w_out

def swiglu(x, w_gate, w_up, w_down):
    return (jax.nn.silu(x @ w_gate) * (x @ w_up)) @ w_down

def moe_swiglu(x, w_router, e_gate, e_up, e_down):
    B, S, D = x.shape
    t = x.reshape(B * S, D)
    logits = (t @ w_router).astype(jnp.float32)
    top_val, top_idx = lax.top_k(logits, TOP_K)
    top_w = jax.nn.softmax(top_val, axis=-1)
    gates = jnp.sum(jax.nn.one_hot(top_idx, N_EXPERTS, dtype=jnp.float32) * top_w[..., None], axis=1)
    gates = gates.astype(t.dtype)
    out = jnp.zeros_like(t)
    for e in range(N_EXPERTS):
        out = out + gates[:, e:e + 1] * swiglu(t, e_gate[e], e_up[e], e_down[e])
    return out.reshape(B, S, D)

def first_inputs(seed: int = 0) -> dict:
    key = jax.random.key(seed)
    ks = jax.random.split(key, 22)
    nrm = jax.random.normal
    f32 = jnp.float32
    D = D_MODEL
    return {
        'x': nrm(ks[0], (BATCH, SEQ, D), f32),
        'w_in': nrm(ks[1], (DEPTH, D, IN_COLS), f32) * D ** -0.5,
        'gm_ws': nrm(ks[2], (DEPTH, GM_HEADS, GM_CHUNK, GM_CHUNK), f32) * GM_CHUNK ** -0.5,
        'gm_bs': 1.0 + 0.1 * nrm(ks[3], (DEPTH, GM_HEADS, GM_CHUNK), f32),
        'gm_ln_g': 1.0 + 0.1 * nrm(ks[4], (DEPTH, GM_WIDTH), f32),
        'gm_ln_b': 0.02 * nrm(ks[5], (DEPTH, GM_WIDTH), f32),
        'gla_wa2': nrm(ks[6], (DEPTH, GLA_GATE_RANK, GLA_KEY_WIDTH), f32) * GLA_GATE_RANK ** -0.5,
        'gla_ba': 0.1 * nrm(ks[7], (DEPTH, GLA_KEY_WIDTH), f32),
        'gla_norm_g': 1.0 + 0.1 * nrm(ks[8], (DEPTH, GLA_WIDTH), f32),
        'w_out': nrm(ks[9], (DEPTH, MIX_WIDTH, D), f32) * MIX_WIDTH ** -0.5 * DEEPNORM_BETA,
        'ln_mix_g': 1.0 + 0.1 * nrm(ks[10], (DEPTH, D), f32),
        'ln_mix_b': 0.02 * nrm(ks[11], (DEPTH, D), f32),
        'ffn_w_gate': nrm(ks[12], (N_DENSE, D, D_FF), f32) * D ** -0.5,
        'ffn_w_up': nrm(ks[13], (N_DENSE, D, D_FF), f32) * D ** -0.5,
        'ffn_w_down': nrm(ks[14], (N_DENSE, D_FF, D), f32) * D_FF ** -0.5 * DEEPNORM_BETA,
        'router_w': nrm(ks[15], (N_MOE, D, N_EXPERTS), f32) * D ** -0.5,
        'exp_w_gate': nrm(ks[16], (N_MOE, N_EXPERTS, D, D_FF_EXPERT), f32) * D ** -0.5,
        'exp_w_up': nrm(ks[17], (N_MOE, N_EXPERTS, D, D_FF_EXPERT), f32) * D ** -0.5,
        'exp_w_down': nrm(ks[18], (N_MOE, N_EXPERTS, D_FF_EXPERT, D), f32) * D_FF_EXPERT ** -0.5 * DEEPNORM_BETA,
        'ln_ffn_g': 1.0 + 0.1 * nrm(ks[19], (DEPTH, D), f32),
        'ln_ffn_b': 0.02 * nrm(ks[20], (DEPTH, D), f32),
    }

def first_block(x, w_in, gm_ws, gm_bs, gm_ln_g, gm_ln_b, gla_wa2, gla_ba, gla_norm_g, w_out,
              ln_mix_g, ln_mix_b, ffn_w_gate, ffn_w_up, ffn_w_down, router_w,
              exp_w_gate, exp_w_up, exp_w_down, ln_ffn_g, ln_ffn_b):
    for layer in range(DEPTH):
        h = hybrid_mixer(x, w_in[layer], gm_ws[layer], gm_bs[layer], gm_ln_g[layer], gm_ln_b[layer],
                         gla_wa2[layer], gla_ba[layer], gla_norm_g[layer], w_out[layer])
        x = layer_norm(DEEPNORM_ALPHA * x + h, ln_mix_g[layer], ln_mix_b[layer])
        i = layer // 2
        if layer % 2 == 0:
            f = swiglu(x, ffn_w_gate[i], ffn_w_up[i], ffn_w_down[i])
        else:
            f = moe_swiglu(x, router_w[i], exp_w_gate[i], exp_w_up[i], exp_w_down[i])
        x = layer_norm(DEEPNORM_ALPHA * x + f, ln_ffn_g[layer], ln_ffn_b[layer])
    return x


GRID_W = 64
HEAD_DIM = 64
A_HEADS = 8
A_KV_HEADS = 2
B_HEADS = 8
B_KV_HEADS = 2
C_HEADS = D_MODEL // HEAD_DIM
Q_BLOCK = 128
WINDOW = 128
NA_KH = 8
NA_KW = 16
MEM_TOKENS = 256
MEM_HEADS = 4
MEM_HEAD_DIM = D_MODEL // MEM_HEADS
D_FF_2 = 256 * ((8 * D_MODEL // 3 + 255) // 256)
ROPE_THETA = 10000.0
ALPHA = (2.0 * DEPTH) ** 0.25
BETA = (8.0 * DEPTH) ** -0.25
N_EVEN = (DEPTH + 1) // 2
N_ODD = DEPTH // 2

A_Q = A_HEADS * HEAD_DIM
A_KV = A_KV_HEADS * HEAD_DIM
B_Q = B_HEADS * HEAD_DIM
B_KV = B_KV_HEADS * HEAD_DIM
AB_IN = A_Q + 2 * A_KV + B_Q + 2 * B_KV
AB_OUT = (A_HEADS + B_HEADS) * HEAD_DIM
AB_SPLITS = [A_Q, A_Q + A_KV, A_Q + 2 * A_KV, A_Q + 2 * A_KV + B_Q, A_Q + 2 * A_KV + B_Q + B_KV]
C_WIDTH = C_HEADS * HEAD_DIM


def layer_norm_2(x, g, b):
    xf = x.astype(jnp.float32)
    mu = xf.mean(-1, keepdims=True)
    var = jnp.square(xf - mu).mean(-1, keepdims=True)
    return ((xf - mu) * lax.rsqrt(var + LN_EPS) * g.astype(jnp.float32) + b.astype(jnp.float32)).astype(x.dtype)

def rms_norm(x, g):
    xf = x.astype(jnp.float32)
    return (xf * lax.rsqrt(jnp.mean(xf * xf, -1, keepdims=True) + RMS_EPS) * g.astype(jnp.float32)).astype(x.dtype)

def swiglu_2(x, w_gate, w_up, w_down):
    return (jax.nn.silu(x @ w_gate) * (x @ w_up)) @ w_down

def rope_angles(pos, dim):
    inv = ROPE_THETA ** (-jnp.arange(0, dim, 2, dtype=jnp.float32) / dim)
    return pos[:, None] * inv[None, :]

def apply_rope(x, ang):
    half = x.shape[-1] // 2
    cos = jnp.cos(ang)[None, :, None, :].astype(x.dtype)
    sin = jnp.sin(ang)[None, :, None, :].astype(x.dtype)
    x1, x2 = x[..., :half], x[..., half:]
    return jnp.concatenate([x1 * cos - x2 * sin, x2 * cos + x1 * sin], axis=-1)

def global_gqa(q, k, v):
    B, S, H, d = q.shape
    Hkv = k.shape[2]
    G = H // Hkv
    nb = S // Q_BLOCK
    scale = d ** -0.5
    qb = q.reshape(B, nb, Q_BLOCK, Hkv, G, d).transpose(1, 0, 2, 3, 4, 5)

    def one_block(q_blk):
        s = jnp.einsum('bqkgd,bskd->bkgqs', q_blk, k).astype(jnp.float32) * scale
        p = jax.nn.softmax(s, axis=-1).astype(v.dtype)
        return jnp.einsum('bkgqs,bskd->bqkgd', p, v)

    o = lax.map(one_block, qb)
    return o.transpose(1, 0, 2, 3, 4, 5).reshape(B, S, H * d)

def window_gqa_sink(q, k, v, sink):
    B, S, H, d = q.shape
    Hkv = k.shape[2]
    G = H // Hkv
    nb = S // Q_BLOCK
    scale = d ** -0.5
    qb = q.reshape(B, nb, Q_BLOCK, Hkv, G, d)
    pad = ((0, 0), (Q_BLOCK, Q_BLOCK), (0, 0), (0, 0))
    kp = jnp.pad(k, pad).reshape(B, nb + 2, Q_BLOCK, Hkv, d)
    vp = jnp.pad(v, pad).reshape(B, nb + 2, Q_BLOCK, Hkv, d)
    k_band = jnp.concatenate([kp[:, :-2], kp[:, 1:-1], kp[:, 2:]], axis=2)
    v_band = jnp.concatenate([vp[:, :-2], vp[:, 1:-1], vp[:, 2:]], axis=2)
    blk = jnp.arange(nb)[:, None] * Q_BLOCK
    qi = blk + jnp.arange(Q_BLOCK)[None, :]
    kj = blk - Q_BLOCK + jnp.arange(3 * Q_BLOCK)[None, :]
    rel = kj[:, None, :] - qi[:, :, None]
    valid = (jnp.abs(rel) <= WINDOW) & (kj[:, None, :] >= 0) & (kj[:, None, :] < S)
    s = jnp.einsum('bnqkgd,bnskd->bnkgqs', qb, k_band).astype(jnp.float32) * scale
    s = jnp.where(valid[None, :, None, None], s, -jnp.inf)
    sink_l = sink.astype(jnp.float32).reshape(Hkv, G)[None, None, :, :, None, None]
    m = jnp.maximum(s.max(-1, keepdims=True), sink_l)
    p = jnp.exp(s - m)
    p = (p / (p.sum(-1, keepdims=True) + jnp.exp(sink_l - m))).astype(v.dtype)
    o = jnp.einsum('bnkgqs,bnskd->bnqkgd', p, v_band)
    return o.reshape(B, S, H * d)

def mixer_ab(h, w_in, w_out, q_gain, k_gain, sink, ang_2d, ang_1d):
    B, S, _ = h.shape
    qa, ka, va, qb, kb, vb = jnp.split(h @ w_in, AB_SPLITS, axis=-1)
    qa = qa.reshape(B, S, A_HEADS, HEAD_DIM)
    ka = ka.reshape(B, S, A_KV_HEADS, HEAD_DIM)
    va = va.reshape(B, S, A_KV_HEADS, HEAD_DIM)
    qa = apply_rope(rms_norm(qa, q_gain), ang_2d)
    ka = apply_rope(rms_norm(ka, k_gain), ang_2d)
    out_a = global_gqa(qa, ka, va)
    qb = apply_rope(qb.reshape(B, S, B_HEADS, HEAD_DIM), ang_1d)
    kb = apply_rope(kb.reshape(B, S, B_KV_HEADS, HEAD_DIM), ang_1d)
    vb = vb.reshape(B, S, B_KV_HEADS, HEAD_DIM)
    out_b = window_gqa_sink(qb, kb, vb, sink)
    return jnp.concatenate([out_a, out_b], axis=-1) @ w_out

def mixer_c(h, w_in, w_out, rpb):
    B, S, _ = h.shape
    rows = S // GRID_W
    kh = min(NA_KH, rows)
    kw = NA_KW
    scale = HEAD_DIM ** -0.5
    q, k, v = jnp.split(h @ w_in, 3, axis=-1)
    qg = q.reshape(B, rows, GRID_W, C_HEADS, HEAD_DIM)
    kg = k.reshape(B, rows, GRID_W, C_HEADS, HEAD_DIM)
    vg = v.reshape(B, rows, GRID_W, C_HEADS, HEAD_DIM)
    col = jnp.arange(GRID_W)
    col_start = jnp.clip(col - kw // 2, 0, GRID_W - kw)
    col_idx = col_start[:, None] + jnp.arange(kw)[None, :]
    dc = col_idx - col[:, None]

    def row_block(r):
        rs = jnp.clip(r - kh // 2, 0, rows - kh)
        k_rows = lax.dynamic_slice_in_dim(kg, rs, kh, axis=1)
        v_rows = lax.dynamic_slice_in_dim(vg, rs, kh, axis=1)
        k_nb = jnp.take(k_rows, col_idx, axis=2)
        v_nb = jnp.take(v_rows, col_idx, axis=2)
        q_r = lax.dynamic_index_in_dim(qg, r, axis=1, keepdims=False)
        dr = rs + jnp.arange(kh) - r
        bias = rpb[:, dr[None, :, None] + NA_KH - 1, dc[:, None, :] + NA_KW - 1]
        s = jnp.einsum('bwhd,bawjhd->bhwaj', q_r, k_nb).astype(jnp.float32) * scale
        s = s + bias.astype(jnp.float32)[None]
        p = jax.nn.softmax(s.reshape(B, C_HEADS, GRID_W, kh * kw), axis=-1)
        p = p.reshape(B, C_HEADS, GRID_W, kh, kw).astype(v.dtype)
        return jnp.einsum('bhwaj,bawjhd->bwhd', p, v_nb)

    o = lax.map(row_block, jnp.arange(rows))
    o = o.transpose(1, 0, 2, 3, 4).reshape(B, S, C_WIDTH)
    return o @ w_out

def memory_attn(h, mem, w_q, w_kv, w_o):
    B, S, _ = h.shape
    M = mem.shape[1]
    q = (h @ w_q).reshape(B, S, MEM_HEADS, MEM_HEAD_DIM)
    k, v = jnp.split(mem @ w_kv, 2, axis=-1)
    k = k.reshape(B, M, MEM_HEADS, MEM_HEAD_DIM)
    v = v.reshape(B, M, MEM_HEADS, MEM_HEAD_DIM)
    s = jnp.einsum('bshd,bmhd->bhsm', q, k).astype(jnp.float32) * (MEM_HEAD_DIM ** -0.5)
    p = jax.nn.softmax(s, axis=-1).astype(v.dtype)
    o = jnp.einsum('bhsm,bmhd->bshd', p, v).reshape(B, S, D_MODEL)
    return o @ w_o

def second_inputs(seed: int = 0) -> dict:
    key = jax.random.key(seed)
    ks = jax.random.split(key, 20)
    nrm = jax.random.normal
    f32 = jnp.float32
    d_sc = D_MODEL ** -0.5
    return {
        "x": nrm(ks[0], (BATCH, SEQ, D_MODEL), f32),
        "mem": nrm(ks[1], (BATCH, MEM_TOKENS, D_MODEL), f32),
        "ln_g": 1.0 + 0.02 * nrm(ks[2], (DEPTH, 4, D_MODEL), f32),
        "ln_b": 0.02 * nrm(ks[3], (DEPTH, 4, D_MODEL), f32),
        "ffn_w_gate": nrm(ks[4], (DEPTH, 2, D_MODEL, D_FF_2), f32) * d_sc,
        "ffn_w_up": nrm(ks[5], (DEPTH, 2, D_MODEL, D_FF_2), f32) * d_sc,
        "ffn_w_down": nrm(ks[6], (DEPTH, 2, D_FF_2, D_MODEL), f32) * (D_FF_2 ** -0.5) * BETA,
        "ab_w_in": nrm(ks[7], (N_EVEN, D_MODEL, AB_IN), f32) * d_sc,
        "ab_w_out": nrm(ks[8], (N_EVEN, AB_OUT, D_MODEL), f32) * (AB_OUT ** -0.5) * BETA,
        "ab_q_gain": 1.0 + 0.02 * nrm(ks[9], (N_EVEN, HEAD_DIM), f32),
        "ab_k_gain": 1.0 + 0.02 * nrm(ks[10], (N_EVEN, HEAD_DIM), f32),
        "ab_sink": 0.5 * nrm(ks[11], (N_EVEN, B_HEADS), f32),
        "c_w_in": nrm(ks[12], (N_ODD, D_MODEL, 3 * C_WIDTH), f32) * d_sc,
        "c_w_out": nrm(ks[13], (N_ODD, C_WIDTH, D_MODEL), f32) * (C_WIDTH ** -0.5) * BETA,
        "c_rpb": 0.1 * nrm(ks[14], (N_ODD, C_HEADS, 2 * NA_KH - 1, 2 * NA_KW - 1), f32),
        "mem_w_q": nrm(ks[15], (DEPTH, D_MODEL, D_MODEL), f32) * d_sc,
        "mem_w_kv": nrm(ks[16], (DEPTH, D_MODEL, 2 * D_MODEL), f32) * d_sc,
        "mem_w_o": nrm(ks[17], (DEPTH, D_MODEL, D_MODEL), f32) * d_sc * BETA,
    }

def second_block(x, mem, ln_g, ln_b, ffn_w_gate, ffn_w_up, ffn_w_down,
              ab_w_in, ab_w_out, ab_q_gain, ab_k_gain, ab_sink,
              c_w_in, c_w_out, c_rpb, mem_w_q, mem_w_kv, mem_w_o):
    S = x.shape[1]
    t = jnp.arange(S)
    row = (t // GRID_W).astype(jnp.float32)
    colp = (t % GRID_W).astype(jnp.float32)
    ang_2d = jnp.concatenate([rope_angles(row, HEAD_DIM // 2), rope_angles(colp, HEAD_DIM // 2)], axis=-1)
    ang_1d = rope_angles(t.astype(jnp.float32), HEAD_DIM)
    for i in range(DEPTH):
        j = i // 2
        y = swiglu_2(x, ffn_w_gate[i, 0], ffn_w_up[i, 0], ffn_w_down[i, 0])
        x = layer_norm_2(ALPHA * x + 0.5 * y, ln_g[i, 0], ln_b[i, 0])
        if i % 2 == 0:
            y = mixer_ab(x, ab_w_in[j], ab_w_out[j], ab_q_gain[j], ab_k_gain[j], ab_sink[j], ang_2d, ang_1d)
        else:
            y = mixer_c(x, c_w_in[j], c_w_out[j], c_rpb[j])
        x = layer_norm_2(ALPHA * x + y, ln_g[i, 1], ln_b[i, 1])
        y = memory_attn(x, mem, mem_w_q[i], mem_w_kv[i], mem_w_o[i])
        x = layer_norm_2(ALPHA * x + y, ln_g[i, 2], ln_b[i, 2])
        y = swiglu_2(x, ffn_w_gate[i, 1], ffn_w_up[i, 1], ffn_w_down[i, 1])
        x = layer_norm_2(ALPHA * x + 0.5 * y, ln_g[i, 3], ln_b[i, 3])
    return x


def setup_inputs(seed=0):
    out = dict(first_inputs(seed))
    for name, value in second_inputs(seed + 1).items():
        if name != "x":
            out[name + "_2"] = value
    return out


def reference(
    x, w_in, gm_ws, gm_bs, gm_ln_g, gm_ln_b, gla_wa2, gla_ba, gla_norm_g, w_out, ln_mix_g,
    ln_mix_b, ffn_w_gate, ffn_w_up, ffn_w_down, router_w, exp_w_gate, exp_w_up, exp_w_down,
    ln_ffn_g, ln_ffn_b, mem_2, ln_g_2, ln_b_2, ffn_w_gate_2, ffn_w_up_2, ffn_w_down_2,
    ab_w_in_2, ab_w_out_2, ab_q_gain_2, ab_k_gain_2, ab_sink_2, c_w_in_2, c_w_out_2, c_rpb_2,
    mem_w_q_2, mem_w_kv_2, mem_w_o_2,
):
    x = first_block(
        x, w_in, gm_ws, gm_bs, gm_ln_g, gm_ln_b, gla_wa2, gla_ba, gla_norm_g, w_out, ln_mix_g,
        ln_mix_b, ffn_w_gate, ffn_w_up, ffn_w_down, router_w, exp_w_gate, exp_w_up, exp_w_down,
        ln_ffn_g, ln_ffn_b,
    )
    return second_block(
        x, mem_2, ln_g_2, ln_b_2, ffn_w_gate_2, ffn_w_up_2, ffn_w_down_2, ab_w_in_2, ab_w_out_2,
        ab_q_gain_2, ab_k_gain_2, ab_sink_2, c_w_in_2, c_w_out_2, c_rpb_2, mem_w_q_2,
        mem_w_kv_2, mem_w_o_2,
    )


_drawn_inputs = setup_inputs


def setup_inputs(seed=0):
    import zlib

    import numpy as np

    out = dict(_drawn_inputs(seed))
    spreads = {}
    factors = {'gm_ln_b': 8.0,
     'gla_ba': 4.957,
     'ab_q_gain_2': 8.0,
     'ab_k_gain_2': 8.0,
     'ab_sink_2': 8.0,
     'c_rpb_2': 8.0}
    for name, (base, spread) in spreads.items():
        noise = np.random.default_rng([zlib.crc32(name.encode()), seed]).standard_normal(out[name].shape)
        drawn = base * np.exp(spread * noise) if base else spread * noise
        out[name] = __import__('jax').numpy.asarray(drawn.astype(out[name].dtype))
    for name, factor in factors.items():
        out[name] = (out[name] * factor).astype(out[name].dtype)
    return out
```

```python
from contextlib import contextmanager

import numpy as np

import concourse.bass as bass
from concourse import mybir

P = 128
F32 = mybir.dt.float32
F32R = mybir.dt.float32r
ALU = mybir.AluOpType
ACT = mybir.ActivationFunctionType
AX = mybir.AxisListType

T = 256
TT = T // P
D = 1024
KT = D // P
DEPTH = 2
LN_EPS, RMS_EPS = 1e-5, 1e-6
ALPHA = (2.0 * DEPTH) ** 0.25

GM_HEADS, GM_DIM = 4, 128
GM_W = GM_HEADS * GM_DIM
GLA_HEADS, GLA_DV, GLA_DK, GLA_RANK, GLA_CHUNK = 4, 128, 64, 16, 64
GLA_W, GLA_KW = GLA_HEADS * GLA_DV, GLA_HEADS * GLA_DK
GLA_TAU = 16.0
NCH = T // GLA_CHUNK
D_FF, D_FFE, N_EXP = 2816, 3584, 8
FC = 256

HD = 64
GRID_W, NA_KH, NA_KW = 64, 8, 16
ROWS = T // GRID_W
C_HEADS = D // HD
MEM_HEADS = 4
BIAS_ROWS = ROWS + 2
NEG = -1e30
WINDOW = 128

RING = 6
MIX_PARTS = 3
SLOT = 2048

CONST = {}


def build_constants():
    cols = []

    def add(name, a):
        a = np.asarray(a, np.float32).reshape(P, -1)
        start = sum(c.shape[1] for c in cols)
        CONST[name] = (start, a.shape[1])
        cols.append(a)

    eye = np.eye(P, dtype=np.float32)
    add("identity", eye)
    add("alpha_identity", eye * np.float32(ALPHA))
    add("alpha2_identity", eye * np.float32(2 * np.float32(ALPHA)))
    q = np.arange(T).reshape(TT, P).T[:, :, None]
    add("window", np.where(np.abs(q - np.arange(T)) <= WINDOW, 0.0, NEG))
    w = np.arange(P)[:, None] % GRID_W
    first = np.clip(w - NA_KW // 2, 0, GRID_W - NA_KW)
    k = np.arange(GRID_W)[None]
    add("neighbours", np.where((k >= first) & (k < first + NA_KW), 0.0, NEG)[:, ::-1])
    t = np.arange(T)

    def angles(pos, dim):
        inv = np.float32(10000.0) ** (-np.arange(0, dim, 2, dtype=np.float32) / np.float32(dim))
        return pos.astype(np.float32)[:, None] * inv[None].astype(np.float32)

    ang_2d = np.concatenate([angles(t // GRID_W, HD // 2), angles(t % GRID_W, HD // 2)], axis=-1)
    for name, ang in (("2d", ang_2d), ("1d", angles(t, HD))):
        for f, fn in (("cos", np.cos), ("sin", np.sin)):
            add(f"{f}_{name}", fn(ang).reshape(TT, P, HD // 2).transpose(1, 0, 2))
    add("scan_keep", np.tile((np.arange(2 * T) % GLA_CHUNK != 0).astype(np.float32), (P, 1)))
    e = np.arange(N_EXP)
    add("earlier_expert", np.tile((e[None, :] < e[:, None]).astype(np.float32).reshape(1, -1), (P, 1)))
    return np.concatenate(cols, axis=1)


CONST_ARRAY = build_constants()


class Token:
    def __init__(self, sem, value, loops):
        self.sem, self.value, self.loops = sem, value, loops


class Loop:
    def __init__(self, per, var):
        self.per, self.var = per, var


class Counter:
    def __init__(self, nc):
        self.nc = nc
        self.count = {}
        self.tokens = []
        self.active = ()
        self.waited = {}

    def mark(self, ins, sem, amount=1):
        ins.then_inc(sem, amount)
        self.count[sem] = self.count.get(sem, 0) + amount
        token = Token(sem, self.count[sem], self.active)
        self.tokens.append(token)
        return token

    def after(self, eng, *tokens):
        for t in tokens:
            if t is None:
                continue
            if isinstance(t, (list, tuple)):
                self.after(eng, *t)
                continue
            key = (eng.name, t.sem, t.loops)
            if self.waited.get(key, 0) >= t.value:
                continue
            self.waited[key] = t.value
            value = t.value
            for loop in t.loops:
                assert loop in self.active
                if loop.per.get(t.sem, 0):
                    value = (loop.var - 1) * loop.per[t.sem] + value
            eng.eng.wait_ge(t.sem, value)

    @contextmanager
    def repeat(self, before, times):
        per = {s: n - before.get(s, 0) for s, n in self.count.items() if n != before.get(s, 0)}
        entry = dict(self.count)
        loop = Loop(per, None)
        for t in self.tokens:
            if t.value > before.get(t.sem, 0):
                t.loops = t.loops + (loop,)
        self.waited = {}
        with self.nc.Fori(1, times) as var:
            loop.var = var
            self.active = self.active + (loop,)
            yield var
            self.active = self.active[:-1]
        for s, n in self.count.items():
            assert n - entry.get(s, 0) == per.get(s, 0), "the body must repeat the hand-run one"
            self.count[s] = n + (times - 2) * per.get(s, 0)
        for t in self.tokens:
            if loop in t.loops:
                t.loops = tuple(x for x in t.loops if x is not loop)
                t.value += (times - 2) * per.get(t.sem, 0)
        self.waited = {}


class Engine:
    def __init__(self, name, eng, sem):
        self.name, self.eng, self.sem = name, eng, sem


class Stream:
    def __init__(self, loads, parts):
        self.loads, self.parts, self.ready, self.sent = loads, parts, [], 0


class Program:
    def __init__(self, nc, a, out, stop=None):
        self.nc, self.a, self.out, self.stop = nc, a, out, stop
        self.c = Counter(nc)
        self.pe = Engine("pe", nc.tensor, nc.alloc_semaphore("tensor_steps"))
        self.act = Engine("act", nc.scalar, nc.alloc_semaphore("scalar_steps"))
        self.dve = Engine("dve", nc.vector, nc.alloc_semaphore("vector_steps"))
        self.pool = Engine("pool", nc.gpsimd, nc.alloc_semaphore("gpsimd_steps"))
        self.sp = Engine("sp", nc.sync, None)
        self.landed_sem = [nc.alloc_semaphore(f"slot{i}_landed") for i in range(RING)]
        self.small_sem = nc.alloc_semaphore("small_loads")
        self.x_sem = nc.alloc_semaphore("x_landed")
        self.const_sem = nc.alloc_semaphore("consts_landed")
        self.last_gb_sem = nc.alloc_semaphore("last_gain_landed")
        self.loads_sem = nc.alloc_semaphore("slots_requested")
        self.out_sem = nc.alloc_semaphore("stores")
        self.place_memory()

    def place_memory(self):
        nc = self.nc
        base = (nc.sbuf_base + 31) // 32 * 32
        at = [base]

        def put(name, shape, dt=F32, offset=None):
            words = int(np.prod(shape[1:]))
            if offset is None:
                offset = at[0]
                at[0] += (words * 4 + 31) // 32 * 32
            return nc.alloc_sbuf_tensor_at(name, shape, dt, offset=offset)

        self.raw = [put(f"raw{i}", [P, SLOT]) for i in range(RING)]
        self.x_hi = put("x_hi", [P, KT, T], F32R)
        self.x_lo = put("x_lo", [P, KT, T], F32R)
        self.xf = [put(f"x_affine{i}", [P, 4, P]) for i in range(2)]
        self.xhat = put("xhat", [P, TT, D])
        self.consts = put("consts", [P, CONST_ARRAY.shape[1]])
        self.resid_hi = put("resid_hi", [P, 2, P], F32R)
        self.resid_lo = put("resid_lo", [P, 2, P], F32R)
        self.rows = put("param_rows", [P, 2, P])
        self.cols = put("param_cols", [P, 2, P])
        self.stats = put("stats", [P, TT, 2, 6])
        self.mv = put("mean_var", [P, TT, 2])
        self.rstd = put("rstd", [P, TT])
        self.minus_half = put("minus_half", [P, 32])
        self.small = put("small", [P, 512])
        self.sink = put("sink", [P, 8])
        self.gains = put("gains", [P, 2, HD])
        self.gates = put("gates", [P, TT, N_EXP])
        self.small2 = put("chunk_spans", [P, 2, 6])
        self.small3 = put("inverse_norms", [P, 32])
        self.vstats = put("gating_stats", [P, TT, GM_HEADS, 8])
        self.att_stats = put("softmax_stats", [P, 16, 3, TT])
        self.router_raw = put("router_raw", [P, KT, N_EXP])
        self.router_hi = put("router_hi", [P, KT, N_EXP], F32R)
        self.router_lo = put("router_lo", [P, KT, N_EXP], F32R)
        self.part_hi = [None] * RING
        self.part_lo = [None] * RING
        for i in range(RING):
            if i == MIX_PARTS:
                arena = at[0]
            self.part_hi[i] = put(f"part_hi{i}", [P, SLOT], F32R)
            self.part_lo[i] = put(f"part_lo{i}", [P, SLOT], F32R)
        self.silu = [put(f"silu{i}", [P, FC]) for i in range(2)]
        self.h = [put(f"h{i}", [P, FC]) for i in range(2)]
        self.hT_hi = [[put(f"hT_hi{i}{t}", [P, 2, P], F32R) for t in range(TT)] for i in range(2)]
        self.hT_lo = [[put(f"hT_lo{i}{t}", [P, 2, P], F32R) for t in range(TT)] for i in range(2)]
        end = at[0]
        assert end <= nc.sbuf_usable_end, (end, nc.sbuf_usable_end)

        self.overlay_at = {}

        def overlay(items):
            o = arena
            made = {}
            for name, shape, dt, over in items:
                words = int(np.prod(shape[1:]))
                if over is None:
                    made[name] = (nc.alloc_sbuf_tensor_at(name, shape, dt, offset=o), o)
                    o += (words * 4 + 31) // 32 * 32
                else:
                    made[name] = (nc.alloc_sbuf_tensor_at(name, shape, dt, offset=made[over][1]), made[over][1])
            assert o <= end, (o - arena, end - arena)
            self.overlay_at.update({k: v[1] for k, v in made.items()})
            return {k: v[0] for k, v in made.items()}

        self.gla = overlay([
            ("u", [P, TT, GM_W], F32, None), ("vg", [P, TT, GM_W], F32, None),
            ("v_gla", [P, TT, GLA_W], F32, None), ("silu_g", [P, TT, GLA_W], F32, None),
            ("q_heads", [P, 2, 2, T], F32, None), ("k_inv", [P, 2, T], F32, None),
            ("k_for_chunk", [P, NCH, 2, T], F32, None), ("scoresT", [P, TT, GLA_HEADS, T], F32, None),
            ("log_a", [P, 2, T], F32, None), ("tmp_a", [P, 2, T], F32, None),
            ("b_cum", [P, 2, T], F32, None), ("exp_b", [P, 2, T], F32, None),
            ("ws", [P, GM_HEADS, P], F32, None), ("wsT", [P, GM_HEADS, P], F32, None),
            ("gm_g", [P, GM_W], F32, None), ("gm_b", [P, GM_W], F32, None),
            ("a_raw", [P, KT, GLA_RANK], F32, None),
            ("a_hi", [P, KT, GLA_RANK], F32R, None), ("a_lo", [P, KT, GLA_RANK], F32R, None),
            ("wa2", [GLA_RANK, GLA_KW], F32, None),
            ("cat_hi_gla", [P, KT, T], F32R, "k_for_chunk"), ("cat_lo_gla", [P, KT, T], F32R, "scoresT"),
            ("norm_g", [P, GLA_W], F32, "ws"),
        ])
        self.qkv = overlay([
            ("qT", [P, KT, T], F32, None), ("kT", [P, KT, T], F32, None), ("v_att", [P, TT, D], F32, None),
            ("p0", [P, TT, T], F32, None), ("p1", [P, TT, T], F32, None),
            ("pT0", [P, TT, T], F32, None), ("pT1", [P, TT, T], F32, None),
            ("bias", [P, C_HEADS, BIAS_ROWS, GRID_W], F32, None),
            ("cat_hi_qkv", [P, KT, T], F32R, "qT"), ("cat_lo_qkv", [P, KT, T], F32R, "kT"),
        ])
        self.ab = overlay([
            ("qT_ab", [P, KT, T], F32, None), ("kT_ab", [P, 4, T], F32, None),
            ("spare", [P, 4, T], F32, None), ("proj", [P, TT, 1536], F32, None),
            ("p0_ab", [P, TT, T], F32, None), ("p1_ab", [P, TT, T], F32, None),
            ("pT0_ab", [P, TT, T], F32, None), ("pT1_ab", [P, TT, T], F32, None),
            ("rot", [P, TT, 12, HD], F32, None),
            ("cat_lo_ab", [P, KT, T], F32R, None),
            ("cat_hi_ab", [P, KT, T], F32R, "qT_ab"),
        ])
        self.mem_row, self.mem_hi, self.mem_lo = (
            nc.alloc_sbuf_tensor_at(name, [P, *shape], dt, offset=self.overlay_at["bias"] + i * D * TT * 4)
            for i, (name, shape, dt) in enumerate((("mem_row", (TT, D), F32), ("mem_hi", (KT, T), F32R), ("mem_lo", (KT, T), F32R))))
        self.bank = [nc.alloc_psum_tensor(f"bank{i}", [P, 512], F32) for i in range(8)]
        self.bank_free = [None] * 8
        self.raw_free = [None] * RING
        self.part_free = [None] * RING
        self.raw_at = self.part_at = 0
        self.x_ready = [None] * 4

    def const(self, name):
        start, n = CONST[name]
        return self.consts[:, start:start + n]

    def after(self, eng, *tokens):
        self.c.after(eng, *tokens)

    def done(self, eng, ins):
        return self.c.mark(ins, eng.sem)

    def do(self, eng, tokens, ins):
        self.c.after(eng, *tokens)
        return self.c.mark(ins(eng.eng), eng.sem)

    def product(self, out, stat_hi, stat_lo, move_hi, move_lo, start=False, stop=False):
        pe = self.nc.tensor
        pe.matmul(out, stat_hi, move_hi, start=start, stop=False, skip_group_check=True)
        pe.matmul(out, stat_hi, move_lo, start=False, stop=False, skip_group_check=True)
        return pe.matmul(out, stat_lo, move_hi, start=False, stop=stop, skip_group_check=True)

    def acc(self, tt, half):
        return self.bank[2 * tt + half]

    def load_and_split(self, loads, parts):
        r = self.raw_at % RING
        self.raw_at += 1
        if self.part_at >= parts:
            self.part_at = 0
        s = self.part_at
        self.part_at += 1
        raw, hi, lo = self.raw[r], self.part_hi[s], self.part_lo[s]
        self.after(self.sp, self.raw_free[r])
        if self.raw_free[r] is not None and self.raw_free[r].loops:
            self.nc.sync.sem_inc(self.loads_sem, 1)
        words = 0
        for view, src in loads:
            dst, words = view(raw)
            landed = self.c.mark(self.nc.sync.dma_start(dst, src), self.landed_sem[r], 16)
        rounded = self.do(self.act, [landed, self.part_free[s]],
                          lambda e: e.activation(hi[:, 0:words], raw[:, 0:words], ACT.Copy))
        split = self.do(self.dve, [landed, rounded, self.part_free[s]],
                        lambda e: e.tensor_tensor(lo[:, 0:words], raw[:, 0:words],
                                                  hi[:, 0:words].bitcast(F32), ALU.subtract))
        self.raw_free[r] = split
        return s, split

    def stream_step(self, st):
        if st.sent < len(st.loads):
            st.ready.append(self.load_and_split(st.loads[st.sent], st.parts))
            st.sent += 1

    def take(self, st):
        s, split = st.ready.pop(0)
        self.after(self.pe, split)
        return s

    def release(self, s, token):
        self.part_free[s] = token

    @staticmethod
    def square_loads(w, col, ncols=512):
        out = []
        for kh in range(2):
            src = w[kh * 512:(kh + 1) * 512, col:col + ncols].rearrange("(k p) n -> p k n", p=P)
            out.append([(lambda raw, n=ncols: (raw[:, 0:4 * n].rearrange("p (k n) -> p k n", k=4), 4 * n), src)])
        return out

    def square_stream(self, blocks):
        return Stream([x for w, col in blocks for x in self.square_loads(w, col)], MIX_PARTS)

    def block_token_major(self, st, banks, hi, lo, ready, start=True, ahead=True):
        pe = self.pe
        done = [None] * TT
        for kh in range(2):
            s = self.take(st)
            for tt in range(TT):
                if kh == 0:
                    self.after(pe, self.bank_free[banks[tt]])
                self.after(pe, ready[tt * 2 + kh])
                for k in range(4):
                    kk = kh * 4 + k
                    mm = self.product(self.bank[banks[tt]][:, :], hi[:, kk, tt * P:(tt + 1) * P],
                                      lo[:, kk, tt * P:(tt + 1) * P],
                                      self.part_hi[s][:, k * 512:(k + 1) * 512],
                                      self.part_lo[s][:, k * 512:(k + 1) * 512],
                                      start=(start and kk == 0), stop=(kk == KT - 1))
                if kh == 1 or tt == TT - 1:
                    done[tt] = self.done(pe, mm)
            self.release(s, done[TT - 1])
            self.stream_step(st)
        return done

    def block_transposed(self, st, banks, hi, lo, ready):
        pe = self.pe
        for kh in range(2):
            s = self.take(st)
            for b in range(2):
                if kh == 0:
                    self.after(pe, self.bank_free[banks[b]])
                self.after(pe, [ready[tt * 2 + kh] for tt in range(TT)])
                for m in (2 * b, 2 * b + 1):
                    for k in range(4):
                        kk = kh * 4 + k
                        w = slice(k * 512 + m * P, k * 512 + (m + 1) * P)
                        mm = self.product(self.bank[banks[b]][:, (m % 2) * T:(m % 2 + 1) * T],
                                          self.part_hi[s][:, w], self.part_lo[s][:, w],
                                          hi[:, kk, :], lo[:, kk, :],
                                          start=(kk == 0 and m % 2 == 0), stop=(kk == KT - 1))
            done = self.done(pe, mm)
            self.release(s, done)
            self.stream_step(st)
        return done

    def residual(self, scale):
        for tt in range(TT):
            for half in range(2):
                b = 2 * tt + half
                self.after(self.pe, self.bank_free[b], self.x_ready[b])
                for k in range(4):
                    kk = half * 4 + k
                    self.product(self.bank[b][:, k * P:(k + 1) * P],
                                 self.x_hi[:, kk, tt * P:(tt + 1) * P], self.x_lo[:, kk, tt * P:(tt + 1) * P],
                                 self.resid_hi[:, scale, :], self.resid_lo[:, scale, :], start=(k == 0))

    def out_projection(self, st, hi, lo, ready, scale=0):
        self.residual(scale)
        for half in range(2):
            done = self.block_token_major(st, [half, 2 + half], hi, lo, ready, start=False)
        for i in range(MIX_PARTS, RING):
            self.part_free[i] = done[1]
        return done

    def transpose_block(self, src, tt, half, bank, ready):
        self.after(self.pe, self.bank_free[bank], ready)
        for k in range(4):
            c = (half * 4 + k) * P
            mm = self.nc.tensor.transpose(self.bank[bank][:, k * P:(k + 1) * P], src[:, tt, c:c + P],
                                          self.const("identity"))
        return self.done(self.pe, mm)

    def split_from_psum(self, bank_ap, hi, lo, ready, waits=()):
        h = self.do(self.act, [ready, *waits], lambda e: e.activation(hi, bank_ap, ACT.Copy))
        return self.do(self.dve, [h, ready, *waits],
                       lambda e: e.tensor_tensor(lo, bank_ap, hi.bitcast(F32), ALU.subtract))

    def layer_norm(self, acc_done, g, b, eps, final=False):
        mean = []
        for tt in range(TT):
            for half in range(2):
                st = self.do(self.dve, [acc_done[tt]],
                             lambda e: e.bn_stats(self.stats[:, tt, half, :], self.acc(tt, half)[:, :]))
            agg = self.do(self.dve, [st], lambda e: e.bn_aggr(self.mv[:, tt, :], self.stats[:, tt, :, :]))
            eps_added = self.do(self.dve, [agg], lambda e: e.tensor_scalar(
                self.rstd[:, tt:tt + 1], self.mv[:, tt, 1:2], eps, None, ALU.add))
            inv = self.do(self.pool, [eps_added], lambda e: e.tensor_tensor(
                self.rstd[:, tt:tt + 1], self.rstd[:, tt:tt + 1], self.minus_half[:, 0:1], ALU.pow))
            mean.append(inv)
        normed = {}
        for tt in range(TT):
            for half in range(2):
                normed[tt, half] = self.do(self.dve, [mean[tt], self.xhat_free], lambda e: e.tensor_scalar(
                    self.xhat[:, tt, half * 512:(half + 1) * 512], self.acc(tt, half)[:, :],
                    self.mv[:, tt, 0:1], self.rstd[:, tt:tt + 1], ALU.subtract, ALU.mult))
                self.bank_free[2 * tt + half] = normed[tt, half]
        if final:
            return normed
        for tt in range(TT):
            for half in range(2):
                n = 2 * tt + half
                bank = 4 + n
                turned = self.transpose_block(self.xhat, tt, half, bank, normed[tt, half])
                xf = self.xf[n % 2]
                for k in range(4):
                    kk = half * 4 + k
                    scaled = self.do(self.act, [turned, self.xf_free[n % 2]], lambda e: e.activation(
                        xf[:, k, :], self.bank[bank][:, k * P:(k + 1) * P], ACT.Identity,
                        bias=self.cols[:, b[0], b[1] + kk:b[1] + kk + 1],
                        scale=self.cols[:, g[0], g[1] + kk:g[1] + kk + 1]))
                self.bank_free[bank] = scaled
                hi = self.x_hi[:, half * 4:half * 4 + 4, tt * P:(tt + 1) * P]
                lo = self.x_lo[:, half * 4:half * 4 + 4, tt * P:(tt + 1) * P]
                rounded = self.do(self.dve, [scaled, acc_done], lambda e: e.tensor_copy(hi, xf[:, :, :]))
                self.x_ready[n] = self.do(self.dve, [rounded], lambda e: e.tensor_tensor(
                    lo, xf[:, :, :], hi.bitcast(F32), ALU.subtract))
                self.xf_free[n % 2] = self.x_ready[n]
        self.xhat_free = turned

    def store_final(self, normed, g_dram, b_dram):
        gb = [self.raw[0][:, 0:D], self.raw[1][:, 0:D]]
        self.after(self.sp, self.raw_free[0], self.raw_free[1])
        for dst, src in zip(gb, (g_dram, b_dram)):
            landed = self.c.mark(self.nc.sync.dma_start(dst, src.partition_broadcast(P)), self.last_gb_sem, 16)
        for tt in range(TT):
            for half in range(2):
                cols = slice(half * 512, (half + 1) * 512)
                x = self.xhat[:, tt, cols]
                m = self.do(self.dve, [normed[tt, half], landed],
                            lambda e: e.tensor_tensor(x, x, gb[0][:, cols], ALU.mult))
                s = self.do(self.dve, [m], lambda e: e.tensor_tensor(x, x, gb[1][:, cols], ALU.add))
                self.after(self.sp, s)
                stored = self.c.mark(self.nc.sync.dma_start(
                    self.out[0, tt * P:(tt + 1) * P, cols], x), self.out_sem, 16)
        self.after(self.sp, stored)

    def ffn_loads_up(self, w_gate, w_up, col):
        loads = []
        for kh in range(2):
            one = []
            for n, w in enumerate((w_gate, w_up)):
                src = w(slice(kh * 512, (kh + 1) * 512), bass.ds(col, FC)).rearrange("(k p) n -> p k n", p=P)
                one.append((lambda raw, n=n: (raw[:, :].rearrange("p (k m n) -> p k m n", k=4, m=2)[:, :, n, :], SLOT), src))
            loads.append(one)
        return loads

    def ffn_load_down(self, w_down, row):
        src = w_down(bass.ds(row, FC), slice(0, D)).rearrange("(j p) n -> p j n", p=P)
        return [(lambda raw: (raw[:, :].rearrange("p (j n) -> p j n", j=2), SLOT), src)]

    def ffn_up(self, tt, slots, gate=None):
        bank = 4 + tt
        pe = self.pe
        self.after(pe, self.bank_free[bank])
        for kh in range(2):
            s, split = slots[kh]
            self.after(pe, split, self.x_ready[2 * tt + kh])
            for k in range(4):
                kk = kh * 4 + k
                mm = self.product(self.bank[bank][:, :], self.x_hi[:, kk, tt * P:(tt + 1) * P],
                                  self.x_lo[:, kk, tt * P:(tt + 1) * P],
                                  self.part_hi[s][:, k * 512:(k + 1) * 512],
                                  self.part_lo[s][:, k * 512:(k + 1) * 512],
                                  start=(kk == 0), stop=(kk == KT - 1))
            token = self.done(pe, mm)
            if tt == TT - 1:
                self.release(s, token)
        return token

    def ffn_act(self, tt, up_done, gate):
        bank = 4 + tt
        act = self.do(self.act, [up_done, self.h_free[tt]], lambda e: e.activation(
            self.silu[tt][:, :], self.bank[bank][:, 0:FC], ACT.Silu))
        if gate is None:
            f = lambda e: e.tensor_tensor(self.h[tt][:, :], self.silu[tt][:, :], self.bank[bank][:, FC:2 * FC], ALU.mult)
        else:
            f = lambda e: e.scalar_tensor_tensor(out=self.h[tt][:, :], in0=self.silu[tt][:, :], scalar=gate(tt),
                                                 in1=self.bank[bank][:, FC:2 * FC], op0=ALU.mult, op1=ALU.mult)
        h = self.do(self.dve, [act, up_done, self.hT_turned[tt]], f)
        self.bank_free[bank] = h
        self.h_free[tt] = h
        return h

    def ffn_turn(self, tt, par, h_ready):
        bank = 6 + tt
        self.after(self.pe, h_ready, self.bank_free[bank])
        for j in range(2):
            mm = self.nc.tensor.transpose(self.bank[bank][:, j * P:(j + 1) * P],
                                          self.h[tt][:, j * P:(j + 1) * P], self.const("identity"))
        self.hT_turned[tt] = turned = self.done(self.pe, mm)
        hi, lo = self.hT_hi[par][tt][:, :, :], self.hT_lo[par][tt][:, :, :]
        src = self.bank[bank][:, 0:FC].rearrange("p (j t) -> p j t", j=2)
        ready = self.split_from_psum(src, hi, lo, turned, [self.hT_used[par][tt]])
        self.bank_free[bank] = ready
        return ready

    def ffn_down(self, tt, par, slot, hT_ready, start=False):
        s, split = slot
        self.after(self.pe, split, hT_ready)
        for j in range(2):
            for half in range(2):
                if start and j == 0:
                    self.after(self.pe, self.bank_free[2 * tt + half])
                mm = self.product(self.acc(tt, half)[:, :], self.hT_hi[par][tt][:, j, :], self.hT_lo[par][tt][:, j, :],
                                  self.part_hi[s][:, j * D + half * 512:j * D + (half + 1) * 512],
                                  self.part_lo[s][:, j * D + half * 512:j * D + (half + 1) * 512])
        token = self.done(self.pe, mm)
        self.hT_used[par][tt] = token
        if tt == TT - 1:
            self.release(s, token)
        return token

    def ffn_prefetch(self, w):
        return [self.load_and_split(x, RING) for x in self.ffn_loads_up(w[0], w[1], 0)]

    def ffn(self, weights, n_chunks, up_slots, gate=None, following=None):
        w_gate, w_up, w_down = weights
        state = {"up": up_slots}

        def phase(c, par, first=False, last=False):
            slots = state["up"]
            nxt = None
            if not last:
                nxt = [self.load_and_split(x, RING) for x in self.ffn_loads_up(w_gate, w_up, (c + 1) * FC)]
            elif following is not None:
                nxt = [self.load_and_split(x, RING) for x in following]
            up0 = self.ffn_up(0, slots)
            h0 = self.ffn_act(0, up0, gate)
            down_slot = self.load_and_split(self.ffn_load_down(w_down, c * FC), RING)
            up1 = self.ffn_up(1, slots)
            h1 = self.ffn_act(1, up1, gate)
            t0 = self.ffn_turn(0, par, h0)
            acc = None
            if not first:
                prev = state["down"]
                for tt in range(TT):
                    self.ffn_down(tt, 1 - par, prev[0], prev[1][tt])
            t1 = self.ffn_turn(1, par, h1)
            state["down"] = (down_slot, [t0, t1])
            state["up"] = nxt

        phase(0, 0, first=True)
        units = (n_chunks - 2) // 2
        before = dict(self.c.count)
        phase(1, 1)
        phase(2, 0)
        with self.c.repeat(before, units) as i:
            phase(i * 2 + 1, 1)
            phase(i * 2 + 2, 0)
        for c in range(1 + 2 * units, n_chunks):
            phase(c, c % 2, last=(c == n_chunks - 1))
        par = (n_chunks - 1) % 2
        slot, turned = state["down"]
        done = [self.ffn_down(tt, par, slot, turned[tt]) for tt in range(TT)]
        return done, state["up"]

    def load_small(self, dst, src, waits=()):
        self.after(self.pool, *waits)
        return self.c.mark(self.nc.gpsimd.dma_start(dst, src), self.small_sem, 16)

    def start(self):
        a, nc = self.a, self.nc
        self.xhat_free = None
        self.xf_free = [None, None]
        self.h_free = [None] * TT
        self.hT_turned = [None] * TT
        self.hT_used = [[None] * TT for _ in range(2)]
        x_landed = self.c.mark(nc.sync.dma_start(self.xhat[:, :, :], a["x"][0].rearrange("(t p) d -> p t d", p=P)),
                               self.x_sem, 16)
        c_landed = self.c.mark(nc.sync.dma_start(self.consts[:, :], a["consts"]), self.const_sem, 16)
        zeroed = self.do(self.pool, [], lambda e: e.memset(self.rows[:, :, :], 0.0))
        halves = self.do(self.pool, [], lambda e: e.memset(self.minus_half[:, :], -0.5))
        self.after(self.pool, zeroed, halves)
        at = 0
        self.col_of = {}
        for name, n in (("ln_mix_g", 16), ("ln_mix_b", 16), ("ln_ffn_g", 16), ("ln_ffn_b", 16), ("gm_bs", 8), ("gla_ba", 4)):
            src = a[name]
            src = src.rearrange("l h t -> (l h) t") if name == "gm_bs" else src.rearrange("l (k p) -> (l k) p", p=P)
            self.load_small(self.rows[at:at + n, 0, :], src)
            self.col_of[name] = (0, at)
            at += n
        for i, name in enumerate(("ln_g_2", "ln_b_2")):
            self.load_small(self.rows[i * 64:(i + 1) * 64, 1, :], a[name].rearrange("l s (k p) -> (l s k) p", p=P))
            self.col_of[name] = (1, i * 64)
        self.load_small(self.sink[:, :], a["ab_sink_2"][0].partition_broadcast(P))
        self.load_small(self.gains[:, 0, :], a["ab_q_gain_2"][0].partition_broadcast(P))
        rows_landed = self.load_small(self.gains[:, 1, :], a["ab_k_gain_2"][0].partition_broadcast(P))
        self.small_loaded = rows_landed
        for i, name in enumerate(("alpha_identity", "alpha2_identity")):
            h = self.do(self.act, [c_landed, rows_landed], lambda e: e.activation(self.resid_hi[:, i, :], self.const(name), ACT.Copy))
            self.resid = self.do(self.dve, [h], lambda e: e.tensor_tensor(
                self.resid_lo[:, i, :], self.const(name), self.resid_hi[:, i, :].bitcast(F32), ALU.subtract))
        self.after(self.pe, rows_landed, self.resid)
        for i in range(2):
            mm = nc.tensor.transpose(self.bank[0][:, i * P:(i + 1) * P], self.rows[:, i, :], self.const("identity"))
        turned = self.done(self.pe, mm)
        self.bank_free[0] = self.do(self.dve, [turned], lambda e: e.tensor_copy(
            self.cols[:, :, :], self.bank[0][:, 0:2 * P].rearrange("p (i c) -> p i c", i=2)))
        self.after(self.act, self.bank_free[0])
        self.after(self.pool, self.bank_free[0], c_landed)
        self.after(self.dve, c_landed)
        self.to_xT(self.xhat, [x_landed] * 2)

    def to_xT(self, src, ready):
        for tt in range(TT):
            for half in range(2):
                n = 2 * tt + half
                turned = self.transpose_block(src, tt, half, 4 + n, ready[tt])
                hi = self.x_hi[:, half * 4:half * 4 + 4, tt * P:(tt + 1) * P]
                lo = self.x_lo[:, half * 4:half * 4 + 4, tt * P:(tt + 1) * P]
                self.x_ready[n] = self.split_from_psum(
                    self.bank[4 + n][:, :].rearrange("p (k t) -> p k t", k=4), hi, lo, turned)
                self.bank_free[4 + n] = self.x_ready[n]
        self.xhat_free = turned

    def gla_stream(self, layer):
        w = self.a["w_in"][layer]
        cols = [1024, 0, 512, 1536, 2048]
        w_out = self.a["w_out"][layer]
        return self.square_stream([(w, c) for c in cols] + [(w_out, 0), (w_out, 512)])

    def hybrid_mixer(self, layer, st, free):
        a, g, nc = self.a, self.gla, self.nc
        dve, act, pool, pe = self.dve, self.act, self.pool, self.pe
        self.load_small(g["a_raw"][:, :, :], a["w_in"][layer][:, 2560:2576].rearrange("(k p) n -> p k n", p=P), [free])
        self.load_small(g["wa2"][:, :], a["gla_wa2"][layer])
        self.load_small(g["ws"][:, :, :], a["gm_ws"][layer].rearrange("h t s -> t h s"))
        self.load_small(g["gm_g"][:, :], a["gm_ln_g"][layer].partition_broadcast(P))
        loaded = self.load_small(g["gm_b"][:, :], a["gm_ln_b"][layer].partition_broadcast(P))
        k_zero = self.do(pool, [free], lambda e: e.memset(g["k_for_chunk"][:, :, :, :], 0.0))
        q_zero = self.do(pool, [free], lambda e: e.memset(g["q_heads"][:, :, :, :], 0.0))
        alr = self.small[:, 0:2 * P].rearrange("p (t c) -> p t c", t=TT)
        alr_zero = self.do(pool, [self.small_free], lambda e: e.memset(alr, 0.0))
        masked = self.do(pool, [loaded], lambda e: e.affine_select(
            out=g["ws"][:, :, :], in_=g["ws"][:, :, :], compare_op=ALU.is_ge, fill=0.0, base=0,
            pattern=[[0, GM_HEADS], [-1, P]], channel_multiplier=1))
        a_hi = self.do(act, [loaded], lambda e: e.activation(g["a_hi"][:, :, :], g["a_raw"][:, :, :], ACT.Copy))
        a_lo = self.do(dve, [a_hi], lambda e: e.tensor_tensor(
            g["a_lo"][:, :, :], g["a_raw"][:, :, :], g["a_hi"][:, :, :].bitcast(F32), ALU.subtract))
        self.after(pe, a_lo, self.x_ready, self.bank_free[4])
        for tt in range(TT):
            for k in range(KT):
                mm = self.product(self.bank[4][:, tt * 16:tt * 16 + 16], self.x_hi[:, k, tt * P:(tt + 1) * P],
                                  self.x_lo[:, k, tt * P:(tt + 1) * P], g["a_hi"][:, k, :], g["a_lo"][:, k, :],
                                  start=(k == 0 and tt == 0), stop=(k == KT - 1))
        a_done = self.done(pe, mm)
        a_copied = self.do(dve, [a_done, alr_zero], lambda e: e.tensor_copy(
            alr[:, :, 0:GLA_RANK], self.bank[4][:, 0:32].rearrange("p (t c) -> p t c", t=TT)))
        self.bank_free[4] = a_copied
        qk_done = self.block_transposed(st, [0, 1], self.x_hi, self.x_lo, self.x_ready)
        self.after(pe, a_copied, self.bank_free[5])
        for tt in range(TT):
            mm = nc.tensor.transpose(self.bank[5][:, tt * P:(tt + 1) * P], alr[:, tt, :], self.const("identity"))
        turned = self.done(pe, mm)
        alrT = self.small[0:GLA_RANK, 256:512]
        alrT_ready = self.do(dve, [turned, self.small_free], lambda e: e.tensor_copy(alrT, self.bank[5][0:GLA_RANK, 0:T]))
        self.bank_free[5] = alrT_ready
        self.after(pe, alrT_ready, self.bank_free[6])
        for dt in range(2):
            mm = nc.tensor.matmul(self.bank[6][:, dt * T:(dt + 1) * T], g["wa2"][:, dt * P:(dt + 1) * P], alrT,
                                  start=True, stop=True, skip_group_check=True)
        z_done = self.done(pe, mm)
        self.small_free = z_done
        log_a, tmp, b_cum, exp_b = g["log_a"], g["tmp_a"], g["b_cum"], g["exp_b"]
        ba_t, ba_c = self.col_of["gla_ba"]
        for dt in range(2):
            c = ba_c + 2 * layer + dt
            z = self.do(dve, [z_done, free], lambda e: e.tensor_scalar(
                log_a[:, dt, :], self.bank[6][:, dt * T:(dt + 1) * T], self.cols[:, ba_t, c:c + 1], None, ALU.add))
        self.bank_free[6] = z
        ab = self.do(act, [z], lambda e: e.activation(tmp[:, :, :], log_a[:, :, :], ACT.Abs))
        ex = self.do(act, [ab], lambda e: e.activation(tmp[:, :, :], tmp[:, :, :], ACT.Exp, scale=-1.0))
        ln = self.do(act, [ex], lambda e: e.activation(tmp[:, :, :], tmp[:, :, :], ACT.Ln, bias=1.0))
        mn = self.do(dve, [z, ab], lambda e: e.tensor_scalar(log_a[:, :, :], log_a[:, :, :], 0.0, None, ALU.min))
        la = self.do(dve, [mn, ln], lambda e: e.tensor_tensor(log_a[:, :, :], log_a[:, :, :], tmp[:, :, :], ALU.subtract))
        flat = lambda t: t[:, :, :].rearrange("p d t -> p (d t)")
        scan = self.do(dve, [la], lambda e: e.tensor_tensor_scan(
            flat(b_cum), self.const("scan_keep"), flat(log_a), 0.0, ALU.mult, ALU.add))
        inv = 1.0 / GLA_TAU
        eb = self.do(act, [scan], lambda e: e.activation(exp_b[:, :, :], b_cum[:, :, :], ACT.Exp, scale=inv))
        enb = self.do(act, [scan, la], lambda e: e.activation(tmp[:, :, :], b_cum[:, :, :], ACT.Exp, scale=-inv))
        tot = b_cum[:, :, :].rearrange("p d (c j) -> p d c j", j=GLA_CHUNK)[:, :, :, GLA_CHUNK - 1]
        span = self.small2
        sp1 = self.do(dve, [scan, self.small2_free], lambda e: e.tensor_copy(span[:, :, 0:1], tot[:, :, 0:1]))
        self.do(dve, [], lambda e: e.tensor_copy(span[:, :, 2:3], tot[:, :, 1:2]))
        sp2 = self.do(dve, [], lambda e: e.tensor_copy(span[:, :, 5:6], tot[:, :, 2:3]))
        sp3 = self.do(dve, [sp1, sp2], lambda e: e.tensor_tensor(span[:, :, 1:2], span[:, :, 0:1], tot[:, :, 1:2], ALU.add))
        sp4 = self.do(dve, [sp2], lambda e: e.tensor_tensor(span[:, :, 4:5], span[:, :, 2:3], tot[:, :, 2:3], ALU.add))
        sp5 = self.do(dve, [sp3], lambda e: e.tensor_tensor(span[:, :, 3:4], span[:, :, 1:2], tot[:, :, 2:3], ALU.add))
        es = self.do(act, [sp4, sp5], lambda e: e.activation(span[:, :, :], span[:, :, :], ACT.Exp, scale=inv))
        for dt in range(2):
            for hh in range(2):
                rows = slice(hh * HD, (hh + 1) * HD)
                q_ready = self.do(dve, [eb, qk_done, q_zero], lambda e: e.scalar_tensor_tensor(
                    out=g["q_heads"][rows, dt, hh, :], in0=self.bank[0][rows, dt * T:(dt + 1) * T],
                    scalar=GLA_DK ** -0.5, in1=exp_b[rows, dt, :], op0=ALU.mult, op1=ALU.mult))
        k_inv = self.do(dve, [enb], lambda e: e.tensor_tensor(
            g["k_inv"][:, :, :], self.bank[1][:, :].rearrange("p (d t) -> p d t", d=2), tmp[:, :, :], ALU.mult))
        self.bank_free[0] = self.bank_free[1] = k_inv
        kc = g["k_for_chunk"]
        for c in range(NCH):
            cs = slice(c * GLA_CHUNK, (c + 1) * GLA_CHUNK)
            k_ready = self.do(dve, [k_inv, k_zero], lambda e: e.tensor_copy(kc[:, c, :, cs], g["k_inv"][:, :, cs]))
            if c:
                o = (0, 0, 1, 3)[c]
                for dt in range(2):
                    k_ready = self.do(dve, [es], lambda e: e.tensor_tensor(
                        kc[:, c, dt, 0:c * GLA_CHUNK].rearrange("p (c j) -> p c j", j=GLA_CHUNK),
                        g["k_inv"][:, dt, 0:c * GLA_CHUNK].rearrange("p (c j) -> p c j", j=GLA_CHUNK),
                        span[:, dt, o:o + c].unsqueeze(2).to_broadcast([P, c, GLA_CHUNK]), ALU.mult))
        self.small2_free = k_ready
        u_done = self.block_token_major(st, [2, 3], self.x_hi, self.x_lo, self.x_ready)
        for tt in range(TT):
            u_ready = self.do(act, [u_done[tt], free], lambda e: e.activation(g["u"][:, tt, :], self.bank[2 + tt][:, :], ACT.Gelu))
            self.bank_free[2 + tt] = u_ready
        vg_done = self.block_token_major(st, [0, 1], self.x_hi, self.x_lo, self.x_ready)
        for tt in range(TT):
            vg_ready = self.do(act, [vg_done[tt]], lambda e: e.activation(g["vg"][:, tt, :], self.bank[tt][:, :], ACT.Gelu))
            self.bank_free[tt] = vg_ready
        q_heads = g["q_heads"]
        self.after(pe, k_ready, q_ready, [self.bank_free[b] for b in range(4, 8)])
        for jt in range(TT):
            for dt in range(2):
                out = self.bank[4 + 2 * jt + dt][:, :].rearrange("p (h i) -> p h i", h=2)
                for c in range(2 * jt, NCH):
                    i = slice(c * GLA_CHUNK, (c + 1) * GLA_CHUNK)
                    mm = nc.tensor.matmul(out[:, :, i], kc[:, c, dt, jt * P:(jt + 1) * P], q_heads[:, dt, :, i],
                                          start=True, stop=True, skip_group_check=True)
        s_done = self.done(pe, mm)
        sT = g["scoresT"]
        for jt in range(TT):
            for dt in range(2):
                i = slice(jt * P, T)
                src = self.bank[4 + 2 * jt + dt][:, :].rearrange("p (h i) -> p h i", h=2)
                s_copied = self.do(act, [s_done], lambda e: e.activation(sT[:, jt, 2 * dt:2 * dt + 2, i], src[:, :, i], ACT.Copy))
                self.bank_free[4 + 2 * jt + dt] = s_copied
            s_masked = self.do(pool, [s_copied], lambda e: e.affine_select(
                out=sT[:, jt, :, jt * P:(jt + 1) * P], in_=sT[:, jt, :, jt * P:(jt + 1) * P], compare_op=ALU.is_ge,
                fill=0.0, base=0, pattern=[[0, GLA_HEADS], [1, P]], channel_multiplier=-1))
        v_done = self.block_token_major(st, [2, 3], self.x_hi, self.x_lo, self.x_ready)
        for tt in range(TT):
            v_ready = self.do(act, [v_done[tt]], lambda e: e.activation(g["v_gla"][:, tt, :], self.bank[2 + tt][:, :], ACT.Copy))
            self.bank_free[2 + tt] = v_ready
        g_done = self.block_token_major(st, [0, 1], self.x_hi, self.x_lo, self.x_ready)
        for tt in range(TT):
            g_ready = self.do(act, [g_done[tt]], lambda e: e.activation(g["silu_g"][:, tt, :], self.bank[tt][:, :], ACT.Silu))
            self.bank_free[tt] = g_ready
        vst = self.vstats
        for tt in range(TT):
            for h in range(GM_HEADS):
                bst = self.do(dve, [vg_ready, self.vstats_free], lambda e: e.bn_stats(
                    vst[:, tt, h, 0:6], g["vg"][:, tt, h * P:(h + 1) * P]))
        for tt in range(TT):
            for h in range(GM_HEADS):
                agg = self.do(dve, [bst], lambda e: e.bn_aggr(vst[:, tt, h, 6:8], vst[:, tt, h, 0:6]))
        rs = self.small3[:, 0:8].rearrange("p (t h) -> p t h", t=TT)
        add_eps = self.do(dve, [agg], lambda e: e.tensor_scalar(rs, vst[:, :, :, 7], LN_EPS, None, ALU.add))
        r_ready = self.do(pool, [add_eps], lambda e: e.tensor_tensor(
            self.small3[:, 0:8], self.small3[:, 0:8], self.minus_half[:, 0:8], ALU.pow))
        for tt in range(TT):
            for h in range(GM_HEADS):
                cols = slice(h * P, (h + 1) * P)
                vn = self.do(dve, [r_ready], lambda e: e.tensor_scalar(
                    g["vg"][:, tt, cols], g["vg"][:, tt, cols], vst[:, tt, h, 6:7],
                    rs[:, tt, h:h + 1], ALU.subtract, ALU.mult))
        self.vstats_free = vn
        for tt in range(TT):
            vm = self.do(pool, [vn, loaded], lambda e: e.tensor_tensor(g["vg"][:, tt, :], g["vg"][:, tt, :], g["gm_g"][:, :], ALU.mult))
            v_ln = self.do(pool, [vm], lambda e: e.tensor_tensor(g["vg"][:, tt, :], g["vg"][:, tt, :], g["gm_b"][:, :], ALU.add))
        self.after(pe, masked, self.bank_free[4])
        for h in range(GM_HEADS):
            mm = nc.tensor.transpose(self.bank[4][:, h * P:(h + 1) * P], g["ws"][:, h, :], self.const("identity"))
        w_turned = self.done(pe, mm)
        w_ready = self.do(act, [w_turned], lambda e: e.activation(
            g["wsT"][:, :, :], self.bank[4][:, :].rearrange("p (h t) -> p h t", h=GM_HEADS), ACT.Copy))
        self.bank_free[4] = w_ready
        ng_loaded = self.load_small(g["norm_g"][:, :], a["gla_norm_g"][layer].partition_broadcast(P), [w_turned])
        self.after(pe, v_ready, s_masked, self.bank_free[6], self.bank_free[7])
        for tt in range(TT):
            for h in range(GLA_HEADS):
                for jt in range(tt + 1):
                    mm = nc.tensor.matmul(self.bank[6 + tt][:, h * P:(h + 1) * P], sT[:, jt, h, tt * P:(tt + 1) * P],
                                          g["v_gla"][:, jt, h * P:(h + 1) * P], start=(jt == 0), stop=(jt == tt),
                                          skip_group_check=True)
        o_done = self.done(pe, mm)
        self.after(pe, w_ready, v_ln, self.bank_free[4], self.bank_free[5])
        for tt in range(TT):
            for h in range(GM_HEADS):
                mm = nc.tensor.matmul(self.bank[4 + tt][:, h * P:(h + 1) * P], g["wsT"][:, h, :],
                                      g["vg"][:, tt, h * P:(h + 1) * P], start=True, stop=True, skip_group_check=True)
        sg_done = self.done(pe, mm)
        cat = self.xhat
        for tt in range(TT):
            gg = self.do(pool, [g_ready, ng_loaded], lambda e: e.tensor_tensor(
                g["silu_g"][:, tt, :], g["silu_g"][:, tt, :], g["norm_g"][:, :], ALU.mult))
            sq = self.do(act, [o_done, self.xhat_free], lambda e: e.activation(cat[:, tt, 512:1024], self.bank[6 + tt][:, :], ACT.Square))
            ms = self.do(dve, [sq, vn], lambda e: e.tensor_reduce(
                rs[:, tt, :], cat[:, tt, 512:1024].rearrange("p (h e) -> p h e", h=GLA_HEADS), AX.X, ALU.add))
        me = self.do(dve, [ms], lambda e: e.tensor_scalar(rs, rs, 1.0 / GLA_DV, RMS_EPS, ALU.mult, ALU.add))
        rr = self.do(pool, [me], lambda e: e.tensor_tensor(
            self.small3[:, 0:8], self.small3[:, 0:8], self.minus_half[:, 0:8], ALU.pow))
        cat_ready = [None] * TT
        bs_t, bs_c = self.col_of["gm_bs"]
        for tt in range(TT):
            for h in range(GLA_HEADS):
                cols = slice(h * P, (h + 1) * P)
                self.do(dve, [rr, gg], lambda e: e.scalar_tensor_tensor(
                    out=cat[:, tt, 512 + h * P:512 + (h + 1) * P], in0=self.bank[6 + tt][:, cols],
                    scalar=rs[:, tt, h:h + 1], in1=g["silu_g"][:, tt, cols], op0=ALU.mult, op1=ALU.mult))
                c = bs_c + layer * GM_HEADS + h
                cat_ready[tt] = self.do(dve, [sg_done, u_ready], lambda e: e.scalar_tensor_tensor(
                    out=cat[:, tt, cols], in0=self.bank[4 + tt][:, cols], scalar=self.cols[:, bs_t, c:c + 1],
                    in1=g["u"][:, tt, cols], op0=ALU.add, op1=ALU.mult))
            self.bank_free[4 + tt] = self.bank_free[6 + tt] = cat_ready[tt]
        hi, lo = g["cat_hi_gla"], g["cat_lo_gla"]
        ready = [None] * 4
        for tt in range(TT):
            for half in range(2):
                n = 2 * tt + half
                turned = self.transpose_block(cat, tt, half, 4 + n, cat_ready)
                ready[n] = self.split_from_psum(
                    self.bank[4 + n][:, :].rearrange("p (k t) -> p k t", k=4),
                    hi[:, half * 4:half * 4 + 4, tt * P:(tt + 1) * P], lo[:, half * 4:half * 4 + 4, tt * P:(tt + 1) * P],
                    turned)
                self.bank_free[4 + n] = ready[n]
        self.xhat_free = turned
        return hi, lo, ready

    def attention(self, heads, scale, p, pT, cat_hi, cat_lo):
        dve, act, pe, nc = self.dve, self.act, self.pe, self.nc
        n = len(heads)
        st = self.att_stats
        turned_of, ptr, soft = {}, {}, {}
        last_flush = None
        p_free, pT_free = [None, None], [None, None]

        def scores(i):
            hd, b = heads[i], 4 + i % 2
            self.after(pe, self.bank_free[b], hd["ready"])
            for qt in range(TT):
                for j, (q, k) in enumerate(hd["terms"]):
                    mm = nc.tensor.matmul(self.bank[b][:, qt * T:(qt + 1) * T], q[:, qt * P:(qt + 1) * P], k,
                                          start=(j == 0), stop=(j == len(hd["terms"]) - 1), skip_group_check=True)
            s_done = self.done(pe, mm)
            P_ = p[i % 2]
            top = st[:, i, 0, :]
            if hd["bias"] is None:
                src = self.bank[b][:, :].rearrange("p (q k) -> p q k", q=TT)
                m = self.do(dve, [s_done, self.att_free], lambda e: e.tensor_reduce(top, src, AX.X, ALU.max))
                m = self.do(dve, [m], lambda e: e.tensor_scalar(top, top, -scale, None, ALU.mult))
                mult, waits = scale, [p_free[i % 2]]
            else:
                for qt in range(TT):
                    rows = lambda ap: ap.rearrange("p (m w) -> p m w", w=hd["bias"](qt).shape[2])
                    z = self.do(dve, [s_done, p_free[i % 2], hd["bias_ready"]], lambda e: e.scalar_tensor_tensor(
                        out=rows(P_[:, qt, :]), in0=rows(self.bank[b][:, qt * T:(qt + 1) * T]), scalar=scale,
                        in1=hd["bias"](qt), op0=ALU.mult, op1=ALU.add))
                self.bank_free[b] = z
                m = self.do(dve, [z, self.att_free], lambda e: e.tensor_reduce(top, P_[:, :, :], AX.X, ALU.max))
                if hd["sink"] is None:
                    m = self.do(dve, [m], lambda e: e.tensor_scalar(top, top, -1.0, None, ALU.mult))
                else:
                    m = self.do(dve, [m], lambda e: e.tensor_scalar(top, top, hd["sink"], -1.0, ALU.max, ALU.mult))
                mult, waits = 1.0, []
            for qt in range(TT):
                src = self.bank[b][:, qt * T:(qt + 1) * T] if hd["bias"] is None else P_[:, qt, :]
                ex = self.do(act, [m, *waits], lambda e: e.activation(
                    P_[:, qt, :], src, ACT.Exp, bias=st[:, i, 0, qt:qt + 1], scale=mult,
                    accum_out=st[:, i, 1, qt:qt + 1]))
            if hd["bias"] is None:
                self.bank_free[b] = ex
            if hd["sink"] is not None:
                es = self.do(act, [m], lambda e: e.activation(st[:, i, 2, :], top, ACT.Exp, bias=hd["sink"]))
                ex = self.do(dve, [es, ex], lambda e: e.tensor_tensor(st[:, i, 1, :], st[:, i, 1, :], st[:, i, 2, :], ALU.add))
            r = self.do(dve, [ex], lambda e: e.reciprocal(st[:, i, 1, :], st[:, i, 1, :]))
            for qt in range(TT):
                nrm = self.do(dve, [r], lambda e: e.tensor_scalar(
                    P_[:, qt, :], P_[:, qt, :], st[:, i, 1, qt:qt + 1], None, ALU.mult))
            soft[i] = nrm

        def turn(i):
            b = 6 + i % 2
            self.after(pe, self.bank_free[b], soft[i])
            for qt in range(TT):
                for kt in range(TT):
                    mm = nc.tensor.transpose(self.bank[b][:, kt * T + qt * P:kt * T + (qt + 1) * P],
                                             p[i % 2][:, qt, kt * P:(kt + 1) * P], self.const("identity"))
            t = self.done(pe, mm)
            p_free[i % 2] = t
            ptr[i] = self.do(act, [t, pT_free[i % 2]], lambda e: e.activation(
                pT[i % 2][:, :, :], self.bank[b][:, :].rearrange("p (k q) -> p k q", k=TT), ACT.Copy))
            self.bank_free[b] = ptr[i]

        def weigh(i):
            nonlocal last_flush
            hd = heads[i]
            b, rows, parts = hd["out"]
            self.after(pe, self.bank_free[b], ptr[i])
            for j in range(parts):
                for kt in range(TT):
                    mm = nc.tensor.matmul(self.bank[b][rows, j * T:(j + 1) * T], hd["v"](kt, j), pT[i % 2][:, kt, :],
                                          start=(kt == 0), stop=(kt == TT - 1), skip_group_check=True)
            o = self.done(pe, mm)
            pT_free[i % 2] = o
            if hd["flush"]:
                t0, cnt = hd["flush"]
                src = self.bank[b][:, 0:cnt * T].rearrange("p (j t) -> p j t", j=cnt)
                last_flush = self.split_from_psum(src, cat_hi[:, t0:t0 + cnt, :], cat_lo[:, t0:t0 + cnt, :], o)
                self.bank_free[b] = last_flush

        for i in range(n + 2):
            if i < n:
                scores(i)
            if 1 <= i <= n:
                turn(i - 1)
            if i >= 2:
                weigh(i - 2)
        self.att_free = last_flush
        return [last_flush] * 4

    def ab_stream(self):
        w, wo = self.a["ab_w_in_2"][0], self.a["ab_w_out_2"][0]
        return self.square_stream([(w, c) for c in (0, 512, 1024)] + [(wo, 0), (wo, 512)])

    def mixer_ab(self, st, free):
        g, nc = self.ab, self.nc
        dve, act, pool, pe = self.dve, self.act, self.pool, self.pe
        proj = g["proj"]
        for b in range(3):
            banks = [(0, 1), (2, 3)][b % 2]
            d = self.block_token_major(st, banks, self.x_hi, self.x_lo, self.x_ready)
            for tt in range(TT):
                pr = self.do(act, [d[tt], free], lambda e: e.activation(
                    proj[:, tt, b * 512:(b + 1) * 512], self.bank[banks[tt]][:, :], ACT.Copy))
                self.bank_free[banks[tt]] = pr
            if b == 1:
                first_two = pr
        NH = 10
        tmp = self.xhat
        turned = None
        bank = 0
        tiles_ready = None
        for kind in range(2):
            src = proj[:, :, kind * 768:kind * 768 + NH * HD]
            heads = src.rearrange("p t (h d) -> p t h d", h=NH)
            ready = [first_two, pr][kind]
            if kind == 0:
                rs = self.small3[:, 0:TT * NH]
                for tt in range(TT):
                    sq = self.do(act, [ready, self.xhat_free], lambda e: e.activation(tmp[:, tt, 0:NH * HD], src[:, tt, :], ACT.Square))
                    ms = self.do(dve, [sq], lambda e: e.tensor_reduce(
                        rs[:, tt * NH:(tt + 1) * NH], tmp[:, tt, 0:NH * HD].rearrange("p (h d) -> p h d", h=NH), AX.X, ALU.add))
                me = self.do(dve, [ms], lambda e: e.tensor_scalar(rs, rs, 1.0 / HD, RMS_EPS, ALU.mult, ALU.add))
                rr = self.do(pool, [me], lambda e: e.tensor_tensor(rs, rs, self.minus_half[:, 0:TT * NH], ALU.pow))
                for tt in range(TT):
                    sc = self.do(dve, [rr], lambda e: e.tensor_tensor(
                        heads[:, tt, :, :], heads[:, tt, :, :],
                        rs[:, tt * NH:(tt + 1) * NH].unsqueeze(2).to_broadcast([P, NH, HD]), ALU.mult))
                    for part, (h0, h1) in enumerate(((0, 8), (8, 10))):
                        ready = self.do(dve, [sc, self.small_loaded], lambda e: e.tensor_tensor(
                            heads[:, tt, h0:h1, :], heads[:, tt, h0:h1, :],
                            self.gains[:, part, :].unsqueeze(1).to_broadcast([P, h1 - h0, HD]), ALU.mult))
            name = "2d" if kind == 0 else "1d"
            H2 = HD // 2
            rot = g["rot"]
            rot_done = None
            for tt in range(TT):
                cos = self.const(f"cos_{name}")[:, tt * H2:(tt + 1) * H2].unsqueeze(1).to_broadcast([P, NH, H2])
                sin = self.const(f"sin_{name}")[:, tt * H2:(tt + 1) * H2].unsqueeze(1).to_broadcast([P, NH, H2])
                x1, x2 = heads[:, tt, :, 0:H2], heads[:, tt, :, H2:HD]
                t = [tmp[:, tt, i * 320:(i + 1) * 320].rearrange("p (h d) -> p h d", h=NH) for i in range(3)]
                waits = [ready, self.xhat_free, turned]
                a1 = self.do(dve, waits, lambda e: e.tensor_tensor(t[0], x1, cos, ALU.mult))
                a2 = self.do(dve, waits, lambda e: e.tensor_tensor(t[1], x2, sin, ALU.mult))
                a3 = self.do(pool, waits, lambda e: e.tensor_tensor(t[2], x2, cos, ALU.mult))
                a4 = self.do(pool, [a1, a3], lambda e: e.tensor_tensor(x1, x1, sin, ALU.mult))
                for o0, o1, h0, h1 in ((0, 8, 0, 8), (8, 10, 8, 9), (10, 12, 9, 10)):
                    dup = o1 - o0 != h1 - h0
                    bc = (lambda ap: ap.to_broadcast([P, 2, H2])) if dup else (lambda ap: ap)
                    r1 = self.do(dve, [a1, a2], lambda e: e.tensor_tensor(
                        rot[:, tt, o0:o1, 0:H2], bc(t[0][:, h0:h1, :]), bc(t[1][:, h0:h1, :]), ALU.subtract))
                    r2 = self.do(dve, [a3, a4], lambda e: e.tensor_tensor(
                        rot[:, tt, o0:o1, H2:HD], bc(t[2][:, h0:h1, :]), bc(x1[:, h0:h1, :]), ALU.add))
                rot_done = r2
            for tile in range(6):
                b = 4 + tile % 4
                self.after(pe, self.bank_free[b], rot_done)
                for tt in range(TT):
                    mm = nc.tensor.transpose(self.bank[b][:, tt * P:(tt + 1) * P],
                                             rot[:, tt, 2 * tile:2 * tile + 2, :].rearrange("p h d -> p (h d)"),
                                             self.const("identity"))
                turned = self.done(pe, mm)
                dst = g["qT_ab"][:, kind * 4 + tile, :] if tile < 4 else g["kT_ab"][:, kind * 2 + tile - 4, :]
                tiles_ready = self.do(act, [turned], lambda e: e.activation(dst, self.bank[b][:, 0:T], ACT.Copy))
                self.bank_free[b] = tiles_ready
        self.xhat_free = [a4, r2]
        heads = []
        window = self.const("window").rearrange("p (q k) -> p q k", q=TT)
        for kind in range(2):
            for h in range(8):
                rows = slice((h % 2) * HD, (h % 2 + 1) * HD)
                kv = h // 4
                voff = kind * 768 + 640 + kv * HD
                tile = kind * 4 + h // 2
                heads.append(dict(
                    terms=[(g["qT_ab"][rows, tile, :], g["kT_ab"][rows, kind * 2 + kv, :])],
                    v=lambda kt, j, voff=voff: proj[:, kt, voff:voff + HD],
                    bias=(lambda qt: window[:, qt, :].unsqueeze(1)) if kind else None, bias_ready=None,
                    sink=self.sink[:, h:h + 1] if kind else None,
                    out=(tile % 2, rows, 1), flush=(tile, 1) if h % 2 else None, ready=[tiles_ready, rot_done, r2]))
        ready = self.attention(heads, HD ** -0.5, [g["p0_ab"], g["p1_ab"]], [g["pT0_ab"], g["pT1_ab"]],
                               g["cat_hi_ab"], g["cat_lo_ab"])
        return g["cat_hi_ab"], g["cat_lo_ab"], ready

    def c_stream(self):
        w, wo = self.a["c_w_in_2"][0], self.a["c_w_out_2"][0]
        return self.square_stream([(w, c) for c in range(0, 3 * D, 512)] + [(wo, 0), (wo, 512)])

    def qkv_blocks(self, st, which, hi, lo, ready, free, base):
        g = self.qkv
        for half in range(2):
            banks = [(0, 1), (2, 3)][(base + half) % 2]
            if which == "v_att":
                d = self.block_token_major(st, banks, hi, lo, ready)
            else:
                d = [self.block_transposed(st, banks, hi, lo, ready)] * 2
            for b in range(2):
                if which == "v_att":
                    dst, src = g[which][:, b, half * 512:(half + 1) * 512], self.bank[banks[b]][:, :]
                else:
                    dst = g[which][:, half * 4 + 2 * b:half * 4 + 2 * b + 2, :]
                    src = self.bank[banks[b]][:, :].rearrange("p (m t) -> p m t", m=2)
                r = self.do(self.act, [d[b], free], lambda e: e.activation(dst, src, ACT.Copy))
                self.bank_free[banks[b]] = r
        return r

    def mixer_c(self, st, free):
        g = self.qkv
        bias = g["bias"]
        rpb = self.a["c_rpb_2"]
        n_dr, n_dc = 2 * NA_KH - 1, 2 * NA_KW - 1
        for ro in range(2):
            for h in range(C_HEADS):
                off = h * n_dr * n_dc + (NA_KH - 1 - 2 - ro) * n_dc + NA_KW - GRID_W
                src = bass.AP(rpb.tensor, off, [[1, GRID_W], [n_dc, BIAS_ROWS], [1, GRID_W]])
                bias_landed = self.load_small(bias[ro * GRID_W:(ro + 1) * GRID_W, h, :, :], src, [free])
        masked = []
        for h in range(C_HEADS):
            masked.append(self.do(self.pool, [bias_landed], lambda e: e.tensor_tensor(
                bias[:, h, :, :], bias[:, h, :, :],
                self.const("neighbours").unsqueeze(1).to_broadcast([P, BIAS_ROWS, GRID_W]), ALU.add)))
        self.qkv_blocks(st, "qT", self.x_hi, self.x_lo, self.x_ready, free, 0)
        self.qkv_blocks(st, "kT", self.x_hi, self.x_lo, self.x_ready, free, 0)
        ready = self.qkv_blocks(st, "v_att", self.x_hi, self.x_lo, self.x_ready, free, 0)
        heads = []
        for h in range(C_HEADS):
            rows = slice((h % 2) * HD, (h % 2 + 1) * HD)
            heads.append(dict(
                terms=[(g["qT"][rows, h // 2, :], g["kT"][rows, h // 2, :])],
                v=lambda kt, j, h=h: g["v_att"][:, kt, h * HD:(h + 1) * HD],
                bias=lambda qt, h=h: bias[:, h, 2 - 2 * qt:2 - 2 * qt + ROWS, ::-1],
                bias_ready=masked[h], sink=None, out=((h // 2) % 2, rows, 1),
                flush=(h // 2, 1) if h % 2 else None, ready=ready))
        r = self.attention(heads, HD ** -0.5, [g["p0"], g["p1"]], [g["pT0"], g["pT1"]], g["cat_hi_qkv"], g["cat_lo_qkv"])
        return g["cat_hi_qkv"], g["cat_lo_qkv"], r

    def mem_stream(self, layer):
        wq, wkv, wo = self.a["mem_w_q_2"][layer], self.a["mem_w_kv_2"][layer], self.a["mem_w_o_2"][layer]
        return self.square_stream([(wkv, c) for c in range(0, 2 * D, 512)] + [(wq, 0), (wq, 512), (wo, 0), (wo, 512)])

    def memory_parts(self, free):
        m = self.mem_row
        landed = self.load_small(m[:, :, :], self.a["mem_2"][0].rearrange("(t p) d -> p t d", p=P), [free])
        ready = [None] * 4
        for tt in range(TT):
            for half in range(2):
                n = 2 * tt + half
                turned = self.transpose_block(m, tt, half, 4 + n, landed)
                ready[n] = self.split_from_psum(
                    self.bank[4 + n][:, :].rearrange("p (k t) -> p k t", k=4),
                    self.mem_hi[:, half * 4:half * 4 + 4, tt * P:(tt + 1) * P],
                    self.mem_lo[:, half * 4:half * 4 + 4, tt * P:(tt + 1) * P], turned, [free])
                self.bank_free[4 + n] = ready[n]
        return ready

    def memory_attn(self, layer, st, free, mem_ready):
        g = self.qkv
        self.qkv_blocks(st, "kT", self.mem_hi, self.mem_lo, mem_ready, free, 0)
        self.qkv_blocks(st, "v_att", self.mem_hi, self.mem_lo, mem_ready, free, 0)
        ready = self.qkv_blocks(st, "qT", self.x_hi, self.x_lo, self.x_ready, free, 0)
        dm = D // MEM_HEADS
        heads = []
        for h in range(MEM_HEADS):
            heads.append(dict(
                terms=[(g["qT"][:, 2 * h + j, :], g["kT"][:, 2 * h + j, :]) for j in range(2)],
                v=lambda kt, j, h=h: g["v_att"][:, kt, h * dm + j * P:h * dm + (j + 1) * P],
                bias=None, bias_ready=None, sink=None, out=(h % 2, slice(0, P), 2), flush=(2 * h, 2), ready=ready))
        r = self.attention(heads, dm ** -0.5, [g["p0"], g["p1"]], [g["pT0"], g["pT1"]], g["cat_hi_qkv"], g["cat_lo_qkv"])
        return g["cat_hi_qkv"], g["cat_lo_qkv"], r

    def router(self, acc_free):
        a, nc, dve, act, pe = self.a, self.nc, self.dve, self.act, self.pe
        E = N_EXP
        r_raw, r_hi, r_lo = self.router_raw, self.router_hi, self.router_lo
        landed = self.load_small(r_raw[:, :, :], a["router_w"][0].rearrange("(k p) e -> p k e", p=P), [self.small_free])
        h = self.do(act, [landed], lambda e: e.activation(r_hi[:, :, :], r_raw[:, :, :], ACT.Copy))
        lo = self.do(dve, [h], lambda e: e.tensor_tensor(r_lo[:, :, :], r_raw[:, :, :], r_hi[:, :, :].bitcast(F32), ALU.subtract))
        self.after(pe, lo, self.x_ready, self.bank_free[4])
        for tt in range(TT):
            for k in range(KT):
                mm = self.product(self.bank[4][:, tt * E:(tt + 1) * E], self.x_hi[:, k, tt * P:(tt + 1) * P],
                                  self.x_lo[:, k, tt * P:(tt + 1) * P], r_hi[:, k, :], r_lo[:, k, :],
                                  start=(k == 0 and tt == 0), stop=(k == KT - 1))
        l_done = self.done(pe, mm)
        sm = self.small
        logit = sm[:, 128:128 + TT * E].rearrange("p (t e) -> p t e", t=TT)
        rank = sm[:, 144:144 + TT * E].rearrange("p (t e) -> p t e", t=TT)
        first = sm[:, 160:160 + TT * E].rearrange("p (t e) -> p t e", t=TT)
        top = sm[:, 176:180]
        w2 = sm[:, 180:182]
        cmp_ = sm[:, 192:256].rearrange("p (e j) -> p e j", j=E)
        eq = sm[:, 256:320].rearrange("p (e j) -> p e j", j=E)
        prod = sm[:, 320:320 + TT * E].rearrange("p (t e) -> p t e", t=TT)
        t = self.do(dve, [l_done], lambda e: e.tensor_copy(logit, self.bank[4][:, 0:TT * E].rearrange("p (t e) -> p t e", t=TT)))
        self.bank_free[4] = t
        earlier = self.const("earlier_expert").rearrange("p (e j) -> p e j", j=E)
        for tt in range(TT):
            own = logit[:, tt, :].unsqueeze(2).to_broadcast([P, E, E])
            other = logit[:, tt, :].unsqueeze(1).to_broadcast([P, E, E])
            a1 = self.do(dve, [t], lambda e: e.tensor_tensor(cmp_, other, own, ALU.is_gt))
            a2 = self.do(dve, [t], lambda e: e.tensor_tensor(eq, other, own, ALU.is_equal))
            a3 = self.do(dve, [a2], lambda e: e.tensor_tensor(eq, eq, earlier, ALU.mult))
            a4 = self.do(dve, [a1, a3], lambda e: e.tensor_tensor(cmp_, cmp_, eq, ALU.add))
            t = self.do(dve, [a4], lambda e: e.tensor_reduce(rank[:, tt, :], cmp_, AX.X, ALU.add))
        for i in range(2):
            s = self.do(dve, [t], lambda e: e.tensor_scalar(first, rank, float(i), None, ALU.is_equal))
            s = self.do(dve, [s], lambda e: e.tensor_tensor(prod, first, logit, ALU.mult))
            t = self.do(dve, [s], lambda e: e.tensor_reduce(top[:, 2 * i:2 * i + 2], prod, AX.X, ALU.add))
        d = self.do(dve, [t], lambda e: e.tensor_tensor(top[:, 2:4], top[:, 2:4], top[:, 0:2], ALU.subtract))
        ex = self.do(act, [d], lambda e: e.activation(w2, top[:, 2:4], ACT.Exp))
        d = self.do(dve, [ex], lambda e: e.tensor_scalar(top[:, 0:2], w2, 1.0, None, ALU.add))
        d = self.do(dve, [d], lambda e: e.reciprocal(top[:, 0:2], top[:, 0:2]))
        d = self.do(dve, [d], lambda e: e.tensor_tensor(top[:, 2:4], w2, top[:, 0:2], ALU.mult))
        s1 = self.do(dve, [d], lambda e: e.tensor_scalar(first, rank, 0.0, None, ALU.is_equal))
        s2 = self.do(dve, [d], lambda e: e.tensor_scalar(prod, rank, 1.0, None, ALU.is_equal))
        for tt in range(TT):
            m = self.do(dve, [s1], lambda e: e.tensor_scalar(first[:, tt, :], first[:, tt, :], top[:, tt:tt + 1], None, ALU.mult))
            g = self.do(dve, [m, s2], lambda e: e.scalar_tensor_tensor(
                out=self.gates[:, tt, :], in0=prod[:, tt, :], scalar=top[:, 2 + tt:3 + tt], in1=first[:, tt, :],
                op0=ALU.mult, op1=ALU.add))
        self.small_free = g
        return g

    def expert_weights(self, e):
        one = lambda w: (lambda r, c: w[bass.ds(e, 1), r, c].rearrange("o k n -> (o k) n"))
        return tuple(one(self.a[n][0]) for n in ("exp_w_gate", "exp_w_up", "exp_w_down"))

    def moe(self, up_slots, n_chunks):
        gates_ready = self.router(None)
        self.after(self.dve, gates_ready)
        w0 = self.expert_weights(0)
        done, up = None, up_slots
        e_state = {"up": up}

        def expert(e, last=False):
            w = self.expert_weights(e)
            nxt = None
            if not last:
                wn = self.expert_weights(e + 1)
                nxt = self.ffn_loads_up(wn[0], wn[1], 0)
            gate = lambda tt: self.gates[:, tt, bass.ds(e, 1)]
            done, e_state["up"] = self.ffn(w, n_chunks, e_state["up"], gate=gate, following=nxt)
            return done

        before = dict(self.c.count)
        expert(0)
        with self.c.repeat(before, N_EXP - 1) as e:
            expert(e)
        return expert(N_EXP - 1, last=True)

    def build(self):
        a = self.a
        self.small_free = self.small2_free = self.vstats_free = self.att_free = None
        self.start()
        dense = lambda w: (lambda r, c: w[r, c])
        stages = []
        for layer in range(DEPTH):
            mix_ln = [(t, c + layer * KT) for t, c in (self.col_of["ln_mix_g"], self.col_of["ln_mix_b"])]
            ffn_ln = [(t, c + layer * KT) for t, c in (self.col_of["ln_ffn_g"], self.col_of["ln_ffn_b"])]
            stages.append(("gla", layer, mix_ln))
            stages.append(("ffn" if layer % 2 == 0 else "moe", layer // 2, ffn_ln))
        for layer in range(DEPTH):
            ln = lambda s: [(t, c + (layer * 4 + s) * KT) for t, c in (self.col_of["ln_g_2"], self.col_of["ln_b_2"])]
            stages.append(("ffn2", (layer, 0), ln(0)))
            stages.append(("ab" if layer % 2 == 0 else "c", layer, ln(1)))
            stages.append(("mem", layer, ln(2)))
            stages.append(("ffn2", (layer, 1), ln(3)))
        if self.stop is not None:
            stages = stages[self.stop[0]:self.stop[1]]

        def weights(kind, which):
            if kind == "ffn":
                return tuple(dense(a[n][which]) for n in ("ffn_w_gate", "ffn_w_up", "ffn_w_down"))
            if kind == "ffn2":
                return tuple(dense(a[n][which[0], which[1]]) for n in ("ffn_w_gate_2", "ffn_w_up_2", "ffn_w_down_2"))
            return self.expert_weights(0)

        def prefetch(kind, which):
            if kind in ("ffn", "ffn2", "moe"):
                return self.ffn_prefetch(weights(kind, which))
            st = {"gla": lambda: self.gla_stream(which), "ab": self.ab_stream, "c": self.c_stream,
                  "mem": lambda: self.mem_stream(which)}[kind]()
            self.stream_step(st)
            self.stream_step(st)
            return st

        ahead = prefetch(*stages[0][:2])
        free = None
        for n, (kind, which, (g, b)) in enumerate(stages):
            eps = LN_EPS
            if kind in ("ffn", "moe", "ffn2"):
                scale = 1 if kind == "ffn2" else 0
                if kind == "ffn2":
                    eps = 4 * LN_EPS
                self.residual(scale)
                if kind == "moe":
                    done = self.moe(ahead, D_FFE // FC)
                else:
                    done, _ = self.ffn(weights(kind, which), D_FF // FC, ahead)
            else:
                if kind == "gla":
                    cat = self.hybrid_mixer(which, ahead, free)
                elif kind == "ab":
                    cat = self.mixer_ab(ahead, free)
                elif kind == "c":
                    cat = self.mixer_c(ahead, free)
                else:
                    cat = self.memory_attn(which, ahead, free, self.memory_parts(free))
                done = self.out_projection(ahead, *cat)
            free = done[1]
            last = n == len(stages) - 1
            if not last:
                ahead = prefetch(*stages[n + 1][:2])
            normed = self.layer_norm(done, g, b, eps, final=last)
        layer, s = (DEPTH - 1, 3)
        gd, bd = self.final_gb
        self.store_final(normed, gd, bd)


def build_program(nc, args, out, stop=None, final=None):
    p = Program(nc, args, out, stop)
    p.final_gb = final(args) if final else (args["ln_g_2"][DEPTH - 1, 3], args["ln_b_2"][DEPTH - 1, 3])
    p.build()


_INS = ["x", "w_in", "gm_ws", "gm_bs", "gm_ln_g", "gm_ln_b", "gla_wa2", "gla_ba", "gla_norm_g", "w_out", "ln_mix_g",
        "ln_mix_b", "ffn_w_gate", "ffn_w_up", "ffn_w_down", "router_w", "exp_w_gate", "exp_w_up", "exp_w_down",
        "ln_ffn_g", "ln_ffn_b", "mem_2", "ln_g_2", "ln_b_2", "ffn_w_gate_2", "ffn_w_up_2", "ffn_w_down_2",
        "ab_w_in_2", "ab_w_out_2", "ab_q_gain_2", "ab_k_gain_2", "ab_sink_2", "c_w_in_2", "c_w_out_2", "c_rpb_2",
        "mem_w_q_2", "mem_w_kv_2", "mem_w_o_2"]


def kernel(**inputs):
    import concourse.bacc as _bacc
    from concourse.bass_utils import run_bass_kernel_spmd as _run

    nc = _bacc.Bacc("TRN2", target_bir_lowering=False, num_devices=1)
    arrays, args = {}, {}
    for name in _INS + ["consts"]:
        if name == "consts":
            a = CONST_ARRAY
        elif name == "c_rpb_2":
            a = np.ascontiguousarray(np.asarray(inputs[name])[..., ::-1])
        else:
            a = np.ascontiguousarray(inputs[name])
        arrays[f"in_{name}_dram"] = a
        args[name] = nc.dram_tensor(f"in_{name}_dram", a.shape, mybir.dt.from_np(a.dtype), kind="ExternalInput").ap()
    out = nc.dram_tensor("out_dram", (1, T, D), F32, kind="ExternalOutput").ap()
    build_program(nc, args, out)
    r = _run(nc, [arrays], core_ids=[0])
    return r.results[0]["out_dram"]
```

```python
from contextlib import contextmanager

import numpy as np

import concourse.bass as bass
from concourse import mybir

P = 128
F32 = mybir.dt.float32
F32R = mybir.dt.float32r
ALU = mybir.AluOpType
ACT = mybir.ActivationFunctionType
AX = mybir.AxisListType

T = 256
TT = T // P
D = 1024
KT = D // P
DEPTH = 2
LN_EPS, RMS_EPS = 1e-5, 1e-6
ALPHA = (2.0 * DEPTH) ** 0.25

GM_HEADS, GM_DIM = 4, 128
GM_W = GM_HEADS * GM_DIM
GLA_HEADS, GLA_DV, GLA_DK, GLA_RANK, GLA_CHUNK = 4, 128, 64, 16, 64
GLA_W, GLA_KW = GLA_HEADS * GLA_DV, GLA_HEADS * GLA_DK
GLA_TAU = 16.0
NCH = T // GLA_CHUNK
D_FF, D_FFE, N_EXP = 2816, 3584, 8
FC = 256

HD = 64
GRID_W, NA_KH, NA_KW = 64, 8, 16
ROWS = T // GRID_W
C_HEADS = D // HD
MEM_HEADS = 4
BIAS_ROWS = ROWS + 2
NEG = -1e30
WINDOW = 128

RING = 6
MIX_PARTS = 3
SLOT = 2048

CONST = {}


def build_constants():
    cols = []

    def add(name, a):
        a = np.asarray(a, np.float32).reshape(P, -1)
        start = sum(c.shape[1] for c in cols)
        CONST[name] = (start, a.shape[1])
        cols.append(a)

    eye = np.eye(P, dtype=np.float32)
    add("identity", eye)
    add("alpha_identity", eye * np.float32(ALPHA))
    add("alpha2_identity", eye * np.float32(2 * np.float32(ALPHA)))
    q = np.arange(T).reshape(TT, P).T[:, :, None]
    add("window", np.where(np.abs(q - np.arange(T)) <= WINDOW, 0.0, NEG))
    w = np.arange(P)[:, None] % GRID_W
    first = np.clip(w - NA_KW // 2, 0, GRID_W - NA_KW)
    k = np.arange(GRID_W)[None]
    add("neighbours", np.where((k >= first) & (k < first + NA_KW), 0.0, NEG)[:, ::-1])
    t = np.arange(T)

    def angles(pos, dim):
        inv = np.float32(10000.0) ** (-np.arange(0, dim, 2, dtype=np.float32) / np.float32(dim))
        return pos.astype(np.float32)[:, None] * inv[None].astype(np.float32)

    ang_2d = np.concatenate([angles(t // GRID_W, HD // 2), angles(t % GRID_W, HD // 2)], axis=-1)
    for name, ang in (("2d", ang_2d), ("1d", angles(t, HD))):
        for f, fn in (("cos", np.cos), ("sin", np.sin)):
            add(f"{f}_{name}", fn(ang).reshape(TT, P, HD // 2).transpose(1, 0, 2))
    add("scan_keep", np.tile((np.arange(2 * T) % GLA_CHUNK != 0).astype(np.float32), (P, 1)))
    add("slot_number", np.tile(np.arange(P), (P, 1)))
    e = np.arange(N_EXP)
    add("earlier_expert", np.tile((e[None, :] < e[:, None]).astype(np.float32).reshape(1, -1), (P, 1)))
    return np.concatenate(cols, axis=1)


CONST_ARRAY = build_constants()


class Token:
    def __init__(self, sem, value, loops):
        self.sem, self.value, self.loops = sem, value, loops


class Loop:
    def __init__(self, per, var):
        self.per, self.var = per, var


class Counter:
    def __init__(self, nc):
        self.nc = nc
        self.count = {}
        self.tokens = []
        self.active = ()
        self.waited = {}

    def mark(self, ins, sem, amount=1):
        ins.then_inc(sem, amount)
        self.count[sem] = self.count.get(sem, 0) + amount
        token = Token(sem, self.count[sem], self.active)
        self.tokens.append(token)
        return token

    def after(self, eng, *tokens):
        for t in tokens:
            if t is None:
                continue
            if isinstance(t, (list, tuple)):
                self.after(eng, *t)
                continue
            key = (eng.name, t.sem, t.loops)
            if self.waited.get(key, 0) >= t.value:
                continue
            self.waited[key] = t.value
            value = t.value
            for loop in t.loops:
                assert loop in self.active
                if loop.per.get(t.sem, 0):
                    value = (loop.var - 1) * loop.per[t.sem] + value
            eng.eng.wait_ge(t.sem, value)

    @contextmanager
    def repeat(self, before, times):
        per = {s: n - before.get(s, 0) for s, n in self.count.items() if n != before.get(s, 0)}
        entry = dict(self.count)
        loop = Loop(per, None)
        for t in self.tokens:
            if t.value > before.get(t.sem, 0):
                t.loops = t.loops + (loop,)
        self.waited = {}
        with self.nc.Fori(1, times) as var:
            loop.var = var
            self.active = self.active + (loop,)
            yield var
            self.active = self.active[:-1]
        for s, n in self.count.items():
            assert n - entry.get(s, 0) == per.get(s, 0), "the body must repeat the hand-run one"
            self.count[s] = n + (times - 2) * per.get(s, 0)
        for t in self.tokens:
            if loop in t.loops:
                t.loops = tuple(x for x in t.loops if x is not loop)
                t.value += (times - 2) * per.get(t.sem, 0)
        self.waited = {}


class Engine:
    def __init__(self, name, eng, sem):
        self.name, self.eng, self.sem = name, eng, sem


class Stream:
    def __init__(self, loads, parts):
        self.loads, self.parts, self.ready, self.sent = loads, parts, [], 0


class Program:
    def __init__(self, nc, a, out, stop=None):
        self.nc, self.a, self.out, self.stop = nc, a, out, stop
        self.c = Counter(nc)
        self.pe = Engine("pe", nc.tensor, nc.alloc_semaphore("tensor_steps"))
        self.act = Engine("act", nc.scalar, nc.alloc_semaphore("scalar_steps"))
        self.dve = Engine("dve", nc.vector, nc.alloc_semaphore("vector_steps"))
        self.pool = Engine("pool", nc.gpsimd, nc.alloc_semaphore("gpsimd_steps"))
        self.sp = Engine("sp", nc.sync, None)
        self.landed_sem = [nc.alloc_semaphore(f"slot{i}_landed") for i in range(RING)]
        self.small_sem = nc.alloc_semaphore("small_loads")
        self.second_sems = [nc.alloc_semaphore(f"{n}_steps_second_pass") for n in ("tensor", "scalar", "vector", "gpsimd")]
        self.second_landed = [nc.alloc_semaphore(f"slot{i}_landed_second_pass") for i in range(RING)]
        self.x_sem = nc.alloc_semaphore("x_landed")
        self.const_sem = nc.alloc_semaphore("consts_landed")
        self.last_gb_sem = nc.alloc_semaphore("last_gain_landed")
        self.loads_sem = nc.alloc_semaphore("slots_requested")
        self.out_sem = nc.alloc_semaphore("stores")
        self.place_memory()

    def place_memory(self):
        nc = self.nc
        base = (nc.sbuf_base + 31) // 32 * 32
        at = [base]

        def put(name, shape, dt=F32, offset=None):
            words = int(np.prod(shape[1:]))
            if offset is None:
                offset = at[0]
                at[0] += (words * 4 + 31) // 32 * 32
            return nc.alloc_sbuf_tensor_at(name, shape, dt, offset=offset)

        self.raw = [put(f"raw{i}", [P, SLOT]) for i in range(RING)]
        x_at = at[0]
        self.x_hi = put("x_hi", [P, KT, T], F32R)
        self.x_lo = put("x_lo", [P, KT, T], F32R)
        xf_at = at[0]
        self.xf = [put(f"x_affine{i}", [P, 4, P]) for i in range(2)]
        xhat_at = at[0]
        self.xhat = put("xhat", [P, TT, D])
        self.consts = put("consts", [P, CONST_ARRAY.shape[1]])
        self.resid_hi = put("resid_hi", [P, 2, P], F32R)
        self.resid_lo = put("resid_lo", [P, 2, P], F32R)
        self.rows = put("param_rows", [P, 2, P])
        self.cols = put("param_cols", [P, 2, P])
        self.stats = put("stats", [P, TT, 2, 6])
        self.mv = put("mean_var", [P, TT, 2])
        self.rstd = put("rstd", [P, TT])
        self.minus_half = put("minus_half", [P, 32])
        small_at = at[0]
        self.small = put("small", [P, 512])
        xe_at = at[0]
        self.xe_hi = put("expert_in_hi", [P, KT, P], F32R)
        self.xe_lo = put("expert_in_lo", [P, KT, P], F32R)
        self.place = put("slot_of_token", [P, TT, N_EXP])
        self.chosen = put("chosen", [P, TT, N_EXP])
        self.slot_gate = put("slot_gate", [P, 1])
        self.overflow = put("overflow", [P, 1], mybir.dt.int32)
        self.biggest = put("largest_count", [P, 1])
        self.sink = put("sink", [P, 8])
        self.gains = put("gains", [P, 2, HD])
        self.gates = put("gates", [P, TT, N_EXP])
        self.small2 = put("chunk_spans", [P, 2, 6])
        self.small3 = put("inverse_norms", [P, 32])
        self.vstats = put("gating_stats", [P, TT, GM_HEADS, 8])
        self.att_stats = put("softmax_stats", [P, 16, 3, TT])
        self.part_hi = [None] * RING
        self.part_lo = [None] * RING
        for i in range(RING):
            if i == MIX_PARTS:
                arena = at[0]
            self.part_hi[i] = put(f"part_hi{i}", [P, SLOT], F32R)
            self.part_lo[i] = put(f"part_lo{i}", [P, SLOT], F32R)
        self.silu_at = at[0]
        self.silu = [put(f"silu{i}", [P, FC]) for i in range(2)]
        self.h = [put(f"h{i}", [P, FC]) for i in range(2)]
        self.hT_hi = [[None] * TT for _ in range(2)]
        self.hT_lo = [[None] * TT for _ in range(2)]
        for t in range(TT):
            if t == 1:
                y_at = at[0]
            for i in range(2):
                self.hT_hi[i][t] = put(f"hT_hi{i}{t}", [P, 2, P], F32R)
                self.hT_lo[i][t] = put(f"hT_lo{i}{t}", [P, 2, P], F32R)
        end = at[0]
        assert end <= nc.sbuf_usable_end, (end, nc.sbuf_usable_end)

        over = lambda name, shape, dt, offset: nc.alloc_sbuf_tensor_at(name, shape, dt, offset=offset)
        self.xe_all = over("expert_affine", [P, KT, P], F32, xf_at)
        self.y_hi = [over(f"y_hi{i}", [P, 512], F32R, o) for i, o in enumerate((y_at, xf_at))]
        self.y_lo = [over(f"y_lo{i}", [P, 512], F32R, o + 2048) for i, o in enumerate((y_at, xf_at))]
        self.n_hi = over("normed_hi", [P, TT, D], F32R, x_at)
        self.n_lo = over("normed_lo", [P, TT, D], F32R, x_at + 4 * TT * D)
        self.total = over("expert_sum", [P, TT, D], F32, xhat_at)
        self.pick = over("pick", [P, TT, P], F32R, small_at)
        self.pickT = over("pickT", [P, TT, P], F32R, small_at + 4 * TT * P)
        self.router_raw, self.router_hi, self.router_lo = (
            over(f"router_{n}", [P, KT, N_EXP], dt, xe_at + i * 4 * KT * N_EXP)
            for i, (n, dt) in enumerate((("raw", F32), ("hi", F32R), ("lo", F32R))))
        self.before_me = over("tokens_before", [P, 2, P], F32, self.silu_at)
        self.overlay_at = {}

        def overlay(items):
            o = arena
            made = {}
            for name, shape, dt, over in items:
                words = int(np.prod(shape[1:]))
                if over is None:
                    made[name] = (nc.alloc_sbuf_tensor_at(name, shape, dt, offset=o), o)
                    o += (words * 4 + 31) // 32 * 32
                else:
                    made[name] = (nc.alloc_sbuf_tensor_at(name, shape, dt, offset=made[over][1]), made[over][1])
            assert o <= end, (o - arena, end - arena)
            self.overlay_at.update({k: v[1] for k, v in made.items()})
            return {k: v[0] for k, v in made.items()}

        self.gla = overlay([
            ("u", [P, TT, GM_W], F32, None), ("vg", [P, TT, GM_W], F32, None),
            ("v_gla", [P, TT, GLA_W], F32, None), ("silu_g", [P, TT, GLA_W], F32, None),
            ("q_heads", [P, 2, 2, T], F32, None), ("k_inv", [P, 2, T], F32, None),
            ("k_for_chunk", [P, NCH, 2, T], F32, None), ("scoresT", [P, TT, GLA_HEADS, T], F32, None),
            ("log_a", [P, 2, T], F32, None), ("tmp_a", [P, 2, T], F32, None),
            ("b_cum", [P, 2, T], F32, None), ("exp_b", [P, 2, T], F32, None),
            ("ws", [P, GM_HEADS, P], F32, None), ("wsT", [P, GM_HEADS, P], F32, None),
            ("gm_g", [P, GM_W], F32, None), ("gm_b", [P, GM_W], F32, None),
            ("a_raw", [P, KT, GLA_RANK], F32, None),
            ("a_hi", [P, KT, GLA_RANK], F32R, None), ("a_lo", [P, KT, GLA_RANK], F32R, None),
            ("wa2", [GLA_RANK, GLA_KW], F32, None),
            ("cat_hi_gla", [P, KT, T], F32R, "k_for_chunk"), ("cat_lo_gla", [P, KT, T], F32R, "scoresT"),
            ("norm_g", [P, GLA_W], F32, "ws"),
        ])
        self.qkv = overlay([
            ("qT", [P, KT, T], F32, None), ("kT", [P, KT, T], F32, None), ("v_att", [P, TT, D], F32, None),
            ("p0", [P, TT, T], F32, None), ("p1", [P, TT, T], F32, None),
            ("pT0", [P, TT, T], F32, None), ("pT1", [P, TT, T], F32, None),
            ("bias", [P, C_HEADS, BIAS_ROWS, GRID_W], F32, None),
            ("cat_hi_qkv", [P, KT, T], F32R, "qT"), ("cat_lo_qkv", [P, KT, T], F32R, "kT"),
        ])
        self.ab = overlay([
            ("qT_ab", [P, KT, T], F32, None), ("kT_ab", [P, 4, T], F32, None),
            ("spare", [P, 4, T], F32, None), ("proj", [P, TT, 1536], F32, None),
            ("p0_ab", [P, TT, T], F32, None), ("p1_ab", [P, TT, T], F32, None),
            ("pT0_ab", [P, TT, T], F32, None), ("pT1_ab", [P, TT, T], F32, None),
            ("rot", [P, TT, 12, HD], F32, None),
            ("cat_lo_ab", [P, KT, T], F32R, None),
            ("cat_hi_ab", [P, KT, T], F32R, "qT_ab"),
        ])
        self.mem_row, self.mem_hi, self.mem_lo = (
            nc.alloc_sbuf_tensor_at(name, [P, *shape], dt, offset=self.overlay_at["bias"] + i * D * TT * 4)
            for i, (name, shape, dt) in enumerate((("mem_row", (TT, D), F32), ("mem_hi", (KT, T), F32R), ("mem_lo", (KT, T), F32R))))
        self.bank = [nc.alloc_psum_tensor(f"bank{i}", [P, 512], F32) for i in range(8)]
        self.bank_free = [None] * 8
        self.raw_free = [None] * RING
        self.part_free = [None] * RING
        self.raw_at = self.part_at = 0
        self.x_ready = [None] * 4

    def const(self, name):
        start, n = CONST[name]
        return self.consts[:, start:start + n]

    def after(self, eng, *tokens):
        self.c.after(eng, *tokens)

    def done(self, eng, ins):
        return self.c.mark(ins, eng.sem)

    def do(self, eng, tokens, ins):
        self.c.after(eng, *tokens)
        return self.c.mark(ins(eng.eng), eng.sem)

    def product(self, out, stat_hi, stat_lo, move_hi, move_lo, start=False, stop=False):
        pe = self.nc.tensor
        pe.matmul(out, stat_hi, move_hi, start=start, stop=False, skip_group_check=True)
        pe.matmul(out, stat_hi, move_lo, start=False, stop=False, skip_group_check=True)
        return pe.matmul(out, stat_lo, move_hi, start=False, stop=stop, skip_group_check=True)

    def acc(self, tt, half):
        return self.bank[2 * tt + half]

    def load_and_split(self, loads, parts):
        r = self.raw_at % RING
        self.raw_at += 1
        if self.part_at >= parts:
            self.part_at = 0
        s = self.part_at
        self.part_at += 1
        raw, hi, lo = self.raw[r], self.part_hi[s], self.part_lo[s]
        self.after(self.sp, self.raw_free[r])
        if self.raw_free[r] is not None and self.raw_free[r].loops:
            self.nc.sync.sem_inc(self.loads_sem, 1)
        words = 0
        for view, src in loads:
            dst, words = view(raw)
            landed = self.c.mark(self.nc.sync.dma_start(dst, src), self.landed_sem[r], 16)
        rounded = self.do(self.act, [landed, self.part_free[s]],
                          lambda e: e.activation(hi[:, 0:words], raw[:, 0:words], ACT.Copy))
        split = self.do(self.dve, [landed, rounded, self.part_free[s]],
                        lambda e: e.tensor_tensor(lo[:, 0:words], raw[:, 0:words],
                                                  hi[:, 0:words].bitcast(F32), ALU.subtract))
        self.raw_free[r] = split
        return s, split

    def stream_step(self, st):
        if st.sent < len(st.loads):
            st.ready.append(self.load_and_split(st.loads[st.sent], st.parts))
            st.sent += 1

    def take(self, st):
        s, split = st.ready.pop(0)
        self.after(self.pe, split)
        return s

    def release(self, s, token):
        self.part_free[s] = token

    @staticmethod
    def square_loads(w, col, ncols=512):
        out = []
        for kh in range(2):
            src = w[kh * 512:(kh + 1) * 512, col:col + ncols].rearrange("(k p) n -> p k n", p=P)
            out.append([(lambda raw, n=ncols: (raw[:, 0:4 * n].rearrange("p (k n) -> p k n", k=4), 4 * n), src)])
        return out

    def square_stream(self, blocks):
        return Stream([x for w, col in blocks for x in self.square_loads(w, col)], MIX_PARTS)

    def block_token_major(self, st, banks, hi, lo, ready, start=True, ahead=True):
        pe = self.pe
        done = [None] * TT
        for kh in range(2):
            s = self.take(st)
            for tt in range(TT):
                if kh == 0:
                    self.after(pe, self.bank_free[banks[tt]])
                self.after(pe, ready[tt * 2 + kh])
                for k in range(4):
                    kk = kh * 4 + k
                    mm = self.product(self.bank[banks[tt]][:, :], hi[:, kk, tt * P:(tt + 1) * P],
                                      lo[:, kk, tt * P:(tt + 1) * P],
                                      self.part_hi[s][:, k * 512:(k + 1) * 512],
                                      self.part_lo[s][:, k * 512:(k + 1) * 512],
                                      start=(start and kk == 0), stop=(kk == KT - 1))
                if kh == 1 or tt == TT - 1:
                    done[tt] = self.done(pe, mm)
            self.release(s, done[TT - 1])
            self.stream_step(st)
        return done

    def block_transposed(self, st, banks, hi, lo, ready):
        pe = self.pe
        for kh in range(2):
            s = self.take(st)
            for b in range(2):
                if kh == 0:
                    self.after(pe, self.bank_free[banks[b]])
                self.after(pe, [ready[tt * 2 + kh] for tt in range(TT)])
                for m in (2 * b, 2 * b + 1):
                    for k in range(4):
                        kk = kh * 4 + k
                        w = slice(k * 512 + m * P, k * 512 + (m + 1) * P)
                        mm = self.product(self.bank[banks[b]][:, (m % 2) * T:(m % 2 + 1) * T],
                                          self.part_hi[s][:, w], self.part_lo[s][:, w],
                                          hi[:, kk, :], lo[:, kk, :],
                                          start=(kk == 0 and m % 2 == 0), stop=(kk == KT - 1))
            done = self.done(pe, mm)
            self.release(s, done)
            self.stream_step(st)
        return done

    def residual(self, scale):
        for tt in range(TT):
            for half in range(2):
                b = 2 * tt + half
                self.after(self.pe, self.bank_free[b], self.x_ready[b])
                for k in range(4):
                    kk = half * 4 + k
                    mm = self.product(self.bank[b][:, k * P:(k + 1) * P],
                                 self.x_hi[:, kk, tt * P:(tt + 1) * P], self.x_lo[:, kk, tt * P:(tt + 1) * P],
                                 self.resid_hi[:, scale, :], self.resid_lo[:, scale, :], start=(k == 0))
                    if kk == KT - 1 and tt == TT - 1:
                        return self.done(self.pe, mm)

    def out_projection(self, st, hi, lo, ready, scale=0):
        self.residual(scale)
        for half in range(2):
            done = self.block_token_major(st, [half, 2 + half], hi, lo, ready, start=False)
        for i in range(MIX_PARTS, RING):
            self.part_free[i] = done[1]
        return done

    def transpose_block(self, src, tt, half, bank, ready):
        self.after(self.pe, self.bank_free[bank], ready)
        for k in range(4):
            c = (half * 4 + k) * P
            mm = self.nc.tensor.transpose(self.bank[bank][:, k * P:(k + 1) * P], src[:, tt, c:c + P],
                                          self.const("identity"))
        return self.done(self.pe, mm)

    def split_from_psum(self, bank_ap, hi, lo, ready, waits=()):
        h = self.do(self.act, [ready, *waits], lambda e: e.activation(hi, bank_ap, ACT.Copy))
        return self.do(self.dve, [h, ready, *waits],
                       lambda e: e.tensor_tensor(lo, bank_ap, hi.bitcast(F32), ALU.subtract))

    def layer_norm(self, acc_done, g, b, eps, final=False, source=None):
        src = source or (lambda tt, half: self.acc(tt, half)[:, :])
        normed = {}

        def statistics(tt):
            for half in range(2):
                st = self.do(self.dve, [acc_done[tt]], lambda e: e.bn_stats(self.stats[:, tt, half, :], src(tt, half)))
            agg = self.do(self.dve, [st], lambda e: e.bn_aggr(self.mv[:, tt, :], self.stats[:, tt, :, :]))
            eps_added = self.do(self.dve, [agg], lambda e: e.tensor_scalar(
                self.rstd[:, tt:tt + 1], self.mv[:, tt, 1:2], eps, None, ALU.add))
            return self.do(self.pool, [eps_added], lambda e: e.tensor_tensor(
                self.rstd[:, tt:tt + 1], self.rstd[:, tt:tt + 1], self.minus_half[:, 0:1], ALU.pow))

        def norm(tt, inv):
            for half in range(2):
                normed[tt, half] = self.do(self.dve, [inv, self.xhat_free], lambda e: e.tensor_scalar(
                    self.xhat[:, tt, half * 512:(half + 1) * 512], src(tt, half),
                    self.mv[:, tt, 0:1], self.rstd[:, tt:tt + 1], ALU.subtract, ALU.mult))
                if source is None:
                    self.bank_free[2 * tt + half] = normed[tt, half]

        def turn_and_scale(tt):
            for half in range(2):
                n = 2 * tt + half
                bank = 4 + n
                xf = self.xf[n % 2]
                turned[n] = self.transpose_block(self.xhat, tt, half, bank, normed[tt, half])
                for k in range(4):
                    kk = half * 4 + k
                    scaled[n] = self.do(self.act, [turned[n], self.xf_free[n % 2]], lambda e: e.activation(
                        xf[:, k, :], self.bank[bank][:, k * P:(k + 1) * P], ACT.Identity,
                        bias=self.cols[:, b[0], b[1] + kk:b[1] + kk + 1],
                        scale=self.cols[:, g[0], g[1] + kk:g[1] + kk + 1]))
                self.bank_free[bank] = scaled[n]

        def split(n):
            tt, half = divmod(n, 2)
            xf = self.xf[n % 2]
            hi = self.x_hi[:, half * 4:half * 4 + 4, tt * P:(tt + 1) * P]
            lo = self.x_lo[:, half * 4:half * 4 + 4, tt * P:(tt + 1) * P]
            rounded = self.do(self.dve, [scaled[n], acc_done], lambda e: e.tensor_copy(hi, xf[:, :, :]))
            self.x_ready[n] = self.do(self.dve, [rounded], lambda e: e.tensor_tensor(
                lo, xf[:, :, :], hi.bitcast(F32), ALU.subtract))
            self.xf_free[n % 2] = self.x_ready[n]

        turned, scaled = {}, {}
        norm(0, statistics(0))
        if final:
            norm(1, statistics(1))
            return normed
        turn_and_scale(0)
        second = statistics(1)
        split(0)
        norm(1, second)
        split(1)
        turn_and_scale(1)
        split(2)
        split(3)
        turned = turned[3]
        self.xhat_free = turned
        self.x_affine_of, self.xhat_ready = (g, b), normed

    def store_final(self, normed, g_dram, b_dram):
        gb = [self.raw[0][:, 0:D], self.raw[1][:, 0:D]]
        self.after(self.sp, self.raw_free[0], self.raw_free[1])
        for dst, src in zip(gb, (g_dram, b_dram)):
            landed = self.c.mark(self.nc.sync.dma_start(dst, src.partition_broadcast(P)), self.last_gb_sem, 16)
        for tt in range(TT):
            for half in range(2):
                cols = slice(half * 512, (half + 1) * 512)
                x = self.xhat[:, tt, cols]
                m = self.do(self.dve, [normed[tt, half], landed],
                            lambda e: e.tensor_tensor(x, x, gb[0][:, cols], ALU.mult))
                s = self.do(self.dve, [m], lambda e: e.tensor_tensor(x, x, gb[1][:, cols], ALU.add))
                self.after(self.sp, s)
                stored = self.c.mark(self.nc.sync.dma_start(
                    self.out[0, tt * P:(tt + 1) * P, cols], x), self.out_sem, 16)
        self.after(self.sp, stored)

    def ffn_loads_up(self, w_gate, w_up, col):
        loads = []
        for kh in range(2):
            one = []
            for n, w in enumerate((w_gate, w_up)):
                src = w(slice(kh * 512, (kh + 1) * 512), bass.ds(col, FC)).rearrange("(k p) n -> p k n", p=P)
                one.append((lambda raw, n=n: (raw[:, :].rearrange("p (k m n) -> p k m n", k=4, m=2)[:, :, n, :], SLOT), src))
            loads.append(one)
        return loads

    def ffn_load_down(self, w_down, row):
        src = w_down(bass.ds(row, FC), slice(0, D)).rearrange("(j p) n -> p j n", p=P)
        return [(lambda raw: (raw[:, :].rearrange("p (j n) -> p j n", j=2), SLOT), src)]

    def ffn_up(self, tt, slots, gate=None):
        bank = 4 + tt
        pe = self.pe
        self.after(pe, self.bank_free[bank])
        for kh in range(2):
            s, split = slots[kh]
            self.after(pe, split, self.x_ready[2 * tt + kh])
            for k in range(4):
                kk = kh * 4 + k
                mm = self.product(self.bank[bank][:, :], self.x_hi[:, kk, tt * P:(tt + 1) * P],
                                  self.x_lo[:, kk, tt * P:(tt + 1) * P],
                                  self.part_hi[s][:, k * 512:(k + 1) * 512],
                                  self.part_lo[s][:, k * 512:(k + 1) * 512],
                                  start=(kk == 0), stop=(kk == KT - 1))
            token = self.done(pe, mm)
            if tt == TT - 1:
                self.release(s, token)
        return token

    def ffn_act(self, tt, up_done, gate):
        bank = 4 + tt
        act = self.do(self.act, [up_done, self.h_free[tt]], lambda e: e.activation(
            self.silu[tt][:, :], self.bank[bank][:, 0:FC], ACT.Silu))
        if gate is None:
            f = lambda e: e.tensor_tensor(self.h[tt][:, :], self.silu[tt][:, :], self.bank[bank][:, FC:2 * FC], ALU.mult)
        else:
            f = lambda e: e.scalar_tensor_tensor(out=self.h[tt][:, :], in0=self.silu[tt][:, :], scalar=gate(tt),
                                                 in1=self.bank[bank][:, FC:2 * FC], op0=ALU.mult, op1=ALU.mult)
        h = self.do(self.dve, [act, up_done, self.hT_turned[tt]], f)
        self.bank_free[bank] = h
        self.h_free[tt] = h
        return h

    def ffn_turn(self, tt, par, h_ready):
        bank = 6 + tt
        self.after(self.pe, h_ready, self.bank_free[bank])
        for j in range(2):
            mm = self.nc.tensor.transpose(self.bank[bank][:, j * P:(j + 1) * P],
                                          self.h[tt][:, j * P:(j + 1) * P], self.const("identity"))
        self.hT_turned[tt] = turned = self.done(self.pe, mm)
        hi, lo = self.hT_hi[par][tt][:, :, :], self.hT_lo[par][tt][:, :, :]
        src = self.bank[bank][:, 0:FC].rearrange("p (j t) -> p j t", j=2)
        ready = self.split_from_psum(src, hi, lo, turned, [self.hT_used[par][tt]])
        self.bank_free[bank] = ready
        return ready

    def ffn_down(self, tt, par, slot, hT_ready, start=False):
        s, split = slot
        self.after(self.pe, split, hT_ready)
        for j in range(2):
            for half in range(2):
                if start and j == 0:
                    self.after(self.pe, self.bank_free[2 * tt + half])
                mm = self.product(self.acc(tt, half)[:, :], self.hT_hi[par][tt][:, j, :], self.hT_lo[par][tt][:, j, :],
                                  self.part_hi[s][:, j * D + half * 512:j * D + (half + 1) * 512],
                                  self.part_lo[s][:, j * D + half * 512:j * D + (half + 1) * 512])
        token = self.done(self.pe, mm)
        self.hT_used[par][tt] = token
        if tt == TT - 1:
            self.release(s, token)
        return token

    def ffn_prefetch(self, w):
        return [self.load_and_split(x, RING) for x in self.ffn_loads_up(w[0], w[1], 0)]

    def ffn(self, weights, n_chunks, up_slots, gate=None, following=None):
        w_gate, w_up, w_down = weights
        state = {"up": up_slots}

        def phase(c, par, first=False, last=False):
            slots = state["up"]
            nxt = None
            if not last:
                nxt = [self.load_and_split(x, RING) for x in self.ffn_loads_up(w_gate, w_up, (c + 1) * FC)]
            elif following is not None:
                nxt = [self.load_and_split(x, RING) for x in following]
            up0 = self.ffn_up(0, slots)
            h0 = self.ffn_act(0, up0, gate)
            down_slot = self.load_and_split(self.ffn_load_down(w_down, c * FC), RING)
            up1 = self.ffn_up(1, slots)
            h1 = self.ffn_act(1, up1, gate)
            t0 = self.ffn_turn(0, par, h0)
            acc = None
            if not first:
                prev = state["down"]
                for tt in range(TT):
                    self.ffn_down(tt, 1 - par, prev[0], prev[1][tt])
            t1 = self.ffn_turn(1, par, h1)
            state["down"] = (down_slot, [t0, t1])
            state["up"] = nxt

        phase(0, 0, first=True)
        units = (n_chunks - 2) // 2
        before = dict(self.c.count)
        phase(1, 1)
        phase(2, 0)
        with self.c.repeat(before, units) as i:
            phase(i * 2 + 1, 1)
            phase(i * 2 + 2, 0)
        for c in range(1 + 2 * units, n_chunks):
            phase(c, c % 2, last=(c == n_chunks - 1))
        par = (n_chunks - 1) % 2
        slot, turned = state["down"]
        done = [self.ffn_down(tt, par, slot, turned[tt]) for tt in range(TT)]
        return done, state["up"]

    def load_small(self, dst, src, waits=()):
        self.after(self.pool, *waits)
        return self.c.mark(self.nc.gpsimd.dma_start(dst, src), self.small_sem, 16)

    def start(self):
        a, nc = self.a, self.nc
        self.xhat_free = None
        self.xf_free = [None, None]
        self.h_free = [None] * TT
        self.hT_turned = [None] * TT
        self.hT_used = [[None] * TT for _ in range(2)]
        x_landed = self.c.mark(nc.sync.dma_start(self.xhat[:, :, :], a["x"][0].rearrange("(t p) d -> p t d", p=P)),
                               self.x_sem, 16)
        c_landed = self.c.mark(nc.sync.dma_start(self.consts[:, :], a["consts"]), self.const_sem, 16)
        zeroed = self.do(self.pool, [], lambda e: e.memset(self.rows[:, :, :], 0.0))
        halves = self.do(self.pool, [], lambda e: e.memset(self.minus_half[:, :], -0.5))
        self.after(self.pool, zeroed, halves)
        at = 0
        self.col_of = {}
        for name, n in (("ln_mix_g", 16), ("ln_mix_b", 16), ("ln_ffn_g", 16), ("ln_ffn_b", 16), ("gm_bs", 8), ("gla_ba", 4)):
            src = a[name]
            src = src.rearrange("l h t -> (l h) t") if name == "gm_bs" else src.rearrange("l (k p) -> (l k) p", p=P)
            self.load_small(self.rows[at:at + n, 0, :], src)
            self.col_of[name] = (0, at)
            at += n
        for i, name in enumerate(("ln_g_2", "ln_b_2")):
            self.load_small(self.rows[i * 64:(i + 1) * 64, 1, :], a[name].rearrange("l s (k p) -> (l s k) p", p=P))
            self.col_of[name] = (1, i * 64)
        self.load_small(self.sink[:, :], a["ab_sink_2"][0].partition_broadcast(P))
        self.load_small(self.gains[:, 0, :], a["ab_q_gain_2"][0].partition_broadcast(P))
        rows_landed = self.load_small(self.gains[:, 1, :], a["ab_k_gain_2"][0].partition_broadcast(P))
        self.small_loaded = rows_landed
        self.columns_made = False
        self.after(self.dve, c_landed)
        self.after(self.pe, c_landed)
        self.to_xT(self.xhat, [x_landed] * 2)
        for i, name in enumerate(("alpha_identity", "alpha2_identity")):
            h = self.do(self.act, [c_landed], lambda e: e.activation(self.resid_hi[:, i, :], self.const(name), ACT.Copy))
            resid = self.do(self.dve, [h], lambda e: e.tensor_tensor(
                self.resid_lo[:, i, :], self.const(name), self.resid_hi[:, i, :].bitcast(F32), ALU.subtract))
        self.after(self.pe, resid)

    def start_columns(self):
        self.columns_made = True
        self.after(self.pe, self.small_loaded, self.bank_free[7])
        for i in range(2):
            mm = self.nc.tensor.transpose(self.bank[7][:, i * P:(i + 1) * P], self.rows[:, i, :], self.const("identity"))
        turned = self.done(self.pe, mm)
        ready = self.bank_free[7] = self.do(self.dve, [turned], lambda e: e.tensor_copy(
            self.cols[:, :, :], self.bank[7][:, 0:2 * P].rearrange("p (i c) -> p i c", i=2)))
        for eng in (self.act, self.pool):
            self.after(eng, ready)

    def to_xT(self, src, ready):
        for tt in range(TT):
            for half in range(2):
                n = 2 * tt + half
                turned = self.transpose_block(src, tt, half, 4 + n, ready[tt])
                hi = self.x_hi[:, half * 4:half * 4 + 4, tt * P:(tt + 1) * P]
                lo = self.x_lo[:, half * 4:half * 4 + 4, tt * P:(tt + 1) * P]
                self.x_ready[n] = self.split_from_psum(
                    self.bank[4 + n][:, :].rearrange("p (k t) -> p k t", k=4), hi, lo, turned)
                self.bank_free[4 + n] = self.x_ready[n]
        self.xhat_free = turned

    def gla_stream(self, layer):
        w = self.a["w_in"][layer]
        cols = [1024, 0, 512, 1536, 2048]
        w_out = self.a["w_out"][layer]
        return self.square_stream([(w, c) for c in cols] + [(w_out, 0), (w_out, 512)])

    def hybrid_mixer(self, layer, st, free):
        a, g, nc = self.a, self.gla, self.nc
        dve, act, pool, pe = self.dve, self.act, self.pool, self.pe
        self.load_small(g["a_raw"][:, :, :], a["w_in"][layer][:, 2560:2576].rearrange("(k p) n -> p k n", p=P), [free])
        self.load_small(g["wa2"][:, :], a["gla_wa2"][layer])
        self.load_small(g["ws"][:, :, :], a["gm_ws"][layer].rearrange("h t s -> t h s"))
        self.load_small(g["gm_g"][:, :], a["gm_ln_g"][layer].partition_broadcast(P))
        loaded = self.load_small(g["gm_b"][:, :], a["gm_ln_b"][layer].partition_broadcast(P))
        k_zero = self.do(pool, [free], lambda e: e.memset(g["k_for_chunk"][:, :, :, :], 0.0))
        q_zero = self.do(pool, [free], lambda e: e.memset(g["q_heads"][:, :, :, :], 0.0))
        alr = self.small[:, 0:2 * P].rearrange("p (t c) -> p t c", t=TT)
        alr_zero = self.do(pool, [self.small_free], lambda e: e.memset(alr, 0.0))
        masked = self.do(pool, [loaded], lambda e: e.affine_select(
            out=g["ws"][:, :, :], in_=g["ws"][:, :, :], compare_op=ALU.is_ge, fill=0.0, base=0,
            pattern=[[0, GM_HEADS], [-1, P]], channel_multiplier=1))
        a_hi = self.do(act, [loaded], lambda e: e.activation(g["a_hi"][:, :, :], g["a_raw"][:, :, :], ACT.Copy))
        a_lo = self.do(dve, [a_hi], lambda e: e.tensor_tensor(
            g["a_lo"][:, :, :], g["a_raw"][:, :, :], g["a_hi"][:, :, :].bitcast(F32), ALU.subtract))
        self.after(pe, a_lo, self.x_ready, self.bank_free[4])
        for tt in range(TT):
            for k in range(KT):
                mm = self.product(self.bank[4][:, tt * 16:tt * 16 + 16], self.x_hi[:, k, tt * P:(tt + 1) * P],
                                  self.x_lo[:, k, tt * P:(tt + 1) * P], g["a_hi"][:, k, :], g["a_lo"][:, k, :],
                                  start=(k == 0 and tt == 0), stop=(k == KT - 1))
        a_done = self.done(pe, mm)
        a_copied = self.do(dve, [a_done, alr_zero], lambda e: e.tensor_copy(
            alr[:, :, 0:GLA_RANK], self.bank[4][:, 0:32].rearrange("p (t c) -> p t c", t=TT)))
        self.bank_free[4] = a_copied
        if not self.columns_made:
            self.start_columns()
        qk_done = self.block_transposed(st, [0, 1], self.x_hi, self.x_lo, self.x_ready)
        self.after(pe, a_copied, self.bank_free[5])
        for tt in range(TT):
            mm = nc.tensor.transpose(self.bank[5][:, tt * P:(tt + 1) * P], alr[:, tt, :], self.const("identity"))
        turned = self.done(pe, mm)
        alrT = self.small[0:GLA_RANK, 256:512]
        alrT_ready = self.do(dve, [turned, self.small_free], lambda e: e.tensor_copy(alrT, self.bank[5][0:GLA_RANK, 0:T]))
        self.bank_free[5] = alrT_ready
        self.after(pe, alrT_ready, self.bank_free[6])
        for dt in range(2):
            mm = nc.tensor.matmul(self.bank[6][:, dt * T:(dt + 1) * T], g["wa2"][:, dt * P:(dt + 1) * P], alrT,
                                  start=True, stop=True, skip_group_check=True)
        z_done = self.done(pe, mm)
        self.small_free = z_done
        log_a, tmp, b_cum, exp_b = g["log_a"], g["tmp_a"], g["b_cum"], g["exp_b"]
        ba_t, ba_c = self.col_of["gla_ba"]
        for dt in range(2):
            c = ba_c + 2 * layer + dt
            z = self.do(dve, [z_done, free], lambda e: e.tensor_scalar(
                log_a[:, dt, :], self.bank[6][:, dt * T:(dt + 1) * T], self.cols[:, ba_t, c:c + 1], None, ALU.add))
        self.bank_free[6] = z
        ab = self.do(act, [z], lambda e: e.activation(tmp[:, :, :], log_a[:, :, :], ACT.Abs))
        ex = self.do(act, [ab], lambda e: e.activation(tmp[:, :, :], tmp[:, :, :], ACT.Exp, scale=-1.0))
        ln = self.do(act, [ex], lambda e: e.activation(tmp[:, :, :], tmp[:, :, :], ACT.Ln, bias=1.0))
        mn = self.do(dve, [z, ab], lambda e: e.tensor_scalar(log_a[:, :, :], log_a[:, :, :], 0.0, None, ALU.min))
        la = self.do(dve, [mn, ln], lambda e: e.tensor_tensor(log_a[:, :, :], log_a[:, :, :], tmp[:, :, :], ALU.subtract))
        flat = lambda t: t[:, :, :].rearrange("p d t -> p (d t)")
        scan = self.do(dve, [la], lambda e: e.tensor_tensor_scan(
            flat(b_cum), self.const("scan_keep"), flat(log_a), 0.0, ALU.mult, ALU.add))
        inv = 1.0 / GLA_TAU
        eb = self.do(act, [scan], lambda e: e.activation(exp_b[:, :, :], b_cum[:, :, :], ACT.Exp, scale=inv))
        enb = self.do(act, [scan, la], lambda e: e.activation(tmp[:, :, :], b_cum[:, :, :], ACT.Exp, scale=-inv))
        tot = b_cum[:, :, :].rearrange("p d (c j) -> p d c j", j=GLA_CHUNK)[:, :, :, GLA_CHUNK - 1]
        span = self.small2
        sp1 = self.do(dve, [scan, self.small2_free], lambda e: e.tensor_copy(span[:, :, 0:1], tot[:, :, 0:1]))
        self.do(dve, [], lambda e: e.tensor_copy(span[:, :, 2:3], tot[:, :, 1:2]))
        sp2 = self.do(dve, [], lambda e: e.tensor_copy(span[:, :, 5:6], tot[:, :, 2:3]))
        sp3 = self.do(dve, [sp1, sp2], lambda e: e.tensor_tensor(span[:, :, 1:2], span[:, :, 0:1], tot[:, :, 1:2], ALU.add))
        sp4 = self.do(dve, [sp2], lambda e: e.tensor_tensor(span[:, :, 4:5], span[:, :, 2:3], tot[:, :, 2:3], ALU.add))
        sp5 = self.do(dve, [sp3], lambda e: e.tensor_tensor(span[:, :, 3:4], span[:, :, 1:2], tot[:, :, 2:3], ALU.add))
        es = self.do(act, [sp4, sp5], lambda e: e.activation(span[:, :, :], span[:, :, :], ACT.Exp, scale=inv))
        for dt in range(2):
            for hh in range(2):
                rows = slice(hh * HD, (hh + 1) * HD)
                q_ready = self.do(dve, [eb, qk_done, q_zero], lambda e: e.scalar_tensor_tensor(
                    out=g["q_heads"][rows, dt, hh, :], in0=self.bank[0][rows, dt * T:(dt + 1) * T],
                    scalar=GLA_DK ** -0.5, in1=exp_b[rows, dt, :], op0=ALU.mult, op1=ALU.mult))
        k_inv = self.do(dve, [enb], lambda e: e.tensor_tensor(
            g["k_inv"][:, :, :], self.bank[1][:, :].rearrange("p (d t) -> p d t", d=2), tmp[:, :, :], ALU.mult))
        self.bank_free[0] = self.bank_free[1] = k_inv
        kc = g["k_for_chunk"]
        for c in range(NCH):
            cs = slice(c * GLA_CHUNK, (c + 1) * GLA_CHUNK)
            k_ready = self.do(dve, [k_inv, k_zero], lambda e: e.tensor_copy(kc[:, c, :, cs], g["k_inv"][:, :, cs]))
            if c:
                o = (0, 0, 1, 3)[c]
                for dt in range(2):
                    k_ready = self.do(dve, [es], lambda e: e.tensor_tensor(
                        kc[:, c, dt, 0:c * GLA_CHUNK].rearrange("p (c j) -> p c j", j=GLA_CHUNK),
                        g["k_inv"][:, dt, 0:c * GLA_CHUNK].rearrange("p (c j) -> p c j", j=GLA_CHUNK),
                        span[:, dt, o:o + c].unsqueeze(2).to_broadcast([P, c, GLA_CHUNK]), ALU.mult))
        self.small2_free = k_ready
        u_done = self.block_token_major(st, [2, 3], self.x_hi, self.x_lo, self.x_ready)
        for tt in range(TT):
            u_ready = self.do(act, [u_done[tt], free], lambda e: e.activation(g["u"][:, tt, :], self.bank[2 + tt][:, :], ACT.Gelu))
            self.bank_free[2 + tt] = u_ready
        vg_done = self.block_token_major(st, [0, 1], self.x_hi, self.x_lo, self.x_ready)
        for tt in range(TT):
            vg_ready = self.do(act, [vg_done[tt]], lambda e: e.activation(g["vg"][:, tt, :], self.bank[tt][:, :], ACT.Gelu))
            self.bank_free[tt] = vg_ready
        q_heads = g["q_heads"]
        self.after(pe, k_ready, q_ready, [self.bank_free[b] for b in range(4, 8)])
        for jt in range(TT):
            for dt in range(2):
                out = self.bank[4 + 2 * jt + dt][:, :].rearrange("p (h i) -> p h i", h=2)
                for c in range(2 * jt, NCH):
                    i = slice(c * GLA_CHUNK, (c + 1) * GLA_CHUNK)
                    mm = nc.tensor.matmul(out[:, :, i], kc[:, c, dt, jt * P:(jt + 1) * P], q_heads[:, dt, :, i],
                                          start=True, stop=True, skip_group_check=True)
        s_done = self.done(pe, mm)
        sT = g["scoresT"]
        for jt in range(TT):
            for dt in range(2):
                i = slice(jt * P, T)
                src = self.bank[4 + 2 * jt + dt][:, :].rearrange("p (h i) -> p h i", h=2)
                s_copied = self.do(act, [s_done], lambda e: e.activation(sT[:, jt, 2 * dt:2 * dt + 2, i], src[:, :, i], ACT.Copy))
                self.bank_free[4 + 2 * jt + dt] = s_copied
            s_masked = self.do(pool, [s_copied], lambda e: e.affine_select(
                out=sT[:, jt, :, jt * P:(jt + 1) * P], in_=sT[:, jt, :, jt * P:(jt + 1) * P], compare_op=ALU.is_ge,
                fill=0.0, base=0, pattern=[[0, GLA_HEADS], [1, P]], channel_multiplier=-1))
        v_done = self.block_token_major(st, [2, 3], self.x_hi, self.x_lo, self.x_ready)
        for tt in range(TT):
            v_ready = self.do(act, [v_done[tt]], lambda e: e.activation(g["v_gla"][:, tt, :], self.bank[2 + tt][:, :], ACT.Copy))
            self.bank_free[2 + tt] = v_ready
        g_done = self.block_token_major(st, [0, 1], self.x_hi, self.x_lo, self.x_ready)
        for tt in range(TT):
            g_ready = self.do(act, [g_done[tt]], lambda e: e.activation(g["silu_g"][:, tt, :], self.bank[tt][:, :], ACT.Silu))
            self.bank_free[tt] = g_ready
        vst = self.vstats
        for tt in range(TT):
            for h in range(GM_HEADS):
                bst = self.do(dve, [vg_ready, self.vstats_free], lambda e: e.bn_stats(
                    vst[:, tt, h, 0:6], g["vg"][:, tt, h * P:(h + 1) * P]))
        for tt in range(TT):
            for h in range(GM_HEADS):
                agg = self.do(dve, [bst], lambda e: e.bn_aggr(vst[:, tt, h, 6:8], vst[:, tt, h, 0:6]))
        rs = self.small3[:, 0:8].rearrange("p (t h) -> p t h", t=TT)
        add_eps = self.do(dve, [agg], lambda e: e.tensor_scalar(rs, vst[:, :, :, 7], LN_EPS, None, ALU.add))
        r_ready = self.do(pool, [add_eps], lambda e: e.tensor_tensor(
            self.small3[:, 0:8], self.small3[:, 0:8], self.minus_half[:, 0:8], ALU.pow))
        for tt in range(TT):
            for h in range(GM_HEADS):
                cols = slice(h * P, (h + 1) * P)
                vn = self.do(dve, [r_ready], lambda e: e.tensor_scalar(
                    g["vg"][:, tt, cols], g["vg"][:, tt, cols], vst[:, tt, h, 6:7],
                    rs[:, tt, h:h + 1], ALU.subtract, ALU.mult))
        self.vstats_free = vn
        for tt in range(TT):
            vm = self.do(pool, [vn, loaded], lambda e: e.tensor_tensor(g["vg"][:, tt, :], g["vg"][:, tt, :], g["gm_g"][:, :], ALU.mult))
            v_ln = self.do(pool, [vm], lambda e: e.tensor_tensor(g["vg"][:, tt, :], g["vg"][:, tt, :], g["gm_b"][:, :], ALU.add))
        self.after(pe, masked, self.bank_free[4])
        for h in range(GM_HEADS):
            mm = nc.tensor.transpose(self.bank[4][:, h * P:(h + 1) * P], g["ws"][:, h, :], self.const("identity"))
        w_turned = self.done(pe, mm)
        w_ready = self.do(act, [w_turned], lambda e: e.activation(
            g["wsT"][:, :, :], self.bank[4][:, :].rearrange("p (h t) -> p h t", h=GM_HEADS), ACT.Copy))
        self.bank_free[4] = w_ready
        ng_loaded = self.load_small(g["norm_g"][:, :], a["gla_norm_g"][layer].partition_broadcast(P), [w_turned])
        self.after(pe, v_ready, s_masked, self.bank_free[6], self.bank_free[7])
        for tt in range(TT):
            for h in range(GLA_HEADS):
                for jt in range(tt + 1):
                    mm = nc.tensor.matmul(self.bank[6 + tt][:, h * P:(h + 1) * P], sT[:, jt, h, tt * P:(tt + 1) * P],
                                          g["v_gla"][:, jt, h * P:(h + 1) * P], start=(jt == 0), stop=(jt == tt),
                                          skip_group_check=True)
        o_done = self.done(pe, mm)
        self.after(pe, w_ready, v_ln, self.bank_free[4], self.bank_free[5])
        for tt in range(TT):
            for h in range(GM_HEADS):
                mm = nc.tensor.matmul(self.bank[4 + tt][:, h * P:(h + 1) * P], g["wsT"][:, h, :],
                                      g["vg"][:, tt, h * P:(h + 1) * P], start=True, stop=True, skip_group_check=True)
        sg_done = self.done(pe, mm)
        cat = self.xhat
        for tt in range(TT):
            gg = self.do(pool, [g_ready, ng_loaded], lambda e: e.tensor_tensor(
                g["silu_g"][:, tt, :], g["silu_g"][:, tt, :], g["norm_g"][:, :], ALU.mult))
            sq = self.do(act, [o_done, self.xhat_free], lambda e: e.activation(cat[:, tt, 512:1024], self.bank[6 + tt][:, :], ACT.Square))
            ms = self.do(dve, [sq, vn], lambda e: e.tensor_reduce(
                rs[:, tt, :], cat[:, tt, 512:1024].rearrange("p (h e) -> p h e", h=GLA_HEADS), AX.X, ALU.add))
        me = self.do(dve, [ms], lambda e: e.tensor_scalar(rs, rs, 1.0 / GLA_DV, RMS_EPS, ALU.mult, ALU.add))
        rr = self.do(pool, [me], lambda e: e.tensor_tensor(
            self.small3[:, 0:8], self.small3[:, 0:8], self.minus_half[:, 0:8], ALU.pow))
        cat_ready = [None] * TT
        bs_t, bs_c = self.col_of["gm_bs"]
        for tt in range(TT):
            for h in range(GLA_HEADS):
                cols = slice(h * P, (h + 1) * P)
                self.do(dve, [rr, gg], lambda e: e.scalar_tensor_tensor(
                    out=cat[:, tt, 512 + h * P:512 + (h + 1) * P], in0=self.bank[6 + tt][:, cols],
                    scalar=rs[:, tt, h:h + 1], in1=g["silu_g"][:, tt, cols], op0=ALU.mult, op1=ALU.mult))
                c = bs_c + layer * GM_HEADS + h
                cat_ready[tt] = self.do(dve, [sg_done, u_ready], lambda e: e.scalar_tensor_tensor(
                    out=cat[:, tt, cols], in0=self.bank[4 + tt][:, cols], scalar=self.cols[:, bs_t, c:c + 1],
                    in1=g["u"][:, tt, cols], op0=ALU.add, op1=ALU.mult))
            self.bank_free[4 + tt] = self.bank_free[6 + tt] = cat_ready[tt]
        hi, lo = g["cat_hi_gla"], g["cat_lo_gla"]
        ready = [None] * 4
        for tt in range(TT):
            for half in range(2):
                n = 2 * tt + half
                turned = self.transpose_block(cat, tt, half, 4 + n, cat_ready)
                ready[n] = self.split_from_psum(
                    self.bank[4 + n][:, :].rearrange("p (k t) -> p k t", k=4),
                    hi[:, half * 4:half * 4 + 4, tt * P:(tt + 1) * P], lo[:, half * 4:half * 4 + 4, tt * P:(tt + 1) * P],
                    turned)
                self.bank_free[4 + n] = ready[n]
        self.xhat_free = turned
        return hi, lo, ready

    def attention(self, heads, scale, p, pT, cat_hi, cat_lo):
        dve, act, pe, nc = self.dve, self.act, self.pe, self.nc
        n = len(heads)
        st = self.att_stats
        ptr, soft, sums = {}, {}, {}
        last_flush = None
        p_free, pT_free = [None, None], [None, None]

        def scores(i):
            hd, b = heads[i], 4 + i % 2
            self.after(pe, self.bank_free[b], hd["ready"])
            for qt in range(TT):
                for j, (q, k) in enumerate(hd["terms"]):
                    mm = nc.tensor.matmul(self.bank[b][:, qt * T:(qt + 1) * T], q[:, qt * P:(qt + 1) * P], k,
                                          start=(j == 0), stop=(j == len(hd["terms"]) - 1), skip_group_check=True)
            s_done = self.done(pe, mm)
            P_ = p[i % 2]
            top = st[:, i, 0, :]
            if hd["bias"] is None:
                src = self.bank[b][:, :].rearrange("p (q k) -> p q k", q=TT)
                m = self.do(dve, [s_done, self.att_free], lambda e: e.tensor_reduce(top, src, AX.X, ALU.max))
                m = self.do(dve, [m], lambda e: e.tensor_scalar(top, top, -scale, None, ALU.mult))
                mult, waits = scale, [p_free[i % 2]]
            else:
                for qt in range(TT):
                    rows = lambda ap: ap.rearrange("p (m w) -> p m w", w=hd["bias"](qt).shape[2])
                    z = self.do(dve, [s_done, p_free[i % 2], hd["bias_ready"]], lambda e: e.scalar_tensor_tensor(
                        out=rows(P_[:, qt, :]), in0=rows(self.bank[b][:, qt * T:(qt + 1) * T]), scalar=scale,
                        in1=hd["bias"](qt), op0=ALU.mult, op1=ALU.add))
                self.bank_free[b] = z
                m = self.do(dve, [z, self.att_free], lambda e: e.tensor_reduce(top, P_[:, :, :], AX.X, ALU.max))
                if hd["sink"] is None:
                    m = self.do(dve, [m], lambda e: e.tensor_scalar(top, top, -1.0, None, ALU.mult))
                else:
                    m = self.do(dve, [m], lambda e: e.tensor_scalar(top, top, hd["sink"], -1.0, ALU.max, ALU.mult))
                mult, waits = 1.0, []
            for qt in range(TT):
                src = self.bank[b][:, qt * T:(qt + 1) * T] if hd["bias"] is None else P_[:, qt, :]
                ex = self.do(act, [m, *waits], lambda e: e.activation(
                    P_[:, qt, :], src, ACT.Exp, bias=st[:, i, 0, qt:qt + 1], scale=mult,
                    accum_out=st[:, i, 1, qt:qt + 1]))
            if hd["bias"] is None:
                self.bank_free[b] = ex
            if hd["sink"] is not None:
                es = self.do(act, [m], lambda e: e.activation(st[:, i, 2, :], top, ACT.Exp, bias=hd["sink"]))
                sums[i] = (es, ex)
            soft[i] = ex

        def normalize(i):
            P_ = p[i % 2]
            if i in sums:
                soft[i] = self.do(dve, sums[i], lambda e: e.tensor_tensor(
                    st[:, i, 1, :], st[:, i, 1, :], st[:, i, 2, :], ALU.add))
            r = self.do(dve, [soft[i]], lambda e: e.reciprocal(st[:, i, 1, :], st[:, i, 1, :]))
            for qt in range(TT):
                nrm = self.do(dve, [r], lambda e: e.tensor_scalar(
                    P_[:, qt, :], P_[:, qt, :], st[:, i, 1, qt:qt + 1], None, ALU.mult))
            soft[i] = nrm

        def turn(i):
            b = 6 + i % 2
            self.after(pe, self.bank_free[b], soft[i])
            for qt in range(TT):
                for kt in range(TT):
                    mm = nc.tensor.transpose(self.bank[b][:, kt * T + qt * P:kt * T + (qt + 1) * P],
                                             p[i % 2][:, qt, kt * P:(kt + 1) * P], self.const("identity"))
            t = self.done(pe, mm)
            p_free[i % 2] = t
            ptr[i] = self.do(act, [t, pT_free[i % 2]], lambda e: e.activation(
                pT[i % 2][:, :, :], self.bank[b][:, :].rearrange("p (k q) -> p k q", k=TT), ACT.Copy))
            self.bank_free[b] = ptr[i]

        def weigh(i):
            nonlocal last_flush
            hd = heads[i]
            b, rows, parts = hd["out"]
            self.after(pe, self.bank_free[b], ptr[i])
            for j in range(parts):
                for kt in range(TT):
                    mm = nc.tensor.matmul(self.bank[b][rows, j * T:(j + 1) * T], hd["v"](kt, j), pT[i % 2][:, kt, :],
                                          start=(kt == 0), stop=(kt == TT - 1), skip_group_check=True)
            o = self.done(pe, mm)
            pT_free[i % 2] = o
            if hd["flush"]:
                t0, cnt = hd["flush"]
                src = self.bank[b][:, 0:cnt * T].rearrange("p (j t) -> p j t", j=cnt)
                last_flush = self.split_from_psum(src, cat_hi[:, t0:t0 + cnt, :], cat_lo[:, t0:t0 + cnt, :], o)
                self.bank_free[b] = last_flush

        for i in range(n + 2):
            if i < n:
                scores(i)
            if 1 <= i <= n:
                normalize(i - 1)
                turn(i - 1)
            if i >= 2:
                weigh(i - 2)
        self.att_free = last_flush
        return [last_flush] * 4

    def ab_stream(self):
        w, wo = self.a["ab_w_in_2"][0], self.a["ab_w_out_2"][0]
        return self.square_stream([(w, c) for c in (0, 512, 1024)] + [(wo, 0), (wo, 512)])

    def mixer_ab(self, st, free):
        g, nc = self.ab, self.nc
        dve, act, pool, pe = self.dve, self.act, self.pool, self.pe
        proj = g["proj"]

        def project(b):
            banks = [(0, 1), (2, 3)][b % 2]
            d = self.block_token_major(st, banks, self.x_hi, self.x_lo, self.x_ready)
            for tt in range(TT):
                pr = self.do(act, [d[tt], free], lambda e: e.activation(
                    proj[:, tt, b * 512:(b + 1) * 512], self.bank[banks[tt]][:, :], ACT.Copy))
                self.bank_free[banks[tt]] = pr
            return pr

        project(0)
        first_two = project(1)
        NH = 10
        tmp = self.xhat
        turned = None
        bank = 0
        tiles_ready = None
        for kind in range(2):
            src = proj[:, :, kind * 768:kind * 768 + NH * HD]
            heads = src.rearrange("p t (h d) -> p t h d", h=NH)
            ready = pr if kind else first_two
            if kind == 0:
                rs = self.small3[:, 0:TT * NH]
                for tt in range(TT):
                    sq = self.do(act, [ready, self.xhat_free], lambda e: e.activation(tmp[:, tt, 0:NH * HD], src[:, tt, :], ACT.Square))
                    ms = self.do(dve, [sq], lambda e: e.tensor_reduce(
                        rs[:, tt * NH:(tt + 1) * NH], tmp[:, tt, 0:NH * HD].rearrange("p (h d) -> p h d", h=NH), AX.X, ALU.add))
                me = self.do(dve, [ms], lambda e: e.tensor_scalar(rs, rs, 1.0 / HD, RMS_EPS, ALU.mult, ALU.add))
                rr = self.do(pool, [me], lambda e: e.tensor_tensor(rs, rs, self.minus_half[:, 0:TT * NH], ALU.pow))
                for tt in range(TT):
                    sc = self.do(dve, [rr], lambda e: e.tensor_tensor(
                        heads[:, tt, :, :], heads[:, tt, :, :],
                        rs[:, tt * NH:(tt + 1) * NH].unsqueeze(2).to_broadcast([P, NH, HD]), ALU.mult))
                    for part, (h0, h1) in enumerate(((0, 8), (8, 10))):
                        ready = self.do(dve, [sc, self.small_loaded], lambda e: e.tensor_tensor(
                            heads[:, tt, h0:h1, :], heads[:, tt, h0:h1, :],
                            self.gains[:, part, :].unsqueeze(1).to_broadcast([P, h1 - h0, HD]), ALU.mult))
            name = "2d" if kind == 0 else "1d"
            H2 = HD // 2
            rot = g["rot"]
            rot_done = None
            for tt in range(TT):
                cos = self.const(f"cos_{name}")[:, tt * H2:(tt + 1) * H2].unsqueeze(1).to_broadcast([P, NH, H2])
                sin = self.const(f"sin_{name}")[:, tt * H2:(tt + 1) * H2].unsqueeze(1).to_broadcast([P, NH, H2])
                x1, x2 = heads[:, tt, :, 0:H2], heads[:, tt, :, H2:HD]
                t = [tmp[:, tt, i * 320:(i + 1) * 320].rearrange("p (h d) -> p h d", h=NH) for i in range(3)]
                waits = [ready, self.xhat_free, turned]
                a1 = self.do(dve, waits, lambda e: e.tensor_tensor(t[0], x1, cos, ALU.mult))
                a2 = self.do(dve, waits, lambda e: e.tensor_tensor(t[1], x2, sin, ALU.mult))
                a3 = self.do(pool, waits, lambda e: e.tensor_tensor(t[2], x2, cos, ALU.mult))
                a4 = self.do(pool, [a1, a3], lambda e: e.tensor_tensor(x1, x1, sin, ALU.mult))
                for o0, o1, h0, h1 in ((0, 8, 0, 8), (8, 10, 8, 9), (10, 12, 9, 10)):
                    dup = o1 - o0 != h1 - h0
                    bc = (lambda ap: ap.to_broadcast([P, 2, H2])) if dup else (lambda ap: ap)
                    r1 = self.do(dve, [a1, a2], lambda e: e.tensor_tensor(
                        rot[:, tt, o0:o1, 0:H2], bc(t[0][:, h0:h1, :]), bc(t[1][:, h0:h1, :]), ALU.subtract))
                    r2 = self.do(dve, [a3, a4], lambda e: e.tensor_tensor(
                        rot[:, tt, o0:o1, H2:HD], bc(t[2][:, h0:h1, :]), bc(x1[:, h0:h1, :]), ALU.add))
                rot_done = r2
            if kind == 0:
                pr = project(2)
            for tile in range(6):
                b = 4 + tile % 4
                self.after(pe, self.bank_free[b], rot_done)
                for tt in range(TT):
                    mm = nc.tensor.transpose(self.bank[b][:, tt * P:(tt + 1) * P],
                                             rot[:, tt, 2 * tile:2 * tile + 2, :].rearrange("p h d -> p (h d)"),
                                             self.const("identity"))
                turned = self.done(pe, mm)
                dst = g["qT_ab"][:, kind * 4 + tile, :] if tile < 4 else g["kT_ab"][:, kind * 2 + tile - 4, :]
                tiles_ready = self.do(act, [turned], lambda e: e.activation(dst, self.bank[b][:, 0:T], ACT.Copy))
                self.bank_free[b] = tiles_ready
        self.xhat_free = [a4, r2]
        heads = []
        window = self.const("window").rearrange("p (q k) -> p q k", q=TT)
        for kind in range(2):
            for h in range(8):
                rows = slice((h % 2) * HD, (h % 2 + 1) * HD)
                kv = h // 4
                voff = kind * 768 + 640 + kv * HD
                tile = kind * 4 + h // 2
                heads.append(dict(
                    terms=[(g["qT_ab"][rows, tile, :], g["kT_ab"][rows, kind * 2 + kv, :])],
                    v=lambda kt, j, voff=voff: proj[:, kt, voff:voff + HD],
                    bias=(lambda qt: window[:, qt, :].unsqueeze(1)) if kind else None, bias_ready=None,
                    sink=self.sink[:, h:h + 1] if kind else None,
                    out=(tile % 2, rows, 1), flush=(tile, 1) if h % 2 else None, ready=[tiles_ready, rot_done, r2]))
        ready = self.attention(heads, HD ** -0.5, [g["p0_ab"], g["p1_ab"]], [g["pT0_ab"], g["pT1_ab"]],
                               g["cat_hi_ab"], g["cat_lo_ab"])
        return g["cat_hi_ab"], g["cat_lo_ab"], ready

    def c_stream(self):
        w, wo = self.a["c_w_in_2"][0], self.a["c_w_out_2"][0]
        return self.square_stream([(w, c) for c in range(0, 3 * D, 512)] + [(wo, 0), (wo, 512)])

    def qkv_blocks(self, st, which, hi, lo, ready, free, base):
        g = self.qkv
        for half in range(2):
            banks = [(0, 1), (2, 3)][(base + half) % 2]
            if which == "v_att":
                d = self.block_token_major(st, banks, hi, lo, ready)
            else:
                d = [self.block_transposed(st, banks, hi, lo, ready)] * 2
            for b in range(2):
                if which == "v_att":
                    dst, src = g[which][:, b, half * 512:(half + 1) * 512], self.bank[banks[b]][:, :]
                else:
                    dst = g[which][:, half * 4 + 2 * b:half * 4 + 2 * b + 2, :]
                    src = self.bank[banks[b]][:, :].rearrange("p (m t) -> p m t", m=2)
                r = self.do(self.act, [d[b], free], lambda e: e.activation(dst, src, ACT.Copy))
                self.bank_free[banks[b]] = r
        return r

    def mixer_c(self, st, free):
        g = self.qkv
        bias = g["bias"]
        rpb = self.a["c_rpb_2"]
        n_dr, n_dc = 2 * NA_KH - 1, 2 * NA_KW - 1
        for ro in range(2):
            for h in range(C_HEADS):
                off = h * n_dr * n_dc + (NA_KH - 1 - 2 - ro) * n_dc + NA_KW - GRID_W
                src = bass.AP(rpb.tensor, off, [[1, GRID_W], [n_dc, BIAS_ROWS], [1, GRID_W]])
                bias_landed = self.load_small(bias[ro * GRID_W:(ro + 1) * GRID_W, h, :, :], src, [free])
        masked = []
        for h in range(C_HEADS):
            masked.append(self.do(self.pool, [bias_landed], lambda e: e.tensor_tensor(
                bias[:, h, :, :], bias[:, h, :, :],
                self.const("neighbours").unsqueeze(1).to_broadcast([P, BIAS_ROWS, GRID_W]), ALU.add)))
        self.qkv_blocks(st, "qT", self.x_hi, self.x_lo, self.x_ready, free, 0)
        self.qkv_blocks(st, "kT", self.x_hi, self.x_lo, self.x_ready, free, 0)
        ready = self.qkv_blocks(st, "v_att", self.x_hi, self.x_lo, self.x_ready, free, 0)
        heads = []
        for h in range(C_HEADS):
            rows = slice((h % 2) * HD, (h % 2 + 1) * HD)
            heads.append(dict(
                terms=[(g["qT"][rows, h // 2, :], g["kT"][rows, h // 2, :])],
                v=lambda kt, j, h=h: g["v_att"][:, kt, h * HD:(h + 1) * HD],
                bias=lambda qt, h=h: bias[:, h, 2 - 2 * qt:2 - 2 * qt + ROWS, ::-1],
                bias_ready=masked[h], sink=None, out=((h // 2) % 2, rows, 1),
                flush=(h // 2, 1) if h % 2 else None, ready=ready))
        r = self.attention(heads, HD ** -0.5, [g["p0"], g["p1"]], [g["pT0"], g["pT1"]], g["cat_hi_qkv"], g["cat_lo_qkv"])
        return g["cat_hi_qkv"], g["cat_lo_qkv"], r

    def mem_stream(self, layer):
        wq, wkv, wo = self.a["mem_w_q_2"][layer], self.a["mem_w_kv_2"][layer], self.a["mem_w_o_2"][layer]
        return self.square_stream([(wkv, c) for c in range(0, 2 * D, 512)] + [(wq, 0), (wq, 512), (wo, 0), (wo, 512)])

    def memory_parts(self, free):
        m = self.mem_row
        landed = self.load_small(m[:, :, :], self.a["mem_2"][0].rearrange("(t p) d -> p t d", p=P), [free])
        ready = [None] * 4
        for tt in range(TT):
            for half in range(2):
                n = 2 * tt + half
                turned = self.transpose_block(m, tt, half, 4 + n, landed)
                ready[n] = self.split_from_psum(
                    self.bank[4 + n][:, :].rearrange("p (k t) -> p k t", k=4),
                    self.mem_hi[:, half * 4:half * 4 + 4, tt * P:(tt + 1) * P],
                    self.mem_lo[:, half * 4:half * 4 + 4, tt * P:(tt + 1) * P], turned, [free])
                self.bank_free[4 + n] = ready[n]
        return ready

    def memory_attn(self, layer, st, free, mem_ready):
        g = self.qkv
        self.qkv_blocks(st, "kT", self.mem_hi, self.mem_lo, mem_ready, free, 0)
        self.qkv_blocks(st, "v_att", self.mem_hi, self.mem_lo, mem_ready, free, 0)
        ready = self.qkv_blocks(st, "qT", self.x_hi, self.x_lo, self.x_ready, free, 0)
        dm = D // MEM_HEADS
        heads = []
        for h in range(MEM_HEADS):
            heads.append(dict(
                terms=[(g["qT"][:, 2 * h + j, :], g["kT"][:, 2 * h + j, :]) for j in range(2)],
                v=lambda kt, j, h=h: g["v_att"][:, kt, h * dm + j * P:h * dm + (j + 1) * P],
                bias=None, bias_ready=None, sink=None, out=(h % 2, slice(0, P), 2), flush=(2 * h, 2), ready=ready))
        r = self.attention(heads, dm ** -0.5, [g["p0"], g["p1"]], [g["pT0"], g["pT1"]], g["cat_hi_qkv"], g["cat_lo_qkv"])
        return g["cat_hi_qkv"], g["cat_lo_qkv"], r

    def router(self, acc_free):
        a, nc, dve, act, pe = self.a, self.nc, self.dve, self.act, self.pe
        E = N_EXP
        r_raw, r_hi, r_lo = self.router_raw, self.router_hi, self.router_lo
        landed = self.load_small(r_raw[:, :, :], a["router_w"][0].rearrange("(k p) e -> p k e", p=P), [self.small_free])
        h = self.do(act, [landed], lambda e: e.activation(r_hi[:, :, :], r_raw[:, :, :], ACT.Copy))
        lo = self.do(dve, [h], lambda e: e.tensor_tensor(r_lo[:, :, :], r_raw[:, :, :], r_hi[:, :, :].bitcast(F32), ALU.subtract))
        self.after(pe, lo, self.x_ready, self.bank_free[4])
        for tt in range(TT):
            for k in range(KT):
                mm = self.product(self.bank[4][:, tt * E:(tt + 1) * E], self.x_hi[:, k, tt * P:(tt + 1) * P],
                                  self.x_lo[:, k, tt * P:(tt + 1) * P], r_hi[:, k, :], r_lo[:, k, :],
                                  start=(k == 0 and tt == 0), stop=(k == KT - 1))
        l_done = self.done(pe, mm)
        sm = self.small
        logit = sm[:, 128:128 + TT * E].rearrange("p (t e) -> p t e", t=TT)
        rank = sm[:, 144:144 + TT * E].rearrange("p (t e) -> p t e", t=TT)
        first = sm[:, 160:160 + TT * E].rearrange("p (t e) -> p t e", t=TT)
        top = sm[:, 176:180]
        w2 = sm[:, 180:182]
        cmp_ = sm[:, 192:256].rearrange("p (e j) -> p e j", j=E)
        eq = sm[:, 256:320].rearrange("p (e j) -> p e j", j=E)
        prod = sm[:, 320:320 + TT * E].rearrange("p (t e) -> p t e", t=TT)
        t = self.do(dve, [l_done], lambda e: e.tensor_copy(logit, self.bank[4][:, 0:TT * E].rearrange("p (t e) -> p t e", t=TT)))
        self.bank_free[4] = t
        earlier = self.const("earlier_expert").rearrange("p (e j) -> p e j", j=E)
        for tt in range(TT):
            own = logit[:, tt, :].unsqueeze(2).to_broadcast([P, E, E])
            other = logit[:, tt, :].unsqueeze(1).to_broadcast([P, E, E])
            a1 = self.do(dve, [t], lambda e: e.tensor_tensor(cmp_, other, own, ALU.is_gt))
            a2 = self.do(dve, [t], lambda e: e.tensor_tensor(eq, other, own, ALU.is_equal))
            a3 = self.do(dve, [a2], lambda e: e.tensor_tensor(eq, eq, earlier, ALU.mult))
            a4 = self.do(dve, [a1, a3], lambda e: e.tensor_tensor(cmp_, cmp_, eq, ALU.add))
            t = self.do(dve, [a4], lambda e: e.tensor_reduce(rank[:, tt, :], cmp_, AX.X, ALU.add))
        for i in range(2):
            s = self.do(dve, [t], lambda e: e.tensor_scalar(first, rank, float(i), None, ALU.is_equal))
            s = self.do(dve, [s], lambda e: e.tensor_tensor(prod, first, logit, ALU.mult))
            t = self.do(dve, [s], lambda e: e.tensor_reduce(top[:, 2 * i:2 * i + 2], prod, AX.X, ALU.add))
        d = self.do(dve, [t], lambda e: e.tensor_tensor(top[:, 2:4], top[:, 2:4], top[:, 0:2], ALU.subtract))
        ex = self.do(act, [d], lambda e: e.activation(w2, top[:, 2:4], ACT.Exp))
        d = self.do(dve, [ex], lambda e: e.tensor_scalar(top[:, 0:2], w2, 1.0, None, ALU.add))
        d = self.do(dve, [d], lambda e: e.reciprocal(top[:, 0:2], top[:, 0:2]))
        d = self.do(dve, [d], lambda e: e.tensor_tensor(top[:, 2:4], w2, top[:, 0:2], ALU.mult))
        s1 = self.do(dve, [d], lambda e: e.tensor_scalar(first, rank, 0.0, None, ALU.is_equal))
        s2 = self.do(dve, [d], lambda e: e.tensor_scalar(prod, rank, 1.0, None, ALU.is_equal))
        for tt in range(TT):
            m = self.do(dve, [s1], lambda e: e.tensor_scalar(first[:, tt, :], first[:, tt, :], top[:, tt:tt + 1], None, ALU.mult))
            g = self.do(dve, [m, s2], lambda e: e.scalar_tensor_tensor(
                out=self.gates[:, tt, :], in0=prod[:, tt, :], scalar=top[:, 2 + tt:3 + tt], in1=first[:, tt, :],
                op0=ALU.mult, op1=ALU.add))
        c = self.do(dve, [d], lambda e: e.tensor_scalar(self.chosen[:, :, :], rank, 2.0, None, ALU.is_lt))
        return [g, c]

    def expert_weights(self, e):
        one = lambda w: (lambda r, c: w[bass.ds(e, 1), r, c].rearrange("o k n -> (o k) n"))
        return tuple(one(self.a[n][0]) for n in ("exp_w_gate", "exp_w_up", "exp_w_down"))

    def plan_slots(self, routed):
        dve, pool, pe, nc = self.dve, self.pool, self.pe, self.nc
        strict, ones = self.before_me[:, 0, :], self.before_me[:, 1, :]
        o = self.do(pool, [routed], lambda e: e.memset(self.before_me[:, :, :], 1.0))
        m = self.do(pool, [o], lambda e: e.affine_select(
            out=strict, in_=strict, compare_op=ALU.is_gt, fill=0.0, base=0, pattern=[[1, P]], channel_multiplier=-1))
        E = N_EXP
        self.after(pe, m, routed, self.bank_free[4])
        out = self.bank[4]
        nc.tensor.matmul(out[:, 0:E], strict, self.chosen[:, 0, :], start=True, stop=True, skip_group_check=True)
        for base, last in ((E, strict), (2 * E, ones)):
            nc.tensor.matmul(out[:, base:base + E], ones, self.chosen[:, 0, :], start=True, stop=False, skip_group_check=True)
            mm = nc.tensor.matmul(out[:, base:base + E], last, self.chosen[:, 1, :], start=False, stop=True, skip_group_check=True)
        counted = self.done(pe, mm)
        far = self.do(dve, [counted], lambda e: e.tensor_scalar(
            self.place[:, :, :], self.chosen[:, :, :], -1000.0, 1000.0, ALU.mult, ALU.add))
        placed = self.do(dve, [far], lambda e: e.tensor_tensor(
            self.place[:, :, :], self.place[:, :, :], out[:, 0:2 * E].rearrange("p (t e) -> p t e", t=TT), ALU.add))
        big = self.do(dve, [counted], lambda e: e.tensor_reduce(self.biggest[:, :], out[:, 2 * E:3 * E], AX.X, ALU.max))
        flag = self.do(dve, [big], lambda e: e.tensor_scalar(self.overflow[:, :], self.biggest[:, :], float(P), None, ALU.is_gt))
        self.bank_free[4] = flag
        self.h_free = [counted, counted]
        return placed, flag

    def build_pick(self, e_, waits):
        for tt in range(TT):
            picked = self.do(self.dve, waits, lambda e: e.tensor_scalar(
                self.pick[:, tt, :], self.const("slot_number"), self.place[:, tt, bass.ds(e_, 1)], None, ALU.is_equal))
        return picked

    def gather(self, e_, picked):
        pe, nc = self.pe, self.nc
        self.after(pe, picked, self.n_ready, self.bank_free[2], self.bank_free[3])
        for k in range(KT):
            out = self.bank[2 + k // 4][:, (k % 4) * P:(k % 4 + 1) * P]
            for tt in range(TT):
                for part in (self.n_hi, self.n_lo):
                    mm = nc.tensor.matmul(out, part[:, tt, k * P:(k + 1) * P], self.pick[:, tt, :],
                                          start=(k % 4 == 0 and tt == 0 and part is self.n_hi), stop=(tt == TT - 1),
                                          skip_group_check=True)
        got = self.done(pe, mm)
        self.after(pe, self.bank_free[6])
        for tt in range(TT):
            mm = nc.tensor.matmul(self.bank[6][:, 0:1], self.pick[:, tt, :].bitcast(F32),
                                  self.gates[:, tt, bass.ds(e_, 1)], start=(tt == 0), stop=(tt == TT - 1), skip_group_check=True)
        gate_got = self.done(pe, mm)
        self.pick_free = gate_got
        (gt, gc), (bt, bc) = self.x_affine_of
        for k in range(KT):
            scaled = self.do(self.act, [got, self.xe_all_free], lambda e: e.activation(
                self.xe_all[:, k, :], self.bank[2 + k // 4][:, (k % 4) * P:(k % 4 + 1) * P], ACT.Identity,
                bias=self.cols[:, bt, bc + k:bc + k + 1], scale=self.cols[:, gt, gc + k:gc + k + 1]))
        self.bank_free[2] = self.bank_free[3] = scaled
        return scaled, gate_got

    def switch_input(self, gathered, last_up, last_h):
        scaled, gate_got = gathered
        for half in range(2):
            ks = slice(half * 4, half * 4 + 4)
            h = self.do(self.act, [scaled, last_up], lambda e: e.activation(self.xe_hi[:, ks, :], self.xe_all[:, ks, :], ACT.Copy))
            lo = self.do(self.dve, [h, last_up], lambda e: e.tensor_tensor(
                self.xe_lo[:, ks, :], self.xe_all[:, ks, :], self.xe_hi[:, ks, :].bitcast(F32), ALU.subtract))
        self.xe_all_free = lo
        g = self.do(self.dve, [gate_got, last_h], lambda e: e.tensor_copy(self.slot_gate[:, :], self.bank[6][:, 0:1]))
        self.bank_free[6] = g
        self.xe_ready, self.gate_ready = lo, g

    def e_up(self, par, slots):
        pe, bank = self.pe, 4 + par
        self.after(pe, self.bank_free[bank], self.xe_ready)
        for kh in range(2):
            s, split = slots[kh]
            self.after(pe, split)
            for k in range(4):
                kk = kh * 4 + k
                mm = self.product(self.bank[bank][:, :], self.xe_hi[:, kk, :], self.xe_lo[:, kk, :],
                                  self.part_hi[s][:, k * 512:(k + 1) * 512], self.part_lo[s][:, k * 512:(k + 1) * 512],
                                  start=(kk == 0), stop=(kk == KT - 1))
            token = self.done(pe, mm)
            self.release(s, token)
        return token

    def e_act(self, par, up_done):
        bank = self.bank[4 + par]
        act = self.do(self.act, [up_done, self.h_free[par]], lambda e: e.activation(
            self.silu[par][:, :], bank[:, 0:FC], ACT.Silu))
        h = self.do(self.dve, [act, up_done, self.hT_turned[par], self.gate_ready], lambda e: e.scalar_tensor_tensor(
            out=self.h[par][:, :], in0=self.silu[par][:, :], scalar=self.slot_gate[:, 0:1],
            in1=bank[:, FC:2 * FC], op0=ALU.mult, op1=ALU.mult))
        self.bank_free[4 + par] = self.h_free[par] = h
        return h

    def e_turn(self, par, h_ready):
        bank = 6 + par
        self.after(self.pe, h_ready, self.bank_free[bank])
        for j in range(2):
            mm = self.nc.tensor.transpose(self.bank[bank][:, j * P:(j + 1) * P],
                                          self.h[par][:, j * P:(j + 1) * P], self.const("identity"))
        self.hT_turned[par] = turned = self.done(self.pe, mm)
        ready = self.split_from_psum(self.bank[bank][:, 0:FC].rearrange("p (j t) -> p j t", j=2),
                                     self.hT_hi[par][0][:, :, :], self.hT_lo[par][0][:, :, :], turned,
                                     [self.hT_used[par][0]])
        self.bank_free[bank] = ready
        return ready

    def e_down(self, par, down, start=False):
        (s, split), hT_ready = down
        self.after(self.pe, split, hT_ready)
        for j in range(2):
            for half in range(2):
                if start and j == 0:
                    self.after(self.pe, self.bank_free[half])
                cols = slice(j * D + half * 512, j * D + (half + 1) * 512)
                mm = self.product(self.bank[half][:, :], self.hT_hi[par][0][:, j, :], self.hT_lo[par][0][:, j, :],
                                  self.part_hi[s][:, cols], self.part_lo[s][:, cols], start=(start and j == 0))
        token = self.done(self.pe, mm)
        self.hT_used[par][0] = token
        self.release(s, token)
        return token

    def split_y(self, y_done):
        for half in range(2):
            self.y_ready[half] = self.split_from_psum(self.bank[half][:, :], self.y_hi[half][:, :], self.y_lo[half][:, :],
                                                      y_done, [self.y_free[half], self.xe_all_free])
            self.bank_free[half] = self.y_ready[half]

    def turn_pick(self, e_):
        pe, nc = self.pe, self.nc
        picked = self.build_pick(e_, [self.pick_free])
        self.after(pe, picked, self.bank_free[7])
        for tt in range(TT):
            mm = nc.tensor.transpose(self.bank[7][:, tt * P:(tt + 1) * P], self.pick[:, tt, :].bitcast(F32), self.const("identity"))
        turned = self.done(pe, mm)
        self.pick_free = turned
        pT = self.do(self.act, [turned, self.pickT_free], lambda e: e.activation(
            self.pickT[:, :, :], self.bank[7][:, 0:TT * P].rearrange("p (t s) -> p t s", t=TT), ACT.Copy))
        self.bank_free[7] = self.pickT_ready = pT

    def scatter(self):
        pe, nc = self.pe, self.nc
        self.after(pe, self.pickT_ready)
        for half in range(2):
            self.after(pe, self.y_ready[half])
            for tt in range(TT):
                self.after(pe, self.bank_free[2 + tt])
                nc.tensor.matmul(self.bank[2 + tt][:, :], self.pickT[:, tt, :], self.y_hi[half][:, :], start=True, stop=False, skip_group_check=True)
                mm = nc.tensor.matmul(self.bank[2 + tt][:, :], self.pickT[:, tt, :], self.y_lo[half][:, :], start=False, stop=True, skip_group_check=True)
                back = self.done(pe, mm)
                part = self.total[:, tt, half * 512:(half + 1) * 512]
                self.total_ready[tt] = self.do(self.dve, [back, self.total_ready[tt]], lambda e: e.tensor_tensor(
                    part, part, self.bank[2 + tt][:, :], ALU.add))
                self.bank_free[2 + tt] = self.total_ready[tt]
            self.y_free[half] = back
        self.pickT_free = back
        self.xe_all_free = [self.xe_all_free, back]

    def experts(self, n_chunks, up_slots):
        st = {"up": up_slots}

        def phase(c, par, e_, first=False, last=False, begin_down=False, between=None):
            gate, up, down = self.expert_weights(e_)
            seam = last and st["next"] is not None
            if c is not None and not last:
                nxt = [self.load_and_split(x, RING) for x in self.ffn_loads_up(gate, up, (c + 1) * FC)]
            elif st["next"] is not None:
                w = self.expert_weights(st["next"])
                nxt = [self.load_and_split(x, RING) for x in self.ffn_loads_up(w[0], w[1], 0)]
            else:
                nxt = None
            if seam:
                picked = self.build_pick(st["next"], [self.pick_free])
            up_done = self.e_up(par, st["up"])
            h = self.e_act(par, up_done)
            down_slot = self.load_and_split(self.ffn_load_down(down, c * FC), RING)
            if between:
                between()
            if seam:
                gathered = self.gather(st["next"], picked)
            if not first:
                self.e_down(1 - par, st["down"], start=begin_down)
            st["down"] = (down_slot, self.e_turn(par, h))
            if seam:
                self.switch_input(gathered, up_done, h)
            st["up"] = nxt

        def expert(e_, last=False):
            st["next"] = None if last else e_ + 1
            units = (n_chunks - 2) // 2
            assert n_chunks == 2 * units + 2
            before = dict(self.c.count)
            phase(1, 1, e_, begin_down=True)
            phase(2, 0, e_)
            with self.c.repeat(before, units) as i:
                phase(i * 2 + 1, 1, e_)
                phase(i * 2 + 2, 0, e_)
            phase(n_chunks - 1, 1, e_, last=True)
            y_done = self.e_down(1, st["down"])
            self.turn_pick(e_)
            self.split_y(y_done)
            if not last:
                phase(0, 0, e_ + 1, first=True, between=self.scatter)
            else:
                self.scatter()

        self.switch_input(self.gather(0, self.build_pick(0, [self.pick_free])), None, None)
        st["next"] = None
        phase(0, 0, 0, first=True)
        before = dict(self.c.count)
        expert(0)
        with self.c.repeat(before, N_EXP - 1) as e_:
            expert(e_)
        expert(N_EXP - 1, last=True)

    def moe(self, up_slots, n_chunks):
        nc = self.nc
        routed = self.router(None)
        placed, flag = self.plan_slots(routed)
        old_x = self.residual(0)
        self.after(self.dve, self.xhat_free)
        for tt in range(TT):
            for half in range(2):
                cols = slice(half * 512, (half + 1) * 512)
                src = self.xhat[:, tt, cols]
                h = self.do(self.act, [old_x, self.xhat_ready[tt, half]], lambda e: e.activation(self.n_hi[:, tt, cols], src, ACT.Copy))
                self.n_ready = self.do(self.dve, [h, old_x], lambda e: e.tensor_tensor(
                    self.n_lo[:, tt, cols], src, self.n_hi[:, tt, cols].bitcast(F32), ALU.subtract))
        self.total_ready = [None] * TT
        for tt in range(TT):
            for half in range(2):
                cols = slice(half * 512, (half + 1) * 512)
                self.total_ready[tt] = self.do(self.act, [old_x, self.n_ready, self.xhat_free], lambda e: e.activation(
                    self.total[:, tt, cols], self.acc(tt, half)[:, :], ACT.Copy))
                self.bank_free[2 * tt + half] = self.total_ready[tt]
        self.after(self.dve, placed, routed)
        self.pick_free = self.pickT_free = flag
        self.y_free = [None, None]
        self.y_ready = [None, None]
        self.xe_all_free = self.x_ready[3]
        self.experts(n_chunks, up_slots)

        for eng in (self.pe, self.act, self.dve, self.pool, self.sp):
            self.after(eng, flag)
        more = nc.values_load(self.overflow[0:1, 0:1], min_val=0, max_val=1,
                              skip_runtime_bounds_check_because="written by is_gt")
        saved = self.save_state()
        with nc.If(more > 0):
            engines = (self.pe, self.act, self.dve, self.pool)
            everything = [self.total_ready, self.pickT_free, self.raw_free, self.part_free, self.bank_free]
            for eng in (*engines, self.sp):
                self.after(eng, everything)
            for eng, sem in zip(engines, self.second_sems):
                eng.sem = sem
            self.landed_sem = self.second_landed
            moved = self.do(self.dve, [], lambda e: e.tensor_scalar(
                self.place[:, :, :], self.place[:, :, :], float(P), None, ALU.subtract))
            self.after(self.dve, moved)
            g, u, _ = self.expert_weights(0)
            self.experts(n_chunks, [self.load_and_split(x, RING) for x in self.ffn_loads_up(g, u, 0)])
            for eng in (*engines, self.sp):
                self.after(eng, self.total_ready, self.pickT_free, self.raw_free, self.part_free, self.bank_free)
        self.restore_state(saved)
        self.small_free = self.pickT_free
        return self.total_ready

    def save_state(self):
        return (list(self.raw_free), list(self.part_free), list(self.bank_free), list(self.h_free),
                list(self.hT_turned), [list(x) for x in self.hT_used], list(self.total_ready),
                self.raw_at, self.part_at, self.pickT_free, self.landed_sem,
                [e.sem for e in (self.pe, self.act, self.dve, self.pool)], dict(self.c.waited))

    def restore_state(self, saved):
        (self.raw_free, self.part_free, self.bank_free, self.h_free, self.hT_turned, self.hT_used, self.total_ready,
         self.raw_at, self.part_at, self.pickT_free, self.landed_sem, sems, self.c.waited) = saved
        for e, sem in zip((self.pe, self.act, self.dve, self.pool), sems):
            e.sem = sem

    def build(self):
        a = self.a
        self.small_free = self.small2_free = self.vstats_free = self.att_free = None
        self.start()
        dense = lambda w: (lambda r, c: w[r, c])
        stages = []
        for layer in range(DEPTH):
            mix_ln = [(t, c + layer * KT) for t, c in (self.col_of["ln_mix_g"], self.col_of["ln_mix_b"])]
            ffn_ln = [(t, c + layer * KT) for t, c in (self.col_of["ln_ffn_g"], self.col_of["ln_ffn_b"])]
            stages.append(("gla", layer, mix_ln))
            stages.append(("ffn" if layer % 2 == 0 else "moe", layer // 2, ffn_ln))
        for layer in range(DEPTH):
            ln = lambda s: [(t, c + (layer * 4 + s) * KT) for t, c in (self.col_of["ln_g_2"], self.col_of["ln_b_2"])]
            stages.append(("ffn2", (layer, 0), ln(0)))
            stages.append(("ab" if layer % 2 == 0 else "c", layer, ln(1)))
            stages.append(("mem", layer, ln(2)))
            stages.append(("ffn2", (layer, 1), ln(3)))
        if self.stop is not None:
            stages = stages[self.stop[0]:self.stop[1]]

        def weights(kind, which):
            if kind == "ffn":
                return tuple(dense(a[n][which]) for n in ("ffn_w_gate", "ffn_w_up", "ffn_w_down"))
            if kind == "ffn2":
                return tuple(dense(a[n][which[0], which[1]]) for n in ("ffn_w_gate_2", "ffn_w_up_2", "ffn_w_down_2"))
            return self.expert_weights(0)

        def prefetch(kind, which):
            if kind in ("ffn", "ffn2", "moe"):
                return self.ffn_prefetch(weights(kind, which))
            st = {"gla": lambda: self.gla_stream(which), "ab": self.ab_stream, "c": self.c_stream,
                  "mem": lambda: self.mem_stream(which)}[kind]()
            self.stream_step(st)
            self.stream_step(st)
            return st

        ahead = prefetch(*stages[0][:2])
        free = None
        for n, (kind, which, (g, b)) in enumerate(stages):
            eps = LN_EPS
            if kind in ("ffn", "moe", "ffn2"):
                scale = 1 if kind == "ffn2" else 0
                if kind == "ffn2":
                    eps = 4 * LN_EPS
                if n == 0:
                    self.start_columns()
                if kind != "moe":
                    self.residual(scale)
                if kind == "moe":
                    done = self.moe(ahead, D_FFE // FC)
                else:
                    done, _ = self.ffn(weights(kind, which), D_FF // FC, ahead)
            else:
                if n == 0 and kind != "gla":
                    self.start_columns()
                if kind == "gla":
                    cat = self.hybrid_mixer(which, ahead, free)
                elif kind == "ab":
                    cat = self.mixer_ab(ahead, free)
                elif kind == "c":
                    cat = self.mixer_c(ahead, free)
                else:
                    cat = self.memory_attn(which, ahead, free, self.memory_parts(free))
                done = self.out_projection(ahead, *cat)
            free = done[1]
            last = n == len(stages) - 1
            if not last:
                ahead = prefetch(*stages[n + 1][:2])
            source = (lambda tt, half: self.total[:, tt, half * 512:(half + 1) * 512]) if kind == "moe" else None
            normed = self.layer_norm(done, g, b, eps, final=last, source=source)
        layer, s = (DEPTH - 1, 3)
        gd, bd = self.final_gb
        self.store_final(normed, gd, bd)


def build_program(nc, args, out, stop=None, final=None):
    p = Program(nc, args, out, stop)
    p.final_gb = final(args) if final else (args["ln_g_2"][DEPTH - 1, 3], args["ln_b_2"][DEPTH - 1, 3])
    p.build()


_INS = ["x", "w_in", "gm_ws", "gm_bs", "gm_ln_g", "gm_ln_b", "gla_wa2", "gla_ba", "gla_norm_g", "w_out", "ln_mix_g",
        "ln_mix_b", "ffn_w_gate", "ffn_w_up", "ffn_w_down", "router_w", "exp_w_gate", "exp_w_up", "exp_w_down",
        "ln_ffn_g", "ln_ffn_b", "mem_2", "ln_g_2", "ln_b_2", "ffn_w_gate_2", "ffn_w_up_2", "ffn_w_down_2",
        "ab_w_in_2", "ab_w_out_2", "ab_q_gain_2", "ab_k_gain_2", "ab_sink_2", "c_w_in_2", "c_w_out_2", "c_rpb_2",
        "mem_w_q_2", "mem_w_kv_2", "mem_w_o_2"]


def kernel(**inputs):
    import concourse.bacc as _bacc
    from concourse.bass_utils import run_bass_kernel_spmd as _run

    nc = _bacc.Bacc("TRN2", target_bir_lowering=False, num_devices=1)
    arrays, args = {}, {}
    for name in _INS + ["consts"]:
        if name == "consts":
            a = CONST_ARRAY
        elif name == "c_rpb_2":
            a = np.ascontiguousarray(np.asarray(inputs[name])[..., ::-1])
        else:
            a = np.ascontiguousarray(inputs[name])
        arrays[f"in_{name}_dram"] = a
        args[name] = nc.dram_tensor(f"in_{name}_dram", a.shape, mybir.dt.from_np(a.dtype), kind="ExternalInput").ap()
    out = nc.dram_tensor("out_dram", (1, T, D), F32, kind="ExternalOutput").ap()
    build_program(nc, args, out)
    r = _run(nc, [arrays], core_ids=[0])
    return r.results[0]["out_dram"]
```

```python
from contextlib import contextmanager

import numpy as np

import concourse.bass as bass
from concourse import mybir

P = 128
F32 = mybir.dt.float32
F32R = mybir.dt.float32r
ALU = mybir.AluOpType
ACT = mybir.ActivationFunctionType
AX = mybir.AxisListType

T = 256
TT = T // P
D = 1024
KT = D // P
DEPTH = 2
LN_EPS, RMS_EPS = 1e-5, 1e-6
ALPHA = (2.0 * DEPTH) ** 0.25

GM_HEADS, GM_DIM = 4, 128
GM_W = GM_HEADS * GM_DIM
GLA_HEADS, GLA_DV, GLA_DK, GLA_RANK, GLA_CHUNK = 4, 128, 64, 16, 64
GLA_W, GLA_KW = GLA_HEADS * GLA_DV, GLA_HEADS * GLA_DK
GLA_TAU = 16.0
NCH = T // GLA_CHUNK
D_FF, D_FFE, N_EXP = 2816, 3584, 8
FC = 256

HD = 64
GRID_W, NA_KH, NA_KW = 64, 8, 16
ROWS = T // GRID_W
C_HEADS = D // HD
MEM_HEADS = 4
BIAS_ROWS = ROWS + 2
NEG = -1e30
WINDOW = 128

RING = 6
MIX_PARTS = 3
SLOT = 2048

CONST = {}


def build_constants():
    cols = []

    def add(name, a):
        a = np.asarray(a, np.float32).reshape(P, -1)
        start = sum(c.shape[1] for c in cols)
        CONST[name] = (start, a.shape[1])
        cols.append(a)

    eye = np.eye(P, dtype=np.float32)
    add("identity", eye)
    add("alpha_identity", eye * np.float32(ALPHA))
    add("alpha2_identity", eye * np.float32(2 * np.float32(ALPHA)))
    q = np.arange(T).reshape(TT, P).T[:, :, None]
    add("window", np.where(np.abs(q - np.arange(T)) <= WINDOW, 0.0, NEG))
    w = np.arange(P)[:, None] % GRID_W
    first = np.clip(w - NA_KW // 2, 0, GRID_W - NA_KW)
    k = np.arange(GRID_W)[None]
    add("neighbours", np.where((k >= first) & (k < first + NA_KW), 0.0, NEG)[:, ::-1])
    t = np.arange(T)

    def angles(pos, dim):
        inv = np.float32(10000.0) ** (-np.arange(0, dim, 2, dtype=np.float32) / np.float32(dim))
        return pos.astype(np.float32)[:, None] * inv[None].astype(np.float32)

    ang_2d = np.concatenate([angles(t // GRID_W, HD // 2), angles(t % GRID_W, HD // 2)], axis=-1)
    for name, ang in (("2d", ang_2d), ("1d", angles(t, HD))):
        for f, fn in (("cos", np.cos), ("sin", np.sin)):
            add(f"{f}_{name}", fn(ang).reshape(TT, P, HD // 2).transpose(1, 0, 2))
    add("scan_keep", np.tile((np.arange(2 * T) % GLA_CHUNK != 0).astype(np.float32), (P, 1)))
    add("slot_number", np.tile(np.arange(P), (P, 1)))
    e = np.arange(N_EXP)
    add("earlier_expert", np.tile((e[None, :] < e[:, None]).astype(np.float32).reshape(1, -1), (P, 1)))
    return np.concatenate(cols, axis=1)


CONST_ARRAY = build_constants()


class Token:
    def __init__(self, sem, value, loops):
        self.sem, self.value, self.loops = sem, value, loops


class Loop:
    def __init__(self, per, var):
        self.per, self.var = per, var


class Counter:
    def __init__(self, nc):
        self.nc = nc
        self.count = {}
        self.tokens = []
        self.active = ()
        self.waited = {}

    def mark(self, ins, sem, amount=1):
        ins.then_inc(sem, amount)
        self.count[sem] = self.count.get(sem, 0) + amount
        token = Token(sem, self.count[sem], self.active)
        self.tokens.append(token)
        return token

    def after(self, eng, *tokens):
        for t in tokens:
            if t is None:
                continue
            if isinstance(t, (list, tuple)):
                self.after(eng, *t)
                continue
            key = (eng.name, t.sem, t.loops)
            if self.waited.get(key, 0) >= t.value:
                continue
            self.waited[key] = t.value
            value = t.value
            for loop in t.loops:
                assert loop in self.active
                if loop.per.get(t.sem, 0):
                    value = (loop.var - 1) * loop.per[t.sem] + value
            eng.eng.wait_ge(t.sem, value)

    @contextmanager
    def repeat(self, before, times):
        per = {s: n - before.get(s, 0) for s, n in self.count.items() if n != before.get(s, 0)}
        entry = dict(self.count)
        loop = Loop(per, None)
        for t in self.tokens:
            if t.value > before.get(t.sem, 0):
                t.loops = t.loops + (loop,)
        self.waited = {}
        with self.nc.Fori(1, times) as var:
            loop.var = var
            self.active = self.active + (loop,)
            yield var
            self.active = self.active[:-1]
        for s, n in self.count.items():
            assert n - entry.get(s, 0) == per.get(s, 0), "the body must repeat the hand-run one"
            self.count[s] = n + (times - 2) * per.get(s, 0)
        for t in self.tokens:
            if loop in t.loops:
                t.loops = tuple(x for x in t.loops if x is not loop)
                t.value += (times - 2) * per.get(t.sem, 0)
        self.waited = {}


class Engine:
    def __init__(self, name, eng, sem):
        self.name, self.eng, self.sem = name, eng, sem


class Stream:
    def __init__(self, loads, parts):
        self.loads, self.parts, self.ready, self.sent = loads, parts, [], 0


class Program:
    def __init__(self, nc, a, out, stop=None):
        self.nc, self.a, self.out, self.stop = nc, a, out, stop
        self.c = Counter(nc)
        self.pe = Engine("pe", nc.tensor, nc.alloc_semaphore("tensor_steps"))
        self.act = Engine("act", nc.scalar, nc.alloc_semaphore("scalar_steps"))
        self.dve = Engine("dve", nc.vector, nc.alloc_semaphore("vector_steps"))
        self.pool = Engine("pool", nc.gpsimd, nc.alloc_semaphore("gpsimd_steps"))
        self.sp = Engine("sp", nc.sync, None)
        self.landed_sem = [nc.alloc_semaphore(f"slot{i}_landed") for i in range(RING)]
        self.small_sem = nc.alloc_semaphore("small_loads")
        self.second_sems = [nc.alloc_semaphore(f"{n}_steps_second_pass") for n in ("tensor", "scalar", "vector", "gpsimd")]
        self.second_landed = [nc.alloc_semaphore(f"slot{i}_landed_second_pass") for i in range(RING)]
        self.x_sem = nc.alloc_semaphore("x_landed")
        self.const_sem = nc.alloc_semaphore("consts_landed")
        self.last_gb_sem = nc.alloc_semaphore("last_gain_landed")
        self.loads_sem = nc.alloc_semaphore("slots_requested")
        self.out_sem = nc.alloc_semaphore("stores")
        self.place_memory()

    def place_memory(self):
        nc = self.nc
        base = (nc.sbuf_base + 31) // 32 * 32
        at = [base]

        def put(name, shape, dt=F32, offset=None):
            words = int(np.prod(shape[1:]))
            if offset is None:
                offset = at[0]
                at[0] += (words * 4 + 31) // 32 * 32
            return nc.alloc_sbuf_tensor_at(name, shape, dt, offset=offset)

        self.raw = [put(f"raw{i}", [P, SLOT]) for i in range(RING)]
        x_at = at[0]
        self.x_hi = put("x_hi", [P, KT, T], F32R)
        self.x_lo = put("x_lo", [P, KT, T], F32R)
        xf_at = at[0]
        self.xf = [put(f"x_affine{i}", [P, 4, P]) for i in range(2)]
        xhat_at = at[0]
        self.xhat = put("xhat", [P, TT, D])
        self.consts = put("consts", [P, CONST_ARRAY.shape[1]])
        self.resid_hi = put("resid_hi", [P, 2 * P], F32R)
        self.resid_lo = put("resid_lo", [P, 2 * P], F32R)
        rows_at = at[0]
        self.rows = put("param_rows", [P, 2, P])
        self.cols = put("param_cols", [P, 2, P])
        self.stats = put("stats", [P, TT, 2, 6])
        self.mv = put("mean_var", [P, TT, 2])
        self.rstd = put("rstd", [P, TT])
        self.shift = put("minus_mean_times_rstd", [P, TT])
        self.minus_half = put("minus_half", [P, 32])
        small_at = at[0]
        self.small = put("small", [P, 512])
        xe_at = at[0]
        self.xe_hi = put("expert_in_hi", [P, KT, P], F32R)
        self.xe_lo = put("expert_in_lo", [P, KT, P], F32R)
        self.place = put("slot_of_token", [P, TT, N_EXP])
        self.chosen = put("chosen", [P, TT, N_EXP])
        self.slot_gate = put("slot_gate", [P, 1])
        self.overflow = put("overflow", [P, 1], mybir.dt.int32)
        self.biggest = put("largest_count", [P, 1])
        self.sink = put("sink", [P, 8])
        self.gains = put("gains", [P, 2, HD])
        self.gates = put("gates", [P, TT, N_EXP])
        self.small2 = put("chunk_spans", [P, 2, 6])
        self.small3 = put("inverse_norms", [P, 32])
        self.vstats = put("gating_stats", [P, TT, GM_HEADS, 8])
        self.att_stats = put("softmax_stats", [P, 16, 3, TT])
        self.part_hi = [None] * RING
        self.part_lo = [None] * RING
        for i in range(RING):
            if i == MIX_PARTS:
                arena = at[0]
            self.part_hi[i] = put(f"part_hi{i}", [P, SLOT], F32R)
            self.part_lo[i] = put(f"part_lo{i}", [P, SLOT], F32R)
        self.silu_at = at[0]
        self.silu = [put(f"silu{i}", [P, FC]) for i in range(2)]
        self.h = [put(f"h{i}", [P, FC]) for i in range(2)]
        self.hT_hi = [[None] * TT for _ in range(2)]
        self.hT_lo = [[None] * TT for _ in range(2)]
        for t in range(TT):
            if t == 1:
                y_at = at[0]
            for i in range(2):
                self.hT_hi[i][t] = put(f"hT_hi{i}{t}", [P, 2, P], F32R)
                self.hT_lo[i][t] = put(f"hT_lo{i}{t}", [P, 2, P], F32R)
        end = at[0]
        assert end <= nc.sbuf_usable_end, (end, nc.sbuf_usable_end)

        over = lambda name, shape, dt, offset: nc.alloc_sbuf_tensor_at(name, shape, dt, offset=offset)
        self.xe_all = over("expert_affine", [P, KT, P], F32, xf_at)
        self.y_hi = [over(f"y_hi{i}", [P, 512], F32R, o) for i, o in enumerate((y_at, xf_at))]
        self.y_lo = [over(f"y_lo{i}", [P, 512], F32R, o + 2048) for i, o in enumerate((y_at, xf_at))]
        self.n_hi = over("normed_hi", [P, TT, D], F32R, x_at)
        self.n_lo = over("normed_lo", [P, TT, D], F32R, x_at + 4 * TT * D)
        self.total = over("expert_sum", [P, TT, D], F32, xhat_at)
        self.pick = over("pick", [P, TT, 2 * P], F32R, small_at)
        self.pickT = over("pickT", [P, TT, P], F32R, rows_at)
        self.router_raw, self.router_hi, self.router_lo = (
            over(f"router_{n}", [P, KT, N_EXP], dt, xe_at + i * 4 * KT * N_EXP)
            for i, (n, dt) in enumerate((("raw", F32), ("hi", F32R), ("lo", F32R))))
        self.logitT = over("router_logits_transposed", [P, T], F32, xe_at + 3 * 4 * KT * N_EXP)
        self.before_me = over("tokens_before", [P, 2, P], F32, self.silu_at)
        self.overlay_at = {}

        def overlay(items):
            o = arena
            made = {}
            for name, shape, dt, over in items:
                words = int(np.prod(shape[1:]))
                if over is None:
                    made[name] = (nc.alloc_sbuf_tensor_at(name, shape, dt, offset=o), o)
                    o += (words * 4 + 31) // 32 * 32
                else:
                    made[name] = (nc.alloc_sbuf_tensor_at(name, shape, dt, offset=made[over][1]), made[over][1])
            assert o <= end, (o - arena, end - arena)
            self.overlay_at.update({k: v[1] for k, v in made.items()})
            return {k: v[0] for k, v in made.items()}

        self.gla = overlay([
            ("u", [P, TT, GM_W], F32, None), ("vg", [P, TT, GM_W], F32, None),
            ("v_gla", [P, TT, GLA_W], F32, None), ("silu_g", [P, TT, GLA_W], F32, None),
            ("q_heads", [P, 2, 2, T], F32, None), ("k_inv", [P, 2, T], F32, None),
            ("k_for_chunk", [P, NCH, 2, T], F32, None), ("scoresT", [P, TT, GLA_HEADS, T], F32, None),
            ("log_a", [P, 2, T], F32, None), ("tmp_a", [P, 2, T], F32, None),
            ("b_cum", [P, 2, T], F32, None), ("exp_b", [P, 2, T], F32, None),
            ("ws", [P, GM_HEADS, P], F32, None), ("wsT", [P, GM_HEADS, P], F32, None),
            ("gm_g", [P, GM_W], F32, None), ("gm_b", [P, GM_W], F32, None),
            ("a_raw", [P, KT, GLA_RANK], F32, None),
            ("a_hi", [P, KT, GLA_RANK], F32R, None), ("a_lo", [P, KT, GLA_RANK], F32R, None),
            ("wa2", [GLA_RANK, GLA_KW], F32, None),
            ("cat_hi_gla", [P, KT, T], F32R, "k_for_chunk"), ("cat_lo_gla", [P, KT, T], F32R, "scoresT"),
            ("norm_g", [P, GLA_W], F32, "ws"),
        ])
        self.qkv = overlay([
            ("qT", [P, KT, T], F32, None), ("kT", [P, KT, T], F32, None), ("v_att", [P, TT, D], F32, None),
            ("p0", [P, TT, T], F32, None), ("p1", [P, TT, T], F32, None),
            ("pT0", [P, TT, T], F32, None), ("pT1", [P, TT, T], F32, None),
            ("bias", [P, C_HEADS, BIAS_ROWS, GRID_W], F32, None),
            ("cat_hi_qkv", [P, KT, T], F32R, "qT"), ("cat_lo_qkv", [P, KT, T], F32R, "kT"),
        ])
        self.ab = overlay([
            ("qT_ab", [P, KT, T], F32, None), ("kT_ab", [P, 4, T], F32, None),
            ("spare", [P, 4, T], F32, None), ("proj", [P, TT, 1536], F32, None),
            ("p0_ab", [P, TT, T], F32, None), ("p1_ab", [P, TT, T], F32, None),
            ("pT0_ab", [P, TT, T], F32, None), ("pT1_ab", [P, TT, T], F32, None),
            ("rot", [P, TT, 12, HD], F32, None),
            ("cat_lo_ab", [P, KT, T], F32R, None),
            ("cat_hi_ab", [P, KT, T], F32R, "qT_ab"),
        ])
        self.mem_row, self.mem_hi, self.mem_lo = (
            nc.alloc_sbuf_tensor_at(name, [P, *shape], dt, offset=self.overlay_at["bias"] + i * D * TT * 4)
            for i, (name, shape, dt) in enumerate((("mem_row", (TT, D), F32), ("mem_hi", (KT, T), F32R), ("mem_lo", (KT, T), F32R))))
        self.bank = [nc.alloc_psum_tensor(f"bank{i}", [P, 512], F32) for i in range(8)]
        self.bank_free = [None] * 8
        self.raw_free = [None] * RING
        self.part_free = [None] * RING
        self.raw_at = self.part_at = 0
        self.x_ready = [None] * 4

    def const(self, name):
        start, n = CONST[name]
        return self.consts[:, start:start + n]

    def after(self, eng, *tokens):
        self.c.after(eng, *tokens)

    def done(self, eng, ins):
        return self.c.mark(ins, eng.sem)

    def do(self, eng, tokens, ins):
        self.c.after(eng, *tokens)
        return self.c.mark(ins(eng.eng), eng.sem)

    def product(self, out, stat_hi, stat_lo, move_hi, move_lo, start=False, stop=False):
        pe = self.nc.tensor
        pe.matmul(out, stat_hi, move_hi, start=start, stop=False, skip_group_check=True)
        pe.matmul(out, stat_hi, move_lo, start=False, stop=False, skip_group_check=True)
        return pe.matmul(out, stat_lo, move_hi, start=False, stop=stop, skip_group_check=True)

    def acc(self, tt, half):
        return self.bank[2 * tt + half]

    def load_and_split(self, loads, parts):
        r = self.raw_at % RING
        self.raw_at += 1
        if self.part_at >= parts:
            self.part_at = 0
        s = self.part_at
        self.part_at += 1
        raw, hi, lo = self.raw[r], self.part_hi[s], self.part_lo[s]
        self.after(self.sp, self.raw_free[r])
        if self.raw_free[r] is not None and self.raw_free[r].loops:
            self.nc.sync.sem_inc(self.loads_sem, 1)
        words = 0
        for view, src in loads:
            dst, words = view(raw)
            landed = self.c.mark(self.nc.sync.dma_start(dst, src), self.landed_sem[r], 16)
        rounded = self.do(self.act, [landed, self.part_free[s]],
                          lambda e: e.activation(hi[:, 0:words], raw[:, 0:words], ACT.Copy))
        split = self.do(self.dve, [landed, rounded, self.part_free[s]],
                        lambda e: e.tensor_tensor(lo[:, 0:words], raw[:, 0:words],
                                                  hi[:, 0:words].bitcast(F32), ALU.subtract))
        self.raw_free[r] = split
        return s, split

    def stream_step(self, st):
        if st.sent < len(st.loads):
            st.ready.append(self.load_and_split(st.loads[st.sent], st.parts))
            st.sent += 1

    def take(self, st):
        s, split = st.ready.pop(0)
        self.after(self.pe, split)
        return s

    def release(self, s, token):
        self.part_free[s] = token

    @staticmethod
    def square_loads(w, col, ncols=512):
        out = []
        for kh in range(2):
            src = w[kh * 512:(kh + 1) * 512, col:col + ncols].rearrange("(k p) n -> p k n", p=P)
            out.append([(lambda raw, n=ncols: (raw[:, 0:4 * n].rearrange("p (k n) -> p k n", k=4), 4 * n), src)])
        return out

    def square_stream(self, blocks):
        return Stream([x for w, col in blocks for x in self.square_loads(w, col)], MIX_PARTS)

    def block_token_major(self, st, banks, hi, lo, ready, start=True, ahead=True):
        pe = self.pe
        done = [None] * TT
        for kh in range(2):
            s = self.take(st)
            for tt in range(TT):
                if kh == 0:
                    self.after(pe, self.bank_free[banks[tt]])
                self.after(pe, ready[tt * 2 + kh])
                for k in range(4):
                    kk = kh * 4 + k
                    mm = self.product(self.bank[banks[tt]][:, :], hi[:, kk, tt * P:(tt + 1) * P],
                                      lo[:, kk, tt * P:(tt + 1) * P],
                                      self.part_hi[s][:, k * 512:(k + 1) * 512],
                                      self.part_lo[s][:, k * 512:(k + 1) * 512],
                                      start=(start and kk == 0), stop=(kk == KT - 1))
                if kh == 1 or tt == TT - 1:
                    done[tt] = self.done(pe, mm)
            self.release(s, done[TT - 1])
            self.stream_step(st)
        return done

    def block_transposed(self, st, banks, hi, lo, ready):
        pe = self.pe
        for kh in range(2):
            s = self.take(st)
            for b in range(2):
                if kh == 0:
                    self.after(pe, self.bank_free[banks[b]])
                self.after(pe, [ready[tt * 2 + kh] for tt in range(TT)])
                for m in (2 * b, 2 * b + 1):
                    for k in range(4):
                        kk = kh * 4 + k
                        w = slice(k * 512 + m * P, k * 512 + (m + 1) * P)
                        mm = self.product(self.bank[banks[b]][:, (m % 2) * T:(m % 2 + 1) * T],
                                          self.part_hi[s][:, w], self.part_lo[s][:, w],
                                          hi[:, kk, :], lo[:, kk, :],
                                          start=(kk == 0 and m % 2 == 0), stop=(kk == KT - 1))
            done = self.done(pe, mm)
            self.release(s, done)
            self.stream_step(st)
        return done

    def residual(self, banks):
        for b in banks:
            tt, half = divmod(b, 2)
            self.after(self.pe, self.bank_free[b], self.x_ready[b])
            for k in range(4):
                kk, n = half * 4 + k, 2 * P if k < 3 else P
                self.product(self.bank[b][:, k * P:k * P + n],
                             self.x_hi[:, kk, tt * P:(tt + 1) * P], self.x_lo[:, kk, tt * P:(tt + 1) * P],
                             self.resid_hi[:, 0:n], self.resid_lo[:, 0:n], start=(k == 0))
            self.acc_started.add(b)

    def out_projection(self, st, hi, lo, ready):
        self.residual([b for b in range(4) if b not in self.acc_started])
        self.acc_started = set()
        halves = [self.block_token_major(st, [half, 2 + half], hi, lo, ready, start=False) for half in range(2)]
        done = [[halves[0][tt], halves[1][tt]] for tt in range(TT)]
        for i in range(MIX_PARTS, RING):
            self.part_free[i] = done[1]
        return done

    def transpose_block(self, src, tt, half, bank, ready):
        self.after(self.pe, self.bank_free[bank], ready)
        for k in range(4):
            c = (half * 4 + k) * P
            mm = self.nc.tensor.transpose(self.bank[bank][:, k * P:(k + 1) * P], src[:, tt, c:c + P],
                                          self.const("identity"))
        return self.done(self.pe, mm)

    def split_from_psum(self, bank_ap, hi, lo, ready, waits=()):
        h = self.do(self.act, [ready, *waits], lambda e: e.activation(hi, bank_ap, ACT.Copy))
        return self.do(self.dve, [h, ready, *waits],
                       lambda e: e.tensor_tensor(lo, bank_ap, hi.bitcast(F32), ALU.subtract))

    def layer_norm(self, acc_done, g, b, eps, final=False, source=None, residual=None):
        src = source or (lambda tt, half: self.acc(tt, half)[:, :])
        normed = {}

        def statistics(tt):
            for half in range(2):
                st = self.do(self.dve, [acc_done[tt][half]], lambda e: e.bn_stats(self.stats[:, tt, half, :], src(tt, half)))
            agg = self.do(self.dve, [st], lambda e: e.bn_aggr(self.mv[:, tt, :], self.stats[:, tt, :, :]))
            eps_added = self.do(self.dve, [agg], lambda e: e.tensor_scalar(
                self.rstd[:, tt:tt + 1], self.mv[:, tt, 1:2], eps, None, ALU.add))
            return self.do(self.pool, [eps_added], lambda e: e.tensor_tensor(
                self.rstd[:, tt:tt + 1], self.rstd[:, tt:tt + 1], self.minus_half[:, 0:1], ALU.pow))

        def norm(tt, inv):
            shift = self.do(self.dve, [inv], lambda e: e.scalar_tensor_tensor(
                out=self.shift[:, tt:tt + 1], in0=self.mv[:, tt, 0:1], scalar=-1.0, in1=self.rstd[:, tt:tt + 1],
                op0=ALU.mult, op1=ALU.mult))
            for half in range(2):
                dst = self.xhat[:, tt, half * 512:(half + 1) * 512]
                if half == 0:
                    normed[tt, half] = self.do(self.dve, [inv, self.xhat_free], lambda e: e.tensor_scalar(
                        dst, src(tt, half), self.mv[:, tt, 0:1], self.rstd[:, tt:tt + 1], ALU.subtract, ALU.mult))
                else:
                    normed[tt, half] = self.do(self.act, [shift, acc_done[tt][half], self.xhat_free], lambda e: e.activation(
                        dst, src(tt, half), ACT.Identity, bias=self.shift[:, tt:tt + 1], scale=self.rstd[:, tt:tt + 1]))
                if source is None:
                    self.bank_free[2 * tt + half] = normed[tt, half]

        def turn_and_scale(tt):
            for half in range(2):
                n = 2 * tt + half
                bank = 4 + n
                xf = self.xf[n % 2]
                turned[n] = self.transpose_block(self.xhat, tt, half, bank, normed[tt, half])
                for k in range(4):
                    kk = half * 4 + k
                    scaled[n] = self.do(self.act, [turned[n], self.xf_free[n % 2]], lambda e: e.activation(
                        xf[:, k, :], self.bank[bank][:, k * P:(k + 1) * P], ACT.Identity,
                        bias=self.cols[:, b[0], b[1] + kk:b[1] + kk + 1],
                        scale=self.cols[:, g[0], g[1] + kk:g[1] + kk + 1]))
                self.bank_free[bank] = scaled[n]

        def split(n):
            tt, half = divmod(n, 2)
            xf = self.xf[n % 2]
            hi = self.x_hi[:, half * 4:half * 4 + 4, tt * P:(tt + 1) * P]
            lo = self.x_lo[:, half * 4:half * 4 + 4, tt * P:(tt + 1) * P]
            rounded = self.do(self.dve, [scaled[n], acc_done], lambda e: e.tensor_copy(hi, xf[:, :, :]))
            self.x_ready[n] = self.do(self.dve, [rounded], lambda e: e.tensor_tensor(
                lo, xf[:, :, :], hi.bitcast(F32), ALU.subtract))
            self.xf_free[n % 2] = [self.x_ready[n], started.get(n)]

        def start_acc(tt):
            if residual is not None:
                for n in (2 * tt, 2 * tt + 1):
                    self.after(self.pe, scaled[n], self.bank_free[n])
                    for k in range(4):
                        mm = self.nc.tensor.matmul(self.bank[n][:, k * P:(k + 1) * P], self.xf[n % 2][:, k, :],
                                                   self.const(residual), start=(k == 0), stop=False, skip_group_check=True)
                    started[n] = self.residual_done = self.done(self.pe, mm)

        turned, scaled, started = {}, {}, {}
        norm(0, statistics(0))
        if final:
            norm(1, statistics(1))
            return normed
        turn_and_scale(0)
        start_acc(0)
        second = statistics(1)
        split(0)
        norm(1, second)
        split(1)
        turn_and_scale(1)
        start_acc(1)
        split(2)
        split(3)
        turned = turned[3]
        self.xhat_free = turned
        self.x_affine_of, self.xhat_ready = (g, b), normed

    def store_final(self, normed, g_dram, b_dram):
        gb = [self.raw[0][:, 0:D], self.raw[1][:, 0:D]]
        self.after(self.sp, self.raw_free[0], self.raw_free[1])
        for dst, src in zip(gb, (g_dram, b_dram)):
            landed = self.c.mark(self.nc.sync.dma_start(dst, src.partition_broadcast(P)), self.last_gb_sem, 16)
        for tt in range(TT):
            for half in range(2):
                cols = slice(half * 512, (half + 1) * 512)
                x = self.xhat[:, tt, cols]
                m = self.do(self.dve, [normed[tt, half], landed],
                            lambda e: e.tensor_tensor(x, x, gb[0][:, cols], ALU.mult))
                s = self.do(self.dve, [m], lambda e: e.tensor_tensor(x, x, gb[1][:, cols], ALU.add))
                self.after(self.sp, s)
                stored = self.c.mark(self.nc.sync.dma_start(
                    self.out[0, tt * P:(tt + 1) * P, cols], x), self.out_sem, 16)
        self.after(self.sp, stored)

    def ffn_loads_up(self, w_gate, w_up, col):
        loads = []
        for kh in range(2):
            one = []
            for n, w in enumerate((w_gate, w_up)):
                src = w(slice(kh * 512, (kh + 1) * 512), bass.ds(col, FC)).rearrange("(k p) n -> p k n", p=P)
                one.append((lambda raw, n=n: (raw[:, :].rearrange("p (k m n) -> p k m n", k=4, m=2)[:, :, n, :], SLOT), src))
            loads.append(one)
        return loads

    def ffn_load_down(self, w_down, row):
        src = w_down(bass.ds(row, FC), slice(0, D)).rearrange("(j p) n -> p j n", p=P)
        return [(lambda raw: (raw[:, :].rearrange("p (j n) -> p j n", j=2), SLOT), src)]

    def ffn_up(self, tt, slots):
        bank = 4 + tt
        pe = self.pe
        self.after(pe, self.bank_free[bank])
        for kh in range(2):
            s, split = slots[kh]
            self.after(pe, split, self.x_ready[2 * tt + kh])
            for k in range(4):
                kk = kh * 4 + k
                mm = self.product(self.bank[bank][:, :], self.x_hi[:, kk, tt * P:(tt + 1) * P],
                                  self.x_lo[:, kk, tt * P:(tt + 1) * P],
                                  self.part_hi[s][:, k * 512:(k + 1) * 512],
                                  self.part_lo[s][:, k * 512:(k + 1) * 512],
                                  start=(kk == 0), stop=(kk == KT - 1))
            token = self.done(pe, mm)
            if tt == TT - 1:
                self.release(s, token)
        return token

    def ffn_act(self, tt, up_done):
        bank = 4 + tt
        act = self.do(self.act, [up_done, self.h_free[tt]], lambda e: e.activation(
            self.silu[tt][:, :], self.bank[bank][:, 0:FC], ACT.Silu))
        h = self.do(self.dve, [act, up_done, self.hT_turned[tt]], lambda e: e.tensor_tensor(
            self.h[tt][:, :], self.silu[tt][:, :], self.bank[bank][:, FC:2 * FC], ALU.mult))
        self.bank_free[bank] = h
        self.h_free[tt] = h
        return h

    def ffn_turn(self, tt, par, h_ready):
        bank = 6 + tt
        self.after(self.pe, h_ready, self.bank_free[bank])
        for j in range(2):
            mm = self.nc.tensor.transpose(self.bank[bank][:, j * P:(j + 1) * P],
                                          self.h[tt][:, j * P:(j + 1) * P], self.const("identity"))
        self.hT_turned[tt] = turned = self.done(self.pe, mm)
        hi, lo = self.hT_hi[par][tt][:, :, :], self.hT_lo[par][tt][:, :, :]
        src = self.bank[bank][:, 0:FC].rearrange("p (j t) -> p j t", j=2)
        ready = self.split_from_psum(src, hi, lo, turned, [self.hT_used[par][tt]])
        self.bank_free[bank] = ready
        return ready

    def ffn_down(self, tt, par, slot, hT_ready, start=False):
        s, split = slot
        self.after(self.pe, split, hT_ready)
        for j in range(2):
            for half in range(2):
                if start and j == 0:
                    self.after(self.pe, self.bank_free[2 * tt + half])
                mm = self.product(self.acc(tt, half)[:, :], self.hT_hi[par][tt][:, j, :], self.hT_lo[par][tt][:, j, :],
                                  self.part_hi[s][:, j * D + half * 512:j * D + (half + 1) * 512],
                                  self.part_lo[s][:, j * D + half * 512:j * D + (half + 1) * 512])
        token = self.done(self.pe, mm)
        self.hT_used[par][tt] = token
        if tt == TT - 1:
            self.release(s, token)
        return token

    def ffn_prefetch(self, w):
        return [self.load_and_split(x, RING) for x in self.ffn_loads_up(w[0], w[1], 0)]

    def ffn(self, weights, n_chunks, up_slots):
        w_gate, w_up, w_down = weights
        state = {"up": up_slots}

        def phase(c, par, first=False, last=False):
            slots = state["up"]
            nxt = None
            if not last:
                nxt = [self.load_and_split(x, RING) for x in self.ffn_loads_up(w_gate, w_up, (c + 1) * FC)]
            up0 = self.ffn_up(0, slots)
            h0 = self.ffn_act(0, up0)
            down_slot = self.load_and_split(self.ffn_load_down(w_down, c * FC), RING)
            up1 = self.ffn_up(1, slots)
            h1 = self.ffn_act(1, up1)
            t0 = self.ffn_turn(0, par, h0)
            acc = None
            if not first:
                prev = state["down"]
                for tt in range(TT):
                    self.ffn_down(tt, 1 - par, prev[0], prev[1][tt])
            t1 = self.ffn_turn(1, par, h1)
            state["down"] = (down_slot, [t0, t1])
            state["up"] = nxt

        phase(0, 0, first=True)
        units = (n_chunks - 2) // 2
        before = dict(self.c.count)
        phase(1, 1)
        phase(2, 0)
        with self.c.repeat(before, units) as i:
            phase(i * 2 + 1, 1)
            phase(i * 2 + 2, 0)
        for c in range(1 + 2 * units, n_chunks):
            phase(c, c % 2, last=(c == n_chunks - 1))
        par = (n_chunks - 1) % 2
        slot, turned = state["down"]
        return [self.ffn_down(tt, par, slot, turned[tt]) for tt in range(TT)]

    def load_small(self, dst, src, waits=()):
        self.after(self.pool, *waits)
        return self.c.mark(self.nc.gpsimd.dma_start(dst, src), self.small_sem, 16)

    def start(self):
        a, nc = self.a, self.nc
        self.xhat_free = None
        self.xf_free = [None, None]
        self.h_free = [None] * TT
        self.hT_turned = [None] * TT
        self.hT_used = [[None] * TT for _ in range(2)]
        x_landed = self.c.mark(nc.sync.dma_start(self.xhat[:, :, :], a["x"][0].rearrange("(t p) d -> p t d", p=P)),
                               self.x_sem, 16)
        c_landed = self.c.mark(nc.sync.dma_start(self.consts[:, :], a["consts"]), self.const_sem, 16)
        zeroed = self.do(self.pool, [], lambda e: e.memset(self.rows[:, :, :], 0.0))
        halves = self.do(self.pool, [], lambda e: e.memset(self.minus_half[:, :], -0.5))
        self.after(self.pool, zeroed, halves)
        at = 0
        self.col_of = {}
        for name, n in (("ln_mix_g", 16), ("ln_mix_b", 16), ("ln_ffn_g", 16), ("ln_ffn_b", 16), ("gm_bs", 8), ("gla_ba", 4)):
            src = a[name]
            src = src.rearrange("l h t -> (l h) t") if name == "gm_bs" else src.rearrange("l (k p) -> (l k) p", p=P)
            self.load_small(self.rows[at:at + n, 0, :], src)
            self.col_of[name] = (0, at)
            at += n
        for i, name in enumerate(("ln_g_2", "ln_b_2")):
            self.load_small(self.rows[i * 64:(i + 1) * 64, 1, :], a[name].rearrange("l s (k p) -> (l s k) p", p=P))
            self.col_of[name] = (1, i * 64)
        self.load_small(self.sink[:, :], a["ab_sink_2"][0].partition_broadcast(P))
        self.load_small(self.gains[:, 0, :], a["ab_q_gain_2"][0].partition_broadcast(P))
        rows_landed = self.load_small(self.gains[:, 1, :], a["ab_k_gain_2"][0].partition_broadcast(P))
        self.small_loaded = rows_landed
        self.columns_made = False
        self.after(self.dve, c_landed)
        self.after(self.pe, c_landed)
        self.to_xT(self.xhat, [x_landed] * 2)
        alpha = self.const("alpha_identity")
        h = self.do(self.act, [c_landed], lambda e: e.activation(self.resid_hi[:, 0:P], alpha, ACT.Copy))
        lo = self.do(self.dve, [h], lambda e: e.tensor_tensor(
            self.resid_lo[:, 0:P], alpha, self.resid_hi[:, 0:P].bitcast(F32), ALU.subtract))
        for part in (self.resid_hi, self.resid_lo):
            zero = self.do(self.dve, [], lambda e: e.tensor_scalar(part[:, P:2 * P], alpha, 0.0, None, ALU.mult))
        self.after(self.pe, lo, zero)

    def start_columns(self):
        self.columns_made = True
        self.after(self.pe, self.small_loaded, self.bank_free[7])
        for i in range(2):
            mm = self.nc.tensor.transpose(self.bank[7][:, i * P:(i + 1) * P], self.rows[:, i, :], self.const("identity"))
        turned = self.done(self.pe, mm)
        ready = self.bank_free[7] = self.do(self.dve, [turned], lambda e: e.tensor_copy(
            self.cols[:, :, :], self.bank[7][:, 0:2 * P].rearrange("p (i c) -> p i c", i=2)))
        for eng in (self.dve, self.act, self.pool):
            self.after(eng, ready)

    def to_xT(self, src, ready):
        for tt in range(TT):
            for half in range(2):
                n = 2 * tt + half
                turned = self.transpose_block(src, tt, half, 4 + n, ready[tt])
                hi = self.x_hi[:, half * 4:half * 4 + 4, tt * P:(tt + 1) * P]
                lo = self.x_lo[:, half * 4:half * 4 + 4, tt * P:(tt + 1) * P]
                self.x_ready[n] = self.split_from_psum(
                    self.bank[4 + n][:, :].rearrange("p (k t) -> p k t", k=4), hi, lo, turned)
                self.bank_free[4 + n] = self.x_ready[n]
        self.xhat_free = turned

    def gla_stream(self, layer):
        w = self.a["w_in"][layer]
        cols = [1024, 0, 512, 1536, 2048]
        w_out = self.a["w_out"][layer]
        return self.square_stream([(w, c) for c in cols] + [(w_out, 0), (w_out, 512)])

    def hybrid_mixer(self, layer, st, free):
        a, g, nc = self.a, self.gla, self.nc
        dve, act, pool, pe = self.dve, self.act, self.pool, self.pe
        self.load_small(g["a_raw"][:, :, :], a["w_in"][layer][:, 2560:2576].rearrange("(k p) n -> p k n", p=P), [free])
        self.load_small(g["wa2"][:, :], a["gla_wa2"][layer])
        self.load_small(g["ws"][:, :, :], a["gm_ws"][layer].rearrange("h t s -> t h s"))
        self.load_small(g["gm_g"][:, :], a["gm_ln_g"][layer].partition_broadcast(P))
        loaded = self.load_small(g["gm_b"][:, :], a["gm_ln_b"][layer].partition_broadcast(P))
        k_zero = self.do(pool, [free], lambda e: e.memset(g["k_for_chunk"][:, :, :, :], 0.0))
        q_zero = self.do(pool, [free], lambda e: e.memset(g["q_heads"][:, :, :, :], 0.0))
        masked = self.do(pool, [loaded], lambda e: e.affine_select(
            out=g["ws"][:, :, :], in_=g["ws"][:, :, :], compare_op=ALU.is_ge, fill=0.0, base=0,
            pattern=[[0, GM_HEADS], [-1, P]], channel_multiplier=1))
        qk_done = self.block_transposed(st, [0, 1], self.x_hi, self.x_lo, self.x_ready)
        a_hi = self.do(act, [loaded], lambda e: e.activation(g["a_hi"][:, :, :], g["a_raw"][:, :, :], ACT.Copy))
        a_lo = self.do(dve, [a_hi], lambda e: e.tensor_tensor(
            g["a_lo"][:, :, :], g["a_raw"][:, :, :], g["a_hi"][:, :, :].bitcast(F32), ALU.subtract))
        self.after(pe, a_lo, self.x_ready, self.bank_free[4])
        for k in range(KT):
            mm = self.product(self.bank[4][0:GLA_RANK, 0:T], g["a_hi"][:, k, :], g["a_lo"][:, k, :],
                              self.x_hi[:, k, :], self.x_lo[:, k, :], start=(k == 0), stop=(k == KT - 1))
        a_done = self.done(pe, mm)
        alrT = self.small[0:GLA_RANK, 0:T]
        alrT_ready = self.do(dve, [a_done, self.small_free], lambda e: e.tensor_copy(alrT, self.bank[4][0:GLA_RANK, 0:T]))
        self.bank_free[4] = alrT_ready
        if not self.columns_made:
            self.start_columns()
        self.after(pe, alrT_ready, self.bank_free[6])
        for dt in range(2):
            mm = nc.tensor.matmul(self.bank[6][:, dt * T:(dt + 1) * T], g["wa2"][:, dt * P:(dt + 1) * P], alrT,
                                  start=True, stop=True, skip_group_check=True)
        z_done = self.done(pe, mm)
        self.small_free = z_done
        log_a, tmp, b_cum, exp_b = g["log_a"], g["tmp_a"], g["b_cum"], g["exp_b"]
        ba_t, ba_c = self.col_of["gla_ba"]
        for dt in range(2):
            c = ba_c + 2 * layer + dt
            z = self.do(dve, [z_done, free], lambda e: e.tensor_scalar(
                log_a[:, dt, :], self.bank[6][:, dt * T:(dt + 1) * T], self.cols[:, ba_t, c:c + 1], None, ALU.add))
        self.bank_free[6] = z
        ab = self.do(act, [z], lambda e: e.activation(tmp[:, :, :], log_a[:, :, :], ACT.Abs))
        ex = self.do(act, [ab], lambda e: e.activation(tmp[:, :, :], tmp[:, :, :], ACT.Exp, scale=-1.0))
        ln = self.do(act, [ex], lambda e: e.activation(tmp[:, :, :], tmp[:, :, :], ACT.Ln, bias=1.0))
        mn = self.do(dve, [z, ab], lambda e: e.tensor_scalar(log_a[:, :, :], log_a[:, :, :], 0.0, None, ALU.min))
        la = self.do(dve, [mn, ln], lambda e: e.tensor_tensor(log_a[:, :, :], log_a[:, :, :], tmp[:, :, :], ALU.subtract))
        flat = lambda t: t[:, :, :].rearrange("p d t -> p (d t)")
        scan = self.do(dve, [la], lambda e: e.tensor_tensor_scan(
            flat(b_cum), self.const("scan_keep"), flat(log_a), 0.0, ALU.mult, ALU.add))
        inv = 1.0 / GLA_TAU
        eb = self.do(act, [scan], lambda e: e.activation(exp_b[:, :, :], b_cum[:, :, :], ACT.Exp, scale=inv))
        enb = self.do(act, [scan, la], lambda e: e.activation(tmp[:, :, :], b_cum[:, :, :], ACT.Exp, scale=-inv))
        tot = b_cum[:, :, :].rearrange("p d (c j) -> p d c j", j=GLA_CHUNK)[:, :, :, GLA_CHUNK - 1]
        span = self.small2
        sp1 = self.do(dve, [scan, self.small2_free], lambda e: e.tensor_copy(span[:, :, 0:1], tot[:, :, 0:1]))
        self.do(dve, [], lambda e: e.tensor_copy(span[:, :, 2:3], tot[:, :, 1:2]))
        sp2 = self.do(dve, [], lambda e: e.tensor_copy(span[:, :, 5:6], tot[:, :, 2:3]))
        sp3 = self.do(dve, [sp1, sp2], lambda e: e.tensor_tensor(span[:, :, 1:2], span[:, :, 0:1], tot[:, :, 1:2], ALU.add))
        sp4 = self.do(dve, [sp2], lambda e: e.tensor_tensor(span[:, :, 4:5], span[:, :, 2:3], tot[:, :, 2:3], ALU.add))
        sp5 = self.do(dve, [sp3], lambda e: e.tensor_tensor(span[:, :, 3:4], span[:, :, 1:2], tot[:, :, 2:3], ALU.add))
        es = self.do(act, [sp4, sp5], lambda e: e.activation(span[:, :, :], span[:, :, :], ACT.Exp, scale=inv))
        for dt in range(2):
            for hh in range(2):
                rows = slice(hh * HD, (hh + 1) * HD)
                q_ready = self.do(dve, [eb, qk_done, q_zero], lambda e: e.scalar_tensor_tensor(
                    out=g["q_heads"][rows, dt, hh, :], in0=self.bank[0][rows, dt * T:(dt + 1) * T],
                    scalar=GLA_DK ** -0.5, in1=exp_b[rows, dt, :], op0=ALU.mult, op1=ALU.mult))
        k_inv = self.do(dve, [enb], lambda e: e.tensor_tensor(
            g["k_inv"][:, :, :], self.bank[1][:, :].rearrange("p (d t) -> p d t", d=2), tmp[:, :, :], ALU.mult))
        self.bank_free[0] = self.bank_free[1] = k_inv
        kc = g["k_for_chunk"]
        for c in range(NCH):
            cs = slice(c * GLA_CHUNK, (c + 1) * GLA_CHUNK)
            k_ready = self.do(dve, [k_inv, k_zero], lambda e: e.tensor_copy(kc[:, c, :, cs], g["k_inv"][:, :, cs]))
            if c:
                o = (0, 0, 1, 3)[c]
                for dt in range(2):
                    k_ready = self.do(dve, [es], lambda e: e.tensor_tensor(
                        kc[:, c, dt, 0:c * GLA_CHUNK].rearrange("p (c j) -> p c j", j=GLA_CHUNK),
                        g["k_inv"][:, dt, 0:c * GLA_CHUNK].rearrange("p (c j) -> p c j", j=GLA_CHUNK),
                        span[:, dt, o:o + c].unsqueeze(2).to_broadcast([P, c, GLA_CHUNK]), ALU.mult))
        self.small2_free = k_ready
        u_done = self.block_token_major(st, [2, 3], self.x_hi, self.x_lo, self.x_ready)
        for tt in range(TT):
            u_ready = self.do(act, [u_done[tt], free], lambda e: e.activation(g["u"][:, tt, :], self.bank[2 + tt][:, :], ACT.Gelu))
            self.bank_free[2 + tt] = u_ready
        vg_done = self.block_token_major(st, [0, 1], self.x_hi, self.x_lo, self.x_ready)
        for tt in range(TT):
            vg_ready = self.do(act, [vg_done[tt]], lambda e: e.activation(g["vg"][:, tt, :], self.bank[tt][:, :], ACT.Gelu))
            self.bank_free[tt] = vg_ready
        q_heads = g["q_heads"]
        self.after(pe, k_ready, q_ready, [self.bank_free[b] for b in range(4, 8)])
        for jt in range(TT):
            for dt in range(2):
                out = self.bank[4 + 2 * jt + dt][:, :].rearrange("p (h i) -> p h i", h=2)
                for c in range(2 * jt, NCH):
                    i = slice(c * GLA_CHUNK, (c + 1) * GLA_CHUNK)
                    mm = nc.tensor.matmul(out[:, :, i], kc[:, c, dt, jt * P:(jt + 1) * P], q_heads[:, dt, :, i],
                                          start=True, stop=True, skip_group_check=True)
        s_done = self.done(pe, mm)
        sT = g["scoresT"]
        for jt in range(TT):
            for dt in range(2):
                i = slice(jt * P, T)
                src = self.bank[4 + 2 * jt + dt][:, :].rearrange("p (h i) -> p h i", h=2)
                s_copied = self.do(act, [s_done], lambda e: e.activation(sT[:, jt, 2 * dt:2 * dt + 2, i], src[:, :, i], ACT.Copy))
                self.bank_free[4 + 2 * jt + dt] = s_copied
            s_masked = self.do(pool, [s_copied], lambda e: e.affine_select(
                out=sT[:, jt, :, jt * P:(jt + 1) * P], in_=sT[:, jt, :, jt * P:(jt + 1) * P], compare_op=ALU.is_ge,
                fill=0.0, base=0, pattern=[[0, GLA_HEADS], [1, P]], channel_multiplier=-1))
        vst = self.vstats
        for tt in range(TT):
            for h in range(GM_HEADS):
                bst = self.do(dve, [vg_ready, self.vstats_free], lambda e: e.bn_stats(
                    vst[:, tt, h, 0:6], g["vg"][:, tt, h * P:(h + 1) * P]))
        for tt in range(TT):
            for h in range(GM_HEADS):
                agg = self.do(dve, [bst], lambda e: e.bn_aggr(vst[:, tt, h, 6:8], vst[:, tt, h, 0:6]))
        rs = self.small3[:, 0:8].rearrange("p (t h) -> p t h", t=TT)
        add_eps = self.do(dve, [agg], lambda e: e.tensor_scalar(rs, vst[:, :, :, 7], LN_EPS, None, ALU.add))
        r_ready = self.do(pool, [add_eps], lambda e: e.tensor_tensor(
            self.small3[:, 0:8], self.small3[:, 0:8], self.minus_half[:, 0:8], ALU.pow))
        for tt in range(TT):
            for h in range(GM_HEADS):
                cols = slice(h * P, (h + 1) * P)
                vn = self.do(dve, [r_ready], lambda e: e.tensor_scalar(
                    g["vg"][:, tt, cols], g["vg"][:, tt, cols], vst[:, tt, h, 6:7],
                    rs[:, tt, h:h + 1], ALU.subtract, ALU.mult))
        self.vstats_free = vn
        for tt in range(TT):
            vm = self.do(pool, [vn, loaded], lambda e: e.tensor_tensor(g["vg"][:, tt, :], g["vg"][:, tt, :], g["gm_g"][:, :], ALU.mult))
            v_ln = self.do(pool, [vm], lambda e: e.tensor_tensor(g["vg"][:, tt, :], g["vg"][:, tt, :], g["gm_b"][:, :], ALU.add))
        v_done = self.block_token_major(st, [2, 3], self.x_hi, self.x_lo, self.x_ready)
        for tt in range(TT):
            v_ready = self.do(act, [v_done[tt]], lambda e: e.activation(g["v_gla"][:, tt, :], self.bank[2 + tt][:, :], ACT.Copy))
            self.bank_free[2 + tt] = v_ready
        self.after(pe, masked, self.bank_free[4])
        for h in range(GM_HEADS):
            mm = nc.tensor.transpose(self.bank[4][:, h * P:(h + 1) * P], g["ws"][:, h, :], self.const("identity"))
        w_turned = self.done(pe, mm)
        w_ready = self.do(act, [w_turned], lambda e: e.activation(
            g["wsT"][:, :, :], self.bank[4][:, :].rearrange("p (h t) -> p h t", h=GM_HEADS), ACT.Copy))
        self.bank_free[4] = w_ready
        ng_loaded = self.load_small(g["norm_g"][:, :], a["gla_norm_g"][layer].partition_broadcast(P), [w_turned])
        g_done = self.block_token_major(st, [0, 1], self.x_hi, self.x_lo, self.x_ready)
        for tt in range(TT):
            g_ready = self.do(act, [g_done[tt]], lambda e: e.activation(g["silu_g"][:, tt, :], self.bank[tt][:, :], ACT.Silu))
            self.bank_free[tt] = g_ready
        for tt in range(TT):
            gg = self.do(pool, [g_ready, ng_loaded], lambda e: e.tensor_tensor(
                g["silu_g"][:, tt, :], g["silu_g"][:, tt, :], g["norm_g"][:, :], ALU.mult))
        self.after(pe, v_ready, s_masked, self.bank_free[6], self.bank_free[7])
        for tt in range(TT):
            for h in range(GLA_HEADS):
                for jt in range(tt + 1):
                    mm = nc.tensor.matmul(self.bank[6 + tt][:, h * P:(h + 1) * P], sT[:, jt, h, tt * P:(tt + 1) * P],
                                          g["v_gla"][:, jt, h * P:(h + 1) * P], start=(jt == 0), stop=(jt == tt),
                                          skip_group_check=True)
        o_done = self.done(pe, mm)
        self.after(pe, w_ready, v_ln, self.bank_free[4], self.bank_free[5])
        for tt in range(TT):
            for h in range(GM_HEADS):
                mm = nc.tensor.matmul(self.bank[4 + tt][:, h * P:(h + 1) * P], g["wsT"][:, h, :],
                                      g["vg"][:, tt, h * P:(h + 1) * P], start=True, stop=True, skip_group_check=True)
        sg_done = self.done(pe, mm)
        self.residual([0, 1])
        cat = self.xhat
        for tt in range(TT):
            sq = self.do(act, [o_done, self.xhat_free], lambda e: e.activation(cat[:, tt, 512:1024], self.bank[6 + tt][:, :], ACT.Square))
            ms = self.do(dve, [sq, vn], lambda e: e.tensor_reduce(
                rs[:, tt, :], cat[:, tt, 512:1024].rearrange("p (h e) -> p h e", h=GLA_HEADS), AX.X, ALU.add))
        me = self.do(dve, [ms], lambda e: e.tensor_scalar(rs, rs, 1.0 / GLA_DV, RMS_EPS, ALU.mult, ALU.add))
        rr = self.do(pool, [me], lambda e: e.tensor_tensor(
            self.small3[:, 0:8], self.small3[:, 0:8], self.minus_half[:, 0:8], ALU.pow))
        bs_t, bs_c = self.col_of["gm_bs"]
        hi, lo = g["cat_hi_gla"], g["cat_lo_gla"]
        ready = [None] * 4
        order = ((0, 0), (0, 1), (1, 0), (1, 1))
        cat_of, turned = {}, {}
        for half, tt in order:
            for h in range(GLA_HEADS):
                cols = slice(h * P, (h + 1) * P)
                if half:
                    cat_ready = self.do(dve, [rr, gg], lambda e: e.scalar_tensor_tensor(
                        out=cat[:, tt, 512 + h * P:512 + (h + 1) * P], in0=self.bank[6 + tt][:, cols],
                        scalar=rs[:, tt, h:h + 1], in1=g["silu_g"][:, tt, cols], op0=ALU.mult, op1=ALU.mult))
                else:
                    c = bs_c + layer * GM_HEADS + h
                    cat_ready = self.do(dve, [sg_done, u_ready, self.xhat_free], lambda e: e.scalar_tensor_tensor(
                        out=cat[:, tt, cols], in0=self.bank[4 + tt][:, cols], scalar=self.cols[:, bs_t, c:c + 1],
                        in1=g["u"][:, tt, cols], op0=ALU.add, op1=ALU.mult))
            self.bank_free[4 + 2 * half + tt] = cat_of[half, tt] = cat_ready
        for half, tt in order:
            turned[half, tt] = self.transpose_block(cat, tt, half, 4 + 2 * half + tt, cat_of[half, tt])
        self.residual([2, 3])
        for half, tt in order:
            b, n = 4 + 2 * half + tt, 2 * tt + half
            ready[n] = self.bank_free[b] = self.split_from_psum(
                self.bank[b][:, :].rearrange("p (k t) -> p k t", k=4),
                hi[:, half * 4:half * 4 + 4, tt * P:(tt + 1) * P], lo[:, half * 4:half * 4 + 4, tt * P:(tt + 1) * P],
                turned[half, tt])
        self.xhat_free = turned[order[-1]]
        return hi, lo, ready

    def attention(self, heads, scale, p, pT, cat_hi, cat_lo, meanwhile=()):
        dve, act, pe, nc = self.dve, self.act, self.pe, self.nc
        n = len(heads)
        st = self.att_stats
        ptr, soft, sums, weighed = {}, {}, {}, {}
        last_flush = None
        p = [*p, self.xf[0][:, :, :].rearrange("p (q h) k -> p q (h k)", q=TT)]
        p_free, pT_free = [None, None, self.xf_free[0]], [None, None]

        def scores(i):
            hd, b = heads[i], 4 + i % 2
            self.after(pe, self.bank_free[b], hd["ready"])
            for qt in range(TT):
                for j, (q, k) in enumerate(hd["terms"]):
                    mm = nc.tensor.matmul(self.bank[b][:, qt * T:(qt + 1) * T], q[:, qt * P:(qt + 1) * P], k,
                                          start=(j == 0), stop=(j == len(hd["terms"]) - 1), skip_group_check=True)
            s_done = self.done(pe, mm)
            P_ = p[i % 3]
            top = st[:, i, 0, :]
            if hd["bias"] is None:
                src = self.bank[b][:, :].rearrange("p (q k) -> p q k", q=TT)
                m = self.do(dve, [s_done, self.att_free], lambda e: e.tensor_reduce(top, src, AX.X, ALU.max))
                m = self.do(dve, [m], lambda e: e.tensor_scalar(top, top, -scale, None, ALU.mult))
                mult, waits = scale, [p_free[i % 3]]
            else:
                for qt in range(TT):
                    rows = lambda ap: ap.rearrange("p (m w) -> p m w", w=hd["bias"](qt).shape[2])
                    z = self.do(dve, [s_done, p_free[i % 3], hd["bias_ready"]], lambda e: e.scalar_tensor_tensor(
                        out=rows(P_[:, qt, :]), in0=rows(self.bank[b][:, qt * T:(qt + 1) * T]), scalar=scale,
                        in1=hd["bias"](qt), op0=ALU.mult, op1=ALU.add))
                self.bank_free[b] = z
                m = self.do(dve, [z, self.att_free], lambda e: e.tensor_reduce(top, P_[:, :, :], AX.X, ALU.max))
                if hd["sink"] is None:
                    m = self.do(dve, [m], lambda e: e.tensor_scalar(top, top, -1.0, None, ALU.mult))
                else:
                    m = self.do(dve, [m], lambda e: e.tensor_scalar(top, top, hd["sink"], -1.0, ALU.max, ALU.mult))
                mult, waits = 1.0, []
            for qt in range(TT):
                src = self.bank[b][:, qt * T:(qt + 1) * T] if hd["bias"] is None else P_[:, qt, :]
                ex = self.do(act, [m, *waits], lambda e: e.activation(
                    P_[:, qt, :], src, ACT.Exp, bias=st[:, i, 0, qt:qt + 1], scale=mult,
                    accum_out=st[:, i, 1, qt:qt + 1]))
            if hd["bias"] is None:
                self.bank_free[b] = ex
            if hd["sink"] is not None:
                es = self.do(act, [m], lambda e: e.activation(st[:, i, 2, :], top, ACT.Exp, bias=hd["sink"]))
                sums[i] = (es, ex)
            soft[i] = ex

        def normalize(i):
            P_ = p[i % 3]
            if i in sums:
                soft[i] = self.do(dve, sums[i], lambda e: e.tensor_tensor(
                    st[:, i, 1, :], st[:, i, 1, :], st[:, i, 2, :], ALU.add))
            r = self.do(dve, [soft[i]], lambda e: e.reciprocal(st[:, i, 1, :], st[:, i, 1, :]))
            for qt in range(TT):
                nrm = self.do(dve, [r], lambda e: e.tensor_scalar(
                    P_[:, qt, :], P_[:, qt, :], st[:, i, 1, qt:qt + 1], None, ALU.mult))
            soft[i] = nrm

        def turn(i):
            b = 6 + i % 2
            self.after(pe, self.bank_free[b], soft[i])
            for qt in range(TT):
                for kt in range(TT):
                    mm = nc.tensor.transpose(self.bank[b][:, kt * T + qt * P:kt * T + (qt + 1) * P],
                                             p[i % 3][:, qt, kt * P:(kt + 1) * P], self.const("identity"))
            t = self.done(pe, mm)
            p_free[i % 3] = t
            ptr[i] = self.do(act, [t, pT_free[i % 2]], lambda e: e.activation(
                pT[i % 2][:, :, :], self.bank[b][:, :].rearrange("p (k q) -> p k q", k=TT), ACT.Copy))
            self.bank_free[b] = ptr[i]

        def weigh(i):
            hd = heads[i]
            b, rows, parts = hd["out"]
            self.after(pe, self.bank_free[b], ptr[i])
            for j in range(parts):
                for kt in range(TT):
                    mm = nc.tensor.matmul(self.bank[b][rows, j * T:(j + 1) * T], hd["v"](kt, j), pT[i % 2][:, kt, :],
                                          start=(kt == 0), stop=(kt == TT - 1), skip_group_check=True)
            o = self.done(pe, mm)
            pT_free[i % 2] = o
            weighed[i] = o

        def flush(i):
            nonlocal last_flush
            if heads[i]["flush"]:
                b, (t0, cnt) = heads[i]["out"][0], heads[i]["flush"]
                src = self.bank[b][:, 0:cnt * T].rearrange("p (j t) -> p j t", j=cnt)
                last_flush = self.split_from_psum(src, cat_hi[:, t0:t0 + cnt, :], cat_lo[:, t0:t0 + cnt, :], weighed[i])
                self.bank_free[b] = last_flush

        for i in range(n + 4):
            if i < n:
                scores(i)
            if i < len(meanwhile):
                meanwhile[i]()
            if 1 <= i <= n:
                normalize(i - 1)
            if 2 <= i <= n + 1:
                turn(i - 2)
            if i >= 4:
                flush(i - 4)
            if 3 <= i < n + 3:
                weigh(i - 3)
        self.xf_free[0] = p_free[2]
        self.att_free = last_flush
        return [last_flush] * 4

    def ab_stream(self):
        w, wo = self.a["ab_w_in_2"][0], self.a["ab_w_out_2"][0]
        return self.square_stream([(w, c) for c in (0, 512, 1024)] + [(wo, 0), (wo, 512)])

    def mixer_ab(self, st, free):
        g, nc = self.ab, self.nc
        dve, act, pool, pe = self.dve, self.act, self.pool, self.pe
        proj = g["proj"]

        def project(b):
            banks = [(0, 1), (2, 3)][b % 2]
            d = self.block_token_major(st, banks, self.x_hi, self.x_lo, self.x_ready)
            for tt in range(TT):
                pr = self.do(act, [d[tt], free], lambda e: e.activation(
                    proj[:, tt, b * 512:(b + 1) * 512], self.bank[banks[tt]][:, :], ACT.Copy))
                self.bank_free[banks[tt]] = pr
            return pr

        project(0)
        first_two = project(1)
        NH = 10
        tmp, rot = self.xhat, g["rot"]
        H2 = HD // 2
        group = [proj[:, :, kind * 768:kind * 768 + NH * HD].rearrange("p t (h d) -> p t h d", h=NH) for kind in range(2)]

        flat = proj[:, :, 0:NH * HD]
        rs = self.small3[:, 0:TT * NH]
        for tt in range(TT):
            sq = self.do(act, [first_two, self.xhat_free], lambda e: e.activation(tmp[:, tt, 0:NH * HD], flat[:, tt, :], ACT.Square))
            ms = self.do(dve, [sq], lambda e: e.tensor_reduce(
                rs[:, tt * NH:(tt + 1) * NH], tmp[:, tt, 0:NH * HD].rearrange("p (h d) -> p h d", h=NH), AX.X, ALU.add))
        me = self.do(dve, [ms], lambda e: e.tensor_scalar(rs, rs, 1.0 / HD, RMS_EPS, ALU.mult, ALU.add))
        rr = self.do(pool, [me], lambda e: e.tensor_tensor(rs, rs, self.minus_half[:, 0:TT * NH], ALU.pow))
        for tt in range(TT):
            sc = self.do(dve, [rr], lambda e: e.tensor_tensor(
                group[0][:, tt, :, :], group[0][:, tt, :, :],
                rs[:, tt * NH:(tt + 1) * NH].unsqueeze(2).to_broadcast([P, NH, HD]), ALU.mult))
            for part, (h0, h1) in enumerate(((0, 8), (8, 10))):
                normed = self.do(dve, [sc, self.small_loaded], lambda e: e.tensor_tensor(
                    group[0][:, tt, h0:h1, :], group[0][:, tt, h0:h1, :],
                    self.gains[:, part, :].unsqueeze(1).to_broadcast([P, h1 - h0, HD]), ALU.mult))

        rotated = [None] * TT
        tile_ready = [[None] * 6 for _ in range(2)]
        turned = None

        def rotate(kind, tt, ready):
            name = "1d" if kind else "2d"
            heads = group[kind]
            cos = self.const(f"cos_{name}")[:, tt * H2:(tt + 1) * H2].unsqueeze(1).to_broadcast([P, NH, H2])
            sin = self.const(f"sin_{name}")[:, tt * H2:(tt + 1) * H2].unsqueeze(1).to_broadcast([P, NH, H2])
            x1, x2 = heads[:, tt, :, 0:H2], heads[:, tt, :, H2:HD]
            t = [tmp[:, tt, i * 320:(i + 1) * 320].rearrange("p (h d) -> p h d", h=NH) for i in range(3)]
            waits = [ready, self.xhat_free, turned, rotated[tt]]
            a1 = self.do(dve, waits, lambda e: e.tensor_tensor(t[0], x1, cos, ALU.mult))
            a2 = self.do(dve, waits, lambda e: e.tensor_tensor(t[1], x2, sin, ALU.mult))
            a3 = self.do(pool, waits, lambda e: e.tensor_tensor(t[2], x2, cos, ALU.mult))
            a4 = self.do(pool, [a1, a3], lambda e: e.tensor_tensor(x1, x1, sin, ALU.mult))
            for o0, o1, h0, h1 in ((0, 8, 0, 8), (8, 10, 8, 9), (10, 12, 9, 10)):
                dup = o1 - o0 != h1 - h0
                bc = (lambda ap: ap.to_broadcast([P, 2, H2])) if dup else (lambda ap: ap)
                self.do(dve, [a1, a2], lambda e: e.tensor_tensor(
                    rot[:, tt, o0:o1, 0:H2], bc(t[0][:, h0:h1, :]), bc(t[1][:, h0:h1, :]), ALU.subtract))
                r2 = self.do(dve, [a3, a4], lambda e: e.tensor_tensor(
                    rot[:, tt, o0:o1, H2:HD], bc(t[2][:, h0:h1, :]), bc(x1[:, h0:h1, :]), ALU.add))
            rotated[tt] = r2

        def turn_heads(kind, tile, b):
            nonlocal turned
            self.after(pe, self.bank_free[b], rotated)
            for tt in range(TT):
                mm = nc.tensor.transpose(self.bank[b][:, tt * P:(tt + 1) * P],
                                         rot[:, tt, 2 * tile:2 * tile + 2, :].rearrange("p h d -> p (h d)"),
                                         self.const("identity"))
            turned = self.done(pe, mm)
            dst = g["qT_ab"][:, kind * 4 + tile, :] if tile < 4 else g["kT_ab"][:, kind * 2 + tile - 4, :]
            self.bank_free[b] = tile_ready[kind][tile] = self.do(act, [turned], lambda e: e.activation(
                dst, self.bank[b][:, 0:T], ACT.Copy))

        for tt in range(TT):
            rotate(0, tt, normed)
        third = project(2)
        for tile in range(6):
            turn_heads(0, tile, 4 + tile % 4)
        steps = [lambda: rotate(1, 0, third), lambda: rotate(1, 1, third)]
        steps += [lambda: (turn_heads(1, 4, 2), turn_heads(1, 5, 3)), lambda: (turn_heads(1, 0, 2), turn_heads(1, 1, 3)),
                  lambda: (turn_heads(1, 2, 2), turn_heads(1, 3, 3)),
                  lambda: self.residual([2]), lambda: self.residual([3])]
        heads = []
        window = self.const("window").rearrange("p (q k) -> p q k", q=TT)
        for kind in range(2):
            for h in range(8):
                rows = slice((h % 2) * HD, (h % 2 + 1) * HD)
                kv = h // 4
                voff = kind * 768 + 640 + kv * HD
                tile = kind * 4 + h // 2
                heads.append(dict(
                    terms=[(g["qT_ab"][rows, tile, :], g["kT_ab"][rows, kind * 2 + kv, :])],
                    v=lambda kt, j, voff=voff: proj[:, kt, voff:voff + HD],
                    bias=(lambda qt: window[:, qt, :].unsqueeze(1)) if kind else None, bias_ready=None,
                    sink=self.sink[:, h:h + 1] if kind else None,
                    out=(tile % 2, rows, 1), flush=(tile, 1) if h % 2 else None,
                    ready=(first_two, third, tile_ready[kind])))
        ready = self.attention(heads, HD ** -0.5, [g["p0_ab"], g["p1_ab"]], [g["pT0_ab"], g["pT1_ab"]],
                               g["cat_hi_ab"], g["cat_lo_ab"], steps)
        self.xhat_free = rotated
        return g["cat_hi_ab"], g["cat_lo_ab"], ready

    def c_stream(self):
        w, wo = self.a["c_w_in_2"][0], self.a["c_w_out_2"][0]
        return self.square_stream([(w, c) for c in range(0, 3 * D, 512)] + [(wo, 0), (wo, 512)])

    def qkv_blocks(self, st, which, hi, lo, ready, free, base):
        g = self.qkv
        for half in range(2):
            banks = [(0, 1), (2, 3)][(base + half) % 2]
            if which == "v_att":
                d = self.block_token_major(st, banks, hi, lo, ready)
            else:
                d = [self.block_transposed(st, banks, hi, lo, ready)] * 2
            for b in range(2):
                if which == "v_att":
                    dst, src = g[which][:, b, half * 512:(half + 1) * 512], self.bank[banks[b]][:, :]
                else:
                    dst = g[which][:, half * 4 + 2 * b:half * 4 + 2 * b + 2, :]
                    src = self.bank[banks[b]][:, :].rearrange("p (m t) -> p m t", m=2)
                r = self.do(self.act, [d[b], free], lambda e: e.activation(dst, src, ACT.Copy))
                self.bank_free[banks[b]] = r
        return r

    def mixer_c(self, st, free):
        g = self.qkv
        bias = g["bias"]
        rpb = self.a["c_rpb_2"]
        n_dr, n_dc = 2 * NA_KH - 1, 2 * NA_KW - 1
        for ro in range(2):
            for h in range(C_HEADS):
                off = h * n_dr * n_dc + (NA_KH - 1 - 2 - ro) * n_dc + NA_KW - GRID_W
                src = bass.AP(rpb.tensor, off, [[1, GRID_W], [n_dc, BIAS_ROWS], [1, GRID_W]])
                bias_landed = self.load_small(bias[ro * GRID_W:(ro + 1) * GRID_W, h, :, :], src, [free])
        masked = []
        for h in range(C_HEADS):
            masked.append(self.do(self.pool, [bias_landed], lambda e: e.tensor_tensor(
                bias[:, h, :, :], bias[:, h, :, :],
                self.const("neighbours").unsqueeze(1).to_broadcast([P, BIAS_ROWS, GRID_W]), ALU.add)))
        self.qkv_blocks(st, "qT", self.x_hi, self.x_lo, self.x_ready, free, 0)
        self.qkv_blocks(st, "kT", self.x_hi, self.x_lo, self.x_ready, free, 0)
        ready = self.qkv_blocks(st, "v_att", self.x_hi, self.x_lo, self.x_ready, free, 0)
        heads = []
        for h in range(C_HEADS):
            rows = slice((h % 2) * HD, (h % 2 + 1) * HD)
            heads.append(dict(
                terms=[(g["qT"][rows, h // 2, :], g["kT"][rows, h // 2, :])],
                v=lambda kt, j, h=h: g["v_att"][:, kt, h * HD:(h + 1) * HD],
                bias=lambda qt, h=h: bias[:, h, 2 - 2 * qt:2 - 2 * qt + ROWS, ::-1],
                bias_ready=masked[h], sink=None, out=((h // 2) % 2, rows, 1),
                flush=(h // 2, 1) if h % 2 else None, ready=ready))
        r = self.attention(heads, HD ** -0.5, [g["p0"], g["p1"]], [g["pT0"], g["pT1"]], g["cat_hi_qkv"], g["cat_lo_qkv"],
                           [lambda: self.residual([2]), lambda: self.residual([3])])
        return g["cat_hi_qkv"], g["cat_lo_qkv"], r

    def mem_stream(self, layer):
        wq, wkv, wo = self.a["mem_w_q_2"][layer], self.a["mem_w_kv_2"][layer], self.a["mem_w_o_2"][layer]
        return self.square_stream([(wkv, c) for c in range(0, 2 * D, 512)] + [(wq, 0), (wq, 512), (wo, 0), (wo, 512)])

    def memory_parts(self, free):
        m = self.mem_row
        landed = self.load_small(m[:, :, :], self.a["mem_2"][0].rearrange("(t p) d -> p t d", p=P), [free])
        ready = [None] * 4
        for tt in range(TT):
            for half in range(2):
                n = 2 * tt + half
                turned = self.transpose_block(m, tt, half, 4 + n, landed)
                ready[n] = self.split_from_psum(
                    self.bank[4 + n][:, :].rearrange("p (k t) -> p k t", k=4),
                    self.mem_hi[:, half * 4:half * 4 + 4, tt * P:(tt + 1) * P],
                    self.mem_lo[:, half * 4:half * 4 + 4, tt * P:(tt + 1) * P], turned, [free])
                self.bank_free[4 + n] = ready[n]
        return ready

    def memory_attn(self, layer, st, free, mem_ready):
        g = self.qkv
        self.qkv_blocks(st, "kT", self.mem_hi, self.mem_lo, mem_ready, free, 0)
        self.qkv_blocks(st, "v_att", self.mem_hi, self.mem_lo, mem_ready, free, 0)
        ready = self.qkv_blocks(st, "qT", self.x_hi, self.x_lo, self.x_ready, free, 0)
        dm = D // MEM_HEADS
        heads = []
        for h in range(MEM_HEADS):
            heads.append(dict(
                terms=[(g["qT"][:, 2 * h + j, :], g["kT"][:, 2 * h + j, :]) for j in range(2)],
                v=lambda kt, j, h=h: g["v_att"][:, kt, h * dm + j * P:h * dm + (j + 1) * P],
                bias=None, bias_ready=None, sink=None, out=(h % 2, slice(0, P), 2), flush=(2 * h, 2), ready=ready))
        r = self.attention(heads, dm ** -0.5, [g["p0"], g["p1"]], [g["pT0"], g["pT1"]], g["cat_hi_qkv"], g["cat_lo_qkv"],
                           [lambda: self.residual([2]), lambda: self.residual([3])])
        return g["cat_hi_qkv"], g["cat_lo_qkv"], r

    def router(self, acc_free):
        a, nc, dve, act, pe = self.a, self.nc, self.dve, self.act, self.pe
        E = N_EXP
        r_raw, r_hi, r_lo = self.router_raw, self.router_hi, self.router_lo
        landed = self.load_small(r_raw[:, :, :], a["router_w"][0].rearrange("(k p) e -> p k e", p=P), [self.small_free])
        zeroed = self.do(self.pool, [self.small_free], lambda e: e.memset(self.logitT[:, :], 0.0))
        h = self.do(act, [landed], lambda e: e.activation(r_hi[:, :, :], r_raw[:, :, :], ACT.Copy))
        lo = self.do(dve, [h], lambda e: e.tensor_tensor(r_lo[:, :, :], r_raw[:, :, :], r_hi[:, :, :].bitcast(F32), ALU.subtract))
        self.after(pe, lo, self.x_ready, self.bank_free[4])
        for k in range(KT):
            mm = self.product(self.bank[4][0:E, 0:T], r_hi[:, k, :], r_lo[:, k, :],
                              self.x_hi[:, k, :], self.x_lo[:, k, :], start=(k == 0), stop=(k == KT - 1))
        self.router_done = self.done(pe, mm)
        copied = self.do(dve, [self.router_done, zeroed], lambda e: e.tensor_copy(
            self.logitT[0:E, :], self.bank[4][0:E, 0:T]))
        self.after(pe, copied, self.bank_free[5])
        for tt in range(TT):
            mm = nc.tensor.transpose(self.bank[5][:, tt * P:(tt + 1) * P], self.logitT[:, tt * P:(tt + 1) * P],
                                     self.const("identity"))
        l_done = self.done(pe, mm)
        sm = self.small
        logit = sm[:, 128:128 + TT * E].rearrange("p (t e) -> p t e", t=TT)
        rank = sm[:, 144:144 + TT * E].rearrange("p (t e) -> p t e", t=TT)
        first = sm[:, 160:160 + TT * E].rearrange("p (t e) -> p t e", t=TT)
        top = sm[:, 176:180]
        w2 = sm[:, 180:182]
        cmp_ = sm[:, 192:256].rearrange("p (e j) -> p e j", j=E)
        eq = sm[:, 256:320].rearrange("p (e j) -> p e j", j=E)
        prod = sm[:, 320:320 + TT * E].rearrange("p (t e) -> p t e", t=TT)
        t = self.do(dve, [l_done], lambda e: e.tensor_copy(
            logit, self.bank[5][:, 0:T].rearrange("p (t c) -> p t c", t=TT)[:, :, 0:E]))
        self.bank_free[4] = self.bank_free[5] = t
        earlier = self.const("earlier_expert").rearrange("p (e j) -> p e j", j=E)
        for tt in range(TT):
            own = logit[:, tt, :].unsqueeze(2).to_broadcast([P, E, E])
            other = logit[:, tt, :].unsqueeze(1).to_broadcast([P, E, E])
            a1 = self.do(dve, [t], lambda e: e.tensor_tensor(cmp_, other, own, ALU.is_gt))
            a2 = self.do(dve, [t], lambda e: e.tensor_tensor(eq, other, own, ALU.is_equal))
            a3 = self.do(dve, [a2], lambda e: e.tensor_tensor(eq, eq, earlier, ALU.mult))
            a4 = self.do(dve, [a1, a3], lambda e: e.tensor_tensor(cmp_, cmp_, eq, ALU.add))
            t = self.do(dve, [a4], lambda e: e.tensor_reduce(rank[:, tt, :], cmp_, AX.X, ALU.add))
        for i in range(2):
            s = self.do(dve, [t], lambda e: e.tensor_scalar(first, rank, float(i), None, ALU.is_equal))
            s = self.do(dve, [s], lambda e: e.tensor_tensor(prod, first, logit, ALU.mult))
            t = self.do(dve, [s], lambda e: e.tensor_reduce(top[:, 2 * i:2 * i + 2], prod, AX.X, ALU.add))
        d = self.do(dve, [t], lambda e: e.tensor_tensor(top[:, 2:4], top[:, 2:4], top[:, 0:2], ALU.subtract))
        ex = self.do(act, [d], lambda e: e.activation(w2, top[:, 2:4], ACT.Exp))
        d = self.do(dve, [ex], lambda e: e.tensor_scalar(top[:, 0:2], w2, 1.0, None, ALU.add))
        d = self.do(dve, [d], lambda e: e.reciprocal(top[:, 0:2], top[:, 0:2]))
        d = self.do(dve, [d], lambda e: e.tensor_tensor(top[:, 2:4], w2, top[:, 0:2], ALU.mult))
        s1 = self.do(dve, [d], lambda e: e.tensor_scalar(first, rank, 0.0, None, ALU.is_equal))
        s2 = self.do(dve, [d], lambda e: e.tensor_scalar(prod, rank, 1.0, None, ALU.is_equal))
        for tt in range(TT):
            m = self.do(dve, [s1], lambda e: e.tensor_scalar(first[:, tt, :], first[:, tt, :], top[:, tt:tt + 1], None, ALU.mult))
            g = self.do(dve, [m, s2], lambda e: e.scalar_tensor_tensor(
                out=self.gates[:, tt, :], in0=prod[:, tt, :], scalar=top[:, 2 + tt:3 + tt], in1=first[:, tt, :],
                op0=ALU.mult, op1=ALU.add))
        c = self.do(dve, [d], lambda e: e.tensor_scalar(self.chosen[:, :, :], rank, 2.0, None, ALU.is_lt))
        return [g, c]

    def expert_weights(self, e):
        one = lambda w: (lambda r, c: w[bass.ds(e, 1), r, c].rearrange("o k n -> (o k) n"))
        return tuple(one(self.a[n][0]) for n in ("exp_w_gate", "exp_w_up", "exp_w_down"))

    def plan_slots(self, routed, meanwhile):
        dve, pool, pe, nc = self.dve, self.pool, self.pe, self.nc
        strict, ones = self.before_me[:, 0, :], self.before_me[:, 1, :]
        o = self.do(pool, [self.x_ready], lambda e: e.memset(self.before_me[:, :, :], 1.0))
        m = self.do(pool, [o], lambda e: e.affine_select(
            out=strict, in_=strict, compare_op=ALU.is_gt, fill=0.0, base=0, pattern=[[1, P]], channel_multiplier=-1))
        E = N_EXP
        self.after(pe, m, routed, self.bank_free[4])
        out = self.bank[4]
        nc.tensor.matmul(out[:, 0:E], strict, self.chosen[:, 0, :], start=True, stop=True, skip_group_check=True)
        for base, last in ((E, strict), (2 * E, ones)):
            nc.tensor.matmul(out[:, base:base + E], ones, self.chosen[:, 0, :], start=True, stop=False, skip_group_check=True)
            mm = nc.tensor.matmul(out[:, base:base + E], last, self.chosen[:, 1, :], start=False, stop=True, skip_group_check=True)
        counted = self.done(pe, mm)
        padded = meanwhile()
        far = self.do(dve, [counted], lambda e: e.tensor_scalar(
            self.place[:, :, :], self.chosen[:, :, :], -1000.0, 1000.0, ALU.mult, ALU.add))
        placed = self.do(dve, [far], lambda e: e.tensor_tensor(
            self.place[:, :, :], self.place[:, :, :], out[:, 0:2 * E].rearrange("p (t e) -> p t e", t=TT), ALU.add))
        big = self.do(dve, [counted], lambda e: e.tensor_reduce(self.biggest[:, :], out[:, 2 * E:3 * E], AX.X, ALU.max))
        flag = self.do(dve, [big], lambda e: e.tensor_scalar(self.overflow[:, :], self.biggest[:, :], float(P), None, ALU.is_gt))
        self.bank_free[4] = flag
        self.h_free = [counted, counted]
        return placed, flag, padded

    def build_pick(self, e_, waits):
        for tt in range(TT):
            picked = self.do(self.dve, waits, lambda e: e.tensor_scalar(
                self.pick[:, tt, 0:P], self.const("slot_number"), self.place[:, tt, bass.ds(e_, 1)], None, ALU.is_equal))
        return picked

    def gather(self, e_, picked):
        pe, nc = self.pe, self.nc
        self.after(pe, picked, self.n_ready, self.bank_free[2], self.bank_free[3])
        for k in range(KT):
            wide = 2 * P if k % 4 < 3 else P
            out = self.bank[2 + k // 4][:, (k % 4) * P:(k % 4) * P + wide]
            for tt in range(TT):
                for part in (self.n_hi, self.n_lo):
                    mm = nc.tensor.matmul(out, part[:, tt, k * P:(k + 1) * P], self.pick[:, tt, 0:wide],
                                          start=(k % 4 == 0 and tt == 0 and part is self.n_hi), stop=(tt == TT - 1),
                                          skip_group_check=True)
        got = self.done(pe, mm)
        self.after(pe, self.bank_free[6])
        for tt in range(TT):
            mm = nc.tensor.matmul(self.bank[6][:, 0:1], self.pick[:, tt, 0:P].bitcast(F32),
                                  self.gates[:, tt, bass.ds(e_, 1)], start=(tt == 0), stop=(tt == TT - 1), skip_group_check=True)
        gate_got = self.done(pe, mm)
        self.pick_free = gate_got
        (gt, gc), (bt, bc) = self.x_affine_of
        for k in range(KT):
            scaled = self.do(self.act, [got, self.xe_all_free], lambda e: e.activation(
                self.xe_all[:, k, :], self.bank[2 + k // 4][:, (k % 4) * P:(k % 4 + 1) * P], ACT.Identity,
                bias=self.cols[:, bt, bc + k:bc + k + 1], scale=self.cols[:, gt, gc + k:gc + k + 1]))
        self.bank_free[2] = self.bank_free[3] = scaled
        return scaled, gate_got

    def switch_input(self, gathered, last_up, last_h):
        scaled, gate_got = gathered
        for half in range(2):
            ks = slice(half * 4, half * 4 + 4)
            h = self.do(self.act, [scaled, last_up], lambda e: e.activation(self.xe_hi[:, ks, :], self.xe_all[:, ks, :], ACT.Copy))
            lo = self.do(self.dve, [h, last_up], lambda e: e.tensor_tensor(
                self.xe_lo[:, ks, :], self.xe_all[:, ks, :], self.xe_hi[:, ks, :].bitcast(F32), ALU.subtract))
        self.xe_all_free = lo
        g = self.do(self.dve, [gate_got, last_h], lambda e: e.tensor_copy(self.slot_gate[:, :], self.bank[6][:, 0:1]))
        self.bank_free[6] = g
        self.xe_ready, self.gate_ready = lo, g

    def e_up(self, par, slots):
        pe, bank = self.pe, 4 + par
        self.after(pe, self.bank_free[bank], self.xe_ready)
        for kh in range(2):
            s, split = slots[kh]
            self.after(pe, split)
            for k in range(4):
                kk = kh * 4 + k
                mm = self.product(self.bank[bank][:, :], self.xe_hi[:, kk, :], self.xe_lo[:, kk, :],
                                  self.part_hi[s][:, k * 512:(k + 1) * 512], self.part_lo[s][:, k * 512:(k + 1) * 512],
                                  start=(kk == 0), stop=(kk == KT - 1))
            token = self.done(pe, mm)
            self.release(s, token)
        return token

    def e_act(self, par, up_done):
        bank = self.bank[4 + par]
        act = self.do(self.act, [up_done, self.h_free[par]], lambda e: e.activation(
            self.silu[par][:, :], bank[:, 0:FC], ACT.Silu))
        h = self.do(self.dve, [act, up_done, self.hT_turned[par], self.gate_ready], lambda e: e.scalar_tensor_tensor(
            out=self.h[par][:, :], in0=self.silu[par][:, :], scalar=self.slot_gate[:, 0:1],
            in1=bank[:, FC:2 * FC], op0=ALU.mult, op1=ALU.mult))
        self.bank_free[4 + par] = self.h_free[par] = h
        return h

    def e_turn(self, par, h_ready):
        bank = 6 + par
        self.after(self.pe, h_ready, self.bank_free[bank])
        for j in range(2):
            mm = self.nc.tensor.transpose(self.bank[bank][:, j * P:(j + 1) * P],
                                          self.h[par][:, j * P:(j + 1) * P], self.const("identity"))
        self.hT_turned[par] = turned = self.done(self.pe, mm)
        ready = self.split_from_psum(self.bank[bank][:, 0:FC].rearrange("p (j t) -> p j t", j=2),
                                     self.hT_hi[par][0][:, :, :], self.hT_lo[par][0][:, :, :], turned,
                                     [self.hT_used[par][0]])
        self.bank_free[bank] = ready
        return ready

    def e_down(self, par, down, start=False):
        (s, split), hT_ready = down
        self.after(self.pe, split, hT_ready)
        for j in range(2):
            for half in range(2):
                if start and j == 0:
                    self.after(self.pe, self.bank_free[half])
                cols = slice(j * D + half * 512, j * D + (half + 1) * 512)
                mm = self.product(self.bank[half][:, :], self.hT_hi[par][0][:, j, :], self.hT_lo[par][0][:, j, :],
                                  self.part_hi[s][:, cols], self.part_lo[s][:, cols], start=(start and j == 0))
        token = self.done(self.pe, mm)
        self.hT_used[par][0] = token
        self.release(s, token)
        return token

    def split_y(self, y_done):
        for half in range(2):
            self.y_ready[half] = self.split_from_psum(self.bank[half][:, :], self.y_hi[half][:, :], self.y_lo[half][:, :],
                                                      y_done, [self.y_free[half], self.xe_all_free])
            self.bank_free[half] = self.y_ready[half]

    def turn_pick(self):
        pe, nc = self.pe, self.nc
        self.after(pe, self.bank_free[7])
        for tt in range(TT):
            mm = nc.tensor.transpose(self.bank[7][:, tt * P:(tt + 1) * P], self.pick[:, tt, 0:P].bitcast(F32), self.const("identity"))
        self.pick_free = turned = self.done(pe, mm)
        self.bank_free[7] = self.pickT_ready = self.do(self.act, [turned, self.pickT_free], lambda e: e.activation(
            self.pickT[:, :, :], self.bank[7][:, 0:TT * P].rearrange("p (t s) -> p t s", t=TT), ACT.Copy))

    def scatter(self):
        pe, nc = self.pe, self.nc
        self.after(pe, self.pickT_ready)
        for half in range(2):
            self.after(pe, self.y_ready)
            for tt in range(TT):
                b = (2 + tt, tt)[half]
                self.after(pe, self.bank_free[b])
                nc.tensor.matmul(self.bank[b][:, :], self.pickT[:, tt, :], self.y_hi[half][:, :], start=True, stop=False, skip_group_check=True)
                mm = nc.tensor.matmul(self.bank[b][:, :], self.pickT[:, tt, :], self.y_lo[half][:, :], start=False, stop=True, skip_group_check=True)
                back = self.done(pe, mm)
                part = self.total[:, tt, half * 512:(half + 1) * 512]
                self.bank_free[b] = self.total_ready[tt] = self.do(self.dve, [back, self.total_ready[tt]], lambda e: e.tensor_tensor(
                    part, part, self.bank[b][:, :], ALU.add))
            self.y_free[half] = back
        self.pickT_free = back
        self.xe_all_free = [self.xe_all_free, back]

    def experts(self, n_chunks, up_slots):
        st = {"up": up_slots}

        def phase(c, par, e_, first=False, last=False, begin_down=False, between=None):
            gate, up, down = self.expert_weights(e_)
            seam = last and st["next"] is not None
            if seam:
                picked = self.build_pick(st["next"], [self.pick_free])
            if c is not None and not last:
                nxt = [self.load_and_split(x, RING) for x in self.ffn_loads_up(gate, up, (c + 1) * FC)]
            elif st["next"] is not None:
                w = self.expert_weights(st["next"])
                nxt = [self.load_and_split(x, RING) for x in self.ffn_loads_up(w[0], w[1], 0)]
            else:
                nxt = None
            up_done = self.e_up(par, st["up"])
            h = self.e_act(par, up_done)
            down_slot = self.load_and_split(self.ffn_load_down(down, c * FC), RING)
            if between:
                between()
            if seam:
                gathered = self.gather(st["next"], picked)
            if not first:
                self.e_down(1 - par, st["down"], start=begin_down)
            st["down"] = (down_slot, self.e_turn(par, h))
            if seam:
                self.switch_input(gathered, up_done, h)
            st["up"] = nxt

        def expert(e_, last=False):
            st["next"] = None if last else e_ + 1
            units = (n_chunks - 2) // 2
            assert n_chunks == 2 * units + 2
            self.turn_pick()
            before = dict(self.c.count)
            phase(1, 1, e_, begin_down=True)
            phase(2, 0, e_)
            with self.c.repeat(before, units) as i:
                phase(i * 2 + 1, 1, e_)
                phase(i * 2 + 2, 0, e_)
            phase(n_chunks - 1, 1, e_, last=True)
            y_done = self.e_down(1, st["down"])
            self.split_y(y_done)
            if not last:
                phase(0, 0, e_ + 1, first=True, between=self.scatter)
            else:
                self.scatter()

        self.switch_input(self.gather(0, self.build_pick(0, [self.pick_free])), None, None)
        st["next"] = None
        phase(0, 0, 0, first=True)
        before = dict(self.c.count)
        expert(0)
        with self.c.repeat(before, N_EXP - 1) as e_:
            expert(e_)
        expert(N_EXP - 1, last=True)

    def moe(self, up_slots, n_chunks):
        nc = self.nc
        routed = self.router(None)
        old_x = [self.residual_done, self.router_done]

        def split_normed():
            for tt in range(TT):
                for half in range(2):
                    cols = slice(half * 512, (half + 1) * 512)
                    src = self.xhat[:, tt, cols]
                    h = self.do(self.act, [old_x, self.xhat_ready[tt, half]], lambda e: e.activation(self.n_hi[:, tt, cols], src, ACT.Copy))
                    self.n_ready = self.do(self.dve, [h, old_x], lambda e: e.tensor_tensor(
                        self.n_lo[:, tt, cols], src, self.n_hi[:, tt, cols].bitcast(F32), ALU.subtract))
            return self.do(self.dve, [routed], lambda e: e.tensor_scalar(
                self.pick[:, :, P:2 * P], self.n_hi[:, :, 0:P].bitcast(F32), 0.0, None, ALU.mult))

        placed, flag, padded = self.plan_slots(routed, split_normed)
        self.after(self.pe, padded)
        self.total_ready = [None] * TT
        for tt in range(TT):
            for half in range(2):
                cols = slice(half * 512, (half + 1) * 512)
                self.total_ready[tt] = self.do(self.act, [old_x, self.n_ready, self.xhat_free], lambda e: e.activation(
                    self.total[:, tt, cols], self.acc(tt, half)[:, :], ACT.Copy))
                self.bank_free[2 * tt + half] = self.total_ready[tt]
        self.after(self.dve, placed, routed)
        self.pick_free = self.pickT_free = flag
        self.y_free = [None, None]
        self.y_ready = [None, None]
        self.xe_all_free = self.x_ready[3]
        self.experts(n_chunks, up_slots)

        for eng in (self.pe, self.act, self.dve, self.pool, self.sp):
            self.after(eng, flag)
        more = nc.values_load(self.overflow[0:1, 0:1], min_val=0, max_val=1,
                              skip_runtime_bounds_check_because="written by is_gt")
        saved = self.save_state()
        with nc.If(more > 0):
            engines = (self.pe, self.act, self.dve, self.pool)
            everything = [self.total_ready, self.pickT_free, self.raw_free, self.part_free, self.bank_free]
            for eng in (*engines, self.sp):
                self.after(eng, everything)
            for eng, sem in zip(engines, self.second_sems):
                eng.sem = sem
            self.landed_sem = self.second_landed
            moved = self.do(self.dve, [], lambda e: e.tensor_scalar(
                self.place[:, :, :], self.place[:, :, :], float(P), None, ALU.subtract))
            self.after(self.dve, moved)
            g, u, _ = self.expert_weights(0)
            self.experts(n_chunks, [self.load_and_split(x, RING) for x in self.ffn_loads_up(g, u, 0)])
            for eng in (*engines, self.sp):
                self.after(eng, self.total_ready, self.pickT_free, self.raw_free, self.part_free, self.bank_free)
        self.restore_state(saved)
        self.small_free = self.pickT_free
        return self.total_ready

    def save_state(self):
        return (list(self.raw_free), list(self.part_free), list(self.bank_free), list(self.h_free),
                list(self.hT_turned), [list(x) for x in self.hT_used], list(self.total_ready),
                self.raw_at, self.part_at, self.pickT_free, self.landed_sem,
                [e.sem for e in (self.pe, self.act, self.dve, self.pool)], dict(self.c.waited))

    def restore_state(self, saved):
        (self.raw_free, self.part_free, self.bank_free, self.h_free, self.hT_turned, self.hT_used, self.total_ready,
         self.raw_at, self.part_at, self.pickT_free, self.landed_sem, sems, self.c.waited) = saved
        for e, sem in zip((self.pe, self.act, self.dve, self.pool), sems):
            e.sem = sem

    def build(self):
        a = self.a
        self.acc_started = set()
        self.small_free = self.small2_free = self.vstats_free = self.att_free = None
        self.start()
        dense = lambda w: (lambda r, c: w[r, c])
        stages = []
        for layer in range(DEPTH):
            mix_ln = [(t, c + layer * KT) for t, c in (self.col_of["ln_mix_g"], self.col_of["ln_mix_b"])]
            ffn_ln = [(t, c + layer * KT) for t, c in (self.col_of["ln_ffn_g"], self.col_of["ln_ffn_b"])]
            stages.append(("gla", layer, mix_ln))
            stages.append(("ffn" if layer % 2 == 0 else "moe", layer // 2, ffn_ln))
        for layer in range(DEPTH):
            ln = lambda s: [(t, c + (layer * 4 + s) * KT) for t, c in (self.col_of["ln_g_2"], self.col_of["ln_b_2"])]
            stages.append(("ffn2", (layer, 0), ln(0)))
            stages.append(("ab" if layer % 2 == 0 else "c", layer, ln(1)))
            stages.append(("mem", layer, ln(2)))
            stages.append(("ffn2", (layer, 1), ln(3)))
        if self.stop is not None:
            stages = stages[self.stop[0]:self.stop[1]]

        def weights(kind, which):
            if kind == "ffn":
                return tuple(dense(a[n][which]) for n in ("ffn_w_gate", "ffn_w_up", "ffn_w_down"))
            if kind == "ffn2":
                return tuple(dense(a[n][which[0], which[1]]) for n in ("ffn_w_gate_2", "ffn_w_up_2", "ffn_w_down_2"))
            return self.expert_weights(0)

        def prefetch(kind, which):
            if kind in ("ffn", "ffn2", "moe"):
                return self.ffn_prefetch(weights(kind, which))
            st = {"gla": lambda: self.gla_stream(which), "ab": self.ab_stream, "c": self.c_stream,
                  "mem": lambda: self.mem_stream(which)}[kind]()
            self.stream_step(st)
            self.stream_step(st)
            return st

        ahead = prefetch(*stages[0][:2])
        free = None
        for n, (kind, which, (g, b)) in enumerate(stages):
            eps = LN_EPS
            if kind in ("ffn", "moe", "ffn2"):
                if kind == "ffn2":
                    eps = 4 * LN_EPS
                if n == 0:
                    self.start_columns()
                    self.residual(range(4))
                if kind == "moe":
                    done = [[t, t] for t in self.moe(ahead, D_FFE // FC)]
                else:
                    done = [[t, t] for t in self.ffn(weights(kind, which), D_FF // FC, ahead)]
            else:
                if n == 0 and kind != "gla":
                    self.start_columns()
                if kind == "gla":
                    cat = self.hybrid_mixer(which, ahead, free)
                elif kind == "ab":
                    cat = self.mixer_ab(ahead, free)
                elif kind == "c":
                    cat = self.mixer_c(ahead, free)
                else:
                    cat = self.memory_attn(which, ahead, free, self.memory_parts(free))
                done = self.out_projection(ahead, *cat)
            free = done[1][1]
            last = n == len(stages) - 1
            if not last:
                ahead = prefetch(*stages[n + 1][:2])
            source = (lambda tt, half: self.total[:, tt, half * 512:(half + 1) * 512]) if kind == "moe" else None
            following = None if last else stages[n + 1][0]
            residual = {"ffn": "alpha_identity", "moe": "alpha_identity", "ffn2": "alpha2_identity"}.get(following)
            normed = self.layer_norm(done, g, b, eps, final=last, source=source, residual=residual)
        layer, s = (DEPTH - 1, 3)
        gd, bd = self.final_gb
        self.store_final(normed, gd, bd)


def build_program(nc, args, out, stop=None, final=None):
    p = Program(nc, args, out, stop)
    p.final_gb = final(args) if final else (args["ln_g_2"][DEPTH - 1, 3], args["ln_b_2"][DEPTH - 1, 3])
    p.build()


_INS = ["x", "w_in", "gm_ws", "gm_bs", "gm_ln_g", "gm_ln_b", "gla_wa2", "gla_ba", "gla_norm_g", "w_out", "ln_mix_g",
        "ln_mix_b", "ffn_w_gate", "ffn_w_up", "ffn_w_down", "router_w", "exp_w_gate", "exp_w_up", "exp_w_down",
        "ln_ffn_g", "ln_ffn_b", "mem_2", "ln_g_2", "ln_b_2", "ffn_w_gate_2", "ffn_w_up_2", "ffn_w_down_2",
        "ab_w_in_2", "ab_w_out_2", "ab_q_gain_2", "ab_k_gain_2", "ab_sink_2", "c_w_in_2", "c_w_out_2", "c_rpb_2",
        "mem_w_q_2", "mem_w_kv_2", "mem_w_o_2"]


def kernel(**inputs):
    import concourse.bacc as _bacc
    from concourse.bass_utils import run_bass_kernel_spmd as _run

    nc = _bacc.Bacc("TRN2", target_bir_lowering=False, num_devices=1)
    arrays, args = {}, {}
    for name in _INS + ["consts"]:
        if name == "consts":
            a = CONST_ARRAY
        elif name == "c_rpb_2":
            a = np.ascontiguousarray(np.asarray(inputs[name])[..., ::-1])
        else:
            a = np.ascontiguousarray(inputs[name])
        arrays[f"in_{name}_dram"] = a
        args[name] = nc.dram_tensor(f"in_{name}_dram", a.shape, mybir.dt.from_np(a.dtype), kind="ExternalInput").ap()
    out = nc.dram_tensor("out_dram", (1, T, D), F32, kind="ExternalOutput").ap()
    build_program(nc, args, out)
    r = _run(nc, [arrays], core_ids=[0])
    return r.results[0]["out_dram"]
```
